# Optimizing a Trainium2 kernel written in Bass

```python
import jax, jax.numpy as jnp
from jax import lax
import numpy as np

D_MODEL = 1024
BATCH = 1
SEQ = 256
DEPTH = 2

HEAD_DIM = 64
A_HEADS = 8
B_HEADS = 4
C_HEADS = 4
A_WIDTH = A_HEADS * HEAD_DIM
B_WIDTH = B_HEADS * HEAD_DIM
C_WIDTH = C_HEADS * HEAD_DIM
MIX_WIDTH = A_WIDTH + B_WIDTH + C_WIDTH
MOBA_BLOCK = 256
MOBA_TOPK = 3
MOBA_QCHUNK = 128
RET_CHUNK = 256
MLSTM_CHUNK = 128
PAD_MULT = 256
CONV_K = 4
RMS_EPS = 1e-6
HEAD_NORM_EPS = 1e-5
ROPE_BASE = 10000.0
SPLIT_SIZES = [A_WIDTH] * 4 + [B_WIDTH] * 4 + [C_WIDTH] * 5 + [C_HEADS, C_HEADS]
N_IN = sum(SPLIT_SIZES)


def rmsnorm(x, w):
    x32 = x.astype(jnp.float32)
    y = x32 * lax.rsqrt(jnp.mean(x32 * x32, axis=-1, keepdims=True) + RMS_EPS)
    return (y * w.astype(jnp.float32)).astype(x.dtype)

def split_heads(t, n_heads):
    b, s, _ = t.shape
    return t.reshape(b, s, n_heads, HEAD_DIM).transpose(0, 2, 1, 3)

def merge_heads(t):
    b, h, s, d = t.shape
    return t.transpose(0, 2, 1, 3).reshape(b, s, h * d)

def head_norm(y, w):
    mu = jnp.mean(y, axis=-1, keepdims=True)
    var = jnp.mean(jnp.square(y - mu), axis=-1, keepdims=True)
    y = (y - mu) * lax.rsqrt(var + HEAD_NORM_EPS)
    return merge_heads(y) * w.astype(jnp.float32)

def alibi_slopes(n_heads):
    return jnp.exp2(-8.0 * jnp.arange(1, n_heads + 1, dtype=jnp.float32) / n_heads)

def rotate(t, pos):
    half = t.shape[-1] // 2
    theta = 1.0 / (ROPE_BASE ** jnp.linspace(0.0, 1.0, half, dtype=jnp.float32))
    ang = pos[:, None] * theta[None, :]
    cos, sin = jnp.cos(ang), jnp.sin(ang)
    t1, t2 = t[..., :half], t[..., half:]
    return jnp.concatenate([t1 * cos - t2 * sin, t1 * sin + t2 * cos], axis=-1)

def moba_attention(q, k, v):
    b, h, s, dh = q.shape
    nb = s // MOBA_BLOCK
    n_sel = min(MOBA_TOPK, nb - 1)
    scale = dh ** -0.5
    slopes = alibi_slopes(h)[None, :, None, None]
    kb = k.reshape(b, h, nb, MOBA_BLOCK, dh)
    vb = v.reshape(b, h, nb, MOBA_BLOCK, dh)
    kmean = jnp.mean(kb, axis=3)
    bi = jnp.arange(b)[:, None, None, None]
    hi = jnp.arange(h)[None, :, None, None]
    offs = jnp.arange(MOBA_BLOCK)
    qloc = jnp.arange(MOBA_QCHUNK)

    def one_chunk(c):
        t0 = c * MOBA_QCHUNK
        qc = lax.dynamic_slice_in_dim(q, t0, MOBA_QCHUNK, axis=2)
        tpos = t0 + qloc
        j = t0 // MOBA_BLOCK
        k_own = lax.dynamic_slice_in_dim(k, j * MOBA_BLOCK, MOBA_BLOCK, axis=2)
        v_own = lax.dynamic_slice_in_dim(v, j * MOBA_BLOCK, MOBA_BLOCK, axis=2)
        dist_own = tpos[:, None] - (j * MOBA_BLOCK + offs)[None, :]
        s_own = jnp.einsum('bhqd,bhkd->bhqk', qc, k_own) * scale - slopes * dist_own
        s_own = jnp.where(dist_own >= 0, s_own, -jnp.inf)
        if n_sel == 0:
            p = jax.nn.softmax(s_own, axis=-1)
            return jnp.einsum('bhqk,bhkd->bhqd', p, v_own)
        gate = jnp.einsum('bhqd,bhnd->bhqn', qc, kmean)
        gate = jnp.where(jnp.arange(nb) < j, gate, -jnp.inf)
        _, idx = lax.top_k(gate, n_sel)
        valid = jnp.arange(n_sel) < j
        k_sel = kb[bi, hi, idx]
        v_sel = vb[bi, hi, idx]
        dist = tpos[:, None, None] - (idx[..., None] * MOBA_BLOCK + offs)
        s_sel = jnp.einsum('bhqd,bhqnkd->bhqnk', qc, k_sel) * scale - slopes[..., None] * dist
        s_sel = jnp.where(valid[:, None], s_sel, -jnp.inf)
        n_k = n_sel * MOBA_BLOCK
        s_all = jnp.concatenate([s_sel.reshape(b, h, MOBA_QCHUNK, n_k), s_own], axis=-1)
        p = jax.nn.softmax(s_all, axis=-1)
        p_sel = p[..., :n_k].reshape(b, h, MOBA_QCHUNK, n_sel, MOBA_BLOCK)
        p_own = p[..., n_k:]
        return (jnp.einsum('bhqnk,bhqnkd->bhqd', p_sel, v_sel)
                + jnp.einsum('bhqk,bhkd->bhqd', p_own, v_own))

    outs = lax.map(one_chunk, jnp.arange(s // MOBA_QCHUNK))
    return outs.transpose(1, 2, 0, 3, 4).reshape(b, h, s, dh)

def retention(q, k, v):
    b, h, s, dh = q.shape
    L = RET_CHUNK
    nc = s // L
    log_gamma = jnp.log(1.0 - jnp.exp2(-5.0 - jnp.arange(h, dtype=jnp.float32)))
    k = k * (dh ** -0.5)
    qc = q.reshape(b, h, nc, L, dh)
    kc = k.reshape(b, h, nc, L, dh)
    vc = v.reshape(b, h, nc, L, dh)
    pos = jnp.arange(L, dtype=jnp.float32)
    diff = pos[:, None] - pos[None, :]
    decay = jnp.where(diff >= 0, jnp.exp(log_gamma[:, None, None] * jnp.maximum(diff, 0.0)), 0.0)
    scores = jnp.einsum('bhcnd,bhcmd->bhcnm', qc, kc) * decay[None, :, None]
    o_intra = jnp.einsum('bhcnm,bhcme->bhcne', scores, vc)
    zeta = jnp.exp(log_gamma[:, None] * (L - 1.0 - pos))
    kv = jnp.einsum('bhcmd,bhcme->bhcde', kc * zeta[None, :, None, :, None], vc)
    chunk_decay = jnp.exp(log_gamma * L)[None, :, None, None]

    def step(state, kv_c):
        return chunk_decay * state + kv_c, state

    r0 = jnp.zeros((b, h, dh, dh), jnp.float32)
    _, r_prev = lax.scan(step, r0, kv.transpose(2, 0, 1, 3, 4))
    r_prev = r_prev.transpose(1, 2, 0, 3, 4)
    xi = jnp.exp(log_gamma[:, None] * (pos + 1.0))
    o_cross = jnp.einsum('bhcnd,bhcde->bhcne', qc, r_prev) * xi[None, :, None, :, None]
    return (o_intra + o_cross).reshape(b, h, s, dh)

def mlstm(q, k, v, i_pre, f_pre):
    b, h, s, dh = q.shape
    L = MLSTM_CHUNK
    nc = s // L
    k = k * (dh ** -0.5)
    to_chunks = lambda t: t.reshape(b, h, nc, L, dh).transpose(2, 0, 1, 3, 4)
    qc, kc, vc = to_chunks(q), to_chunks(k), to_chunks(v)
    ic = i_pre.reshape(b, h, nc, L).transpose(2, 0, 1, 3)
    bc = jnp.cumsum(jax.nn.log_sigmoid(f_pre).reshape(b, h, nc, L), axis=-1).transpose(2, 0, 1, 3)
    pos = jnp.arange(L)
    causal = pos[:, None] >= pos[None, :]

    def step(carry, inp):
        c_st, n_st, m_st = carry
        qt, kt, vt, it, bt = inp
        d_log = jnp.where(causal, bt[..., :, None] - bt[..., None, :] + it[..., None, :], -jnp.inf)
        inter_log = bt + m_st[..., None]
        m_t = jnp.maximum(inter_log, jnp.max(d_log, axis=-1))
        w_intra = jnp.exp(d_log - m_t[..., None])
        w_inter = jnp.exp(inter_log - m_t)
        sc = jnp.einsum('bhtd,bhsd->bhts', qt, kt) * w_intra
        num = (jnp.einsum('bhts,bhse->bhte', sc, vt)
               + w_inter[..., None] * jnp.einsum('bhtd,bhde->bhte', qt, c_st))
        den = jnp.sum(sc, axis=-1) + w_inter * jnp.einsum('bhtd,bhd->bht', qt, n_st)
        h_t = num / jnp.maximum(jnp.abs(den), jnp.exp(-m_t))[..., None]
        b_last = bt[..., -1]
        g = b_last[..., None] - bt + it
        m_new = jnp.maximum(b_last + m_st, jnp.max(g, axis=-1))
        a = jnp.exp(b_last + m_st - m_new)
        w = jnp.exp(g - m_new[..., None])
        c_new = a[..., None, None] * c_st + jnp.einsum('bhs,bhsd,bhse->bhde', w, kt, vt)
        n_new = a[..., None] * n_st + jnp.einsum('bhs,bhsd->bhd', w, kt)
        return (c_new, n_new, m_new), h_t

    init = (jnp.zeros((b, h, dh, dh), jnp.float32), jnp.zeros((b, h, dh), jnp.float32),
            jnp.zeros((b, h), jnp.float32))
    _, hs = lax.scan(step, init, (qc, kc, vc, ic, bc))
    return hs.transpose(1, 2, 0, 3, 4).reshape(b, h, s, dh)

def causal_dwconv(x, w, bias):
    c = x.shape[-1]
    y = lax.conv_general_dilated(x, w.astype(x.dtype)[:, None, :], window_strides=(1,),
                                 padding=[(CONV_K - 1, 0)], dimension_numbers=('NWC', 'WIO', 'NWC'),
                                 feature_group_count=c)
    return y + bias.astype(x.dtype)

def hybrid_layer(x, norm_w, w_in, conv_w, conv_b, gate_bias, ret_norm_w, mlstm_norm_w, w_out):
    b, s, _ = x.shape
    s_pad = -(-s // PAD_MULT) * PAD_MULT
    h = rmsnorm(x, norm_w)
    proj = jnp.matmul(h, w_in).astype(jnp.float32)
    proj = jnp.pad(proj, ((0, 0), (0, s_pad - s), (0, 0)))
    cuts = np.cumsum(SPLIT_SIZES)[:-1].tolist()
    (aq, ak, av, ag, bq, bk, bv, bg, cq, ck, cv, co, cg, ci, cf) = jnp.split(proj, cuts, axis=-1)

    ya = moba_attention(split_heads(aq, A_HEADS), split_heads(ak, A_HEADS), split_heads(av, A_HEADS))
    ya = merge_heads(ya) * jax.nn.silu(ag)

    pos = jnp.arange(s_pad, dtype=jnp.float32)
    yb = retention(rotate(split_heads(bq, B_HEADS), pos), rotate(split_heads(bk, B_HEADS), pos),
                   split_heads(bv, B_HEADS))
    yb = head_norm(yb, ret_norm_w) * jax.nn.silu(bg)

    qk = jax.nn.silu(causal_dwconv(jnp.concatenate([cq, ck], axis=-1), conv_w, conv_b))
    cq_c, ck_c = qk[..., :C_WIDTH], qk[..., C_WIDTH:]
    gb = gate_bias.astype(jnp.float32)
    i_pre = ci.transpose(0, 2, 1) + gb[:C_HEADS][None, :, None]
    f_pre = cf.transpose(0, 2, 1) + gb[C_HEADS:][None, :, None]
    yc = mlstm(split_heads(cq_c, C_HEADS), split_heads(ck_c, C_HEADS), split_heads(cv, C_HEADS),
               i_pre, f_pre)
    yc = yc * split_heads(jax.nn.sigmoid(co), C_HEADS)
    yc = head_norm(yc, mlstm_norm_w) * jax.nn.silu(cg)

    y = jnp.concatenate([ya, yb, yc], axis=-1)[:, :s].astype(x.dtype)
    return x + jnp.matmul(y, w_out)

def first_inputs(seed: int = 0) -> dict:
    key = jax.random.key(seed)
    ks = jax.random.split(key, 12)
    f32 = jnp.float32
    x = jax.random.normal(ks[0], (BATCH, SEQ, D_MODEL), f32)
    norm_w = 1.0 + 0.02 * jax.random.normal(ks[1], (DEPTH, D_MODEL), f32)
    w_in = jax.random.normal(ks[2], (DEPTH, D_MODEL, N_IN), f32) * D_MODEL ** -0.5
    conv_w = jax.random.normal(ks[3], (DEPTH, CONV_K, 2 * C_WIDTH), f32) * CONV_K ** -0.5
    conv_b = 0.02 * jax.random.normal(ks[4], (DEPTH, 2 * C_WIDTH), f32)
    i_bias = 0.1 * jax.random.normal(ks[5], (DEPTH, C_HEADS), f32)
    f_bias = jnp.linspace(3.0, 6.0, C_HEADS, dtype=f32)[None, :] + 0.1 * jax.random.normal(ks[6], (DEPTH, C_HEADS), f32)
    gate_bias = jnp.concatenate([i_bias, f_bias], axis=-1)
    ret_norm_w = 1.0 + 0.02 * jax.random.normal(ks[7], (DEPTH, B_WIDTH), f32)
    mlstm_norm_w = 1.0 + 0.02 * jax.random.normal(ks[8], (DEPTH, C_WIDTH), f32)
    w_out = jax.random.normal(ks[9], (DEPTH, MIX_WIDTH, D_MODEL), f32) * MIX_WIDTH ** -0.5
    final_norm_w = 1.0 + 0.02 * jax.random.normal(ks[10], (D_MODEL,), f32)
    return {"x": x, "norm_w": norm_w, "w_in": w_in, "conv_w": conv_w, "conv_b": conv_b,
            "gate_bias": gate_bias, "ret_norm_w": ret_norm_w, "mlstm_norm_w": mlstm_norm_w,
            "w_out": w_out, "final_norm_w": final_norm_w}

def first_block(x, norm_w, w_in, conv_w, conv_b, gate_bias, ret_norm_w, mlstm_norm_w, w_out, final_norm_w):
    for layer in range(DEPTH):
        x = hybrid_layer(x, norm_w[layer], w_in[layer], conv_w[layer], conv_b[layer], gate_bias[layer],
                         ret_norm_w[layer], mlstm_norm_w[layer], w_out[layer])
    return rmsnorm(x, final_norm_w)


CTX_LEN = 256
GRID_W = 64
NA_HEADS = 6
NA_WIN_H = 8
NA_WIN_W = 16
NA_QBLK_W = 16
NA_KBLK_W = NA_QBLK_W + NA_WIN_W
SW_HEADS = 6
SW_KV_HEADS = 2
SW_WINDOW = 128
SW_BLOCK = 128
CONV_DIM = 256
CONV_WIDTH = 31
D_FF = 2816
EPS = 1e-6
NEG_INF = -1e30
N_BRANCH = 3
N_MOD = 9

A_DIM = NA_HEADS * HEAD_DIM
B_Q_DIM = SW_HEADS * HEAD_DIM
B_KV_DIM = SW_KV_HEADS * HEAD_DIM
IN_DIM = 3 * A_DIM + B_Q_DIM + 2 * B_KV_DIM + 2 * CONV_DIM + N_BRANCH * D_MODEL
SPLIT_POINTS = (A_DIM, 2 * A_DIM, 3 * A_DIM, 3 * A_DIM + B_Q_DIM,
                3 * A_DIM + B_Q_DIM + B_KV_DIM, 3 * A_DIM + B_Q_DIM + 2 * B_KV_DIM,
                3 * A_DIM + B_Q_DIM + 2 * B_KV_DIM + 2 * CONV_DIM)


def rms_norm(x, g):
    xf = x.astype(jnp.float32)
    y = xf * lax.rsqrt(jnp.mean(xf * xf, axis=-1, keepdims=True) + EPS)
    return (y * g.astype(jnp.float32)).astype(x.dtype)

def layer_norm(x, g, b):
    xf = x.astype(jnp.float32)
    mu = jnp.mean(xf, axis=-1, keepdims=True)
    var = jnp.mean(jnp.square(xf - mu), axis=-1, keepdims=True)
    y = (xf - mu) * lax.rsqrt(var + EPS) * g.astype(jnp.float32) + b.astype(jnp.float32)
    return y.astype(x.dtype)

def modulate(h, shift, scale):
    return h * (1 + scale) + shift

def swiglu(h, w_gu, w_down):
    a, b = jnp.split(h @ w_gu, 2, axis=-1)
    return (jax.nn.silu(a) * b) @ w_down

def axial_rope_tables(n_tokens):
    t = jnp.arange(n_tokens, dtype=jnp.int32)
    row = (t // GRID_W).astype(jnp.float32)
    col = (t % GRID_W).astype(jnp.float32)
    n_freq = HEAD_DIM // 4
    inv_freq = ROPE_BASE ** (-jnp.arange(n_freq, dtype=jnp.float32) / n_freq)
    ang = jnp.concatenate([row[:, None] * inv_freq, col[:, None] * inv_freq], axis=-1)
    return jnp.cos(ang), jnp.sin(ang)

def apply_axial_rope(x, cos, sin):
    half = HEAD_DIM // 2
    xf = x.astype(jnp.float32)
    x1, x2 = xf[..., :half], xf[..., half:]
    cs, sn = cos[None, :, None, :], sin[None, :, None, :]
    return jnp.concatenate([x1 * cs - x2 * sn, x1 * sn + x2 * cs], axis=-1).astype(x.dtype)

def split_combined(z):
    bsz, n, _ = z.shape
    qa, ka, va, qb, kb, vb, u, gates = jnp.split(z, SPLIT_POINTS, axis=-1)
    heads = lambda t, h: t.reshape(bsz, n, h, HEAD_DIM)
    return (heads(qa, NA_HEADS), heads(ka, NA_HEADS), heads(va, NA_HEADS),
            heads(qb, SW_HEADS), heads(kb, SW_KV_HEADS), heads(vb, SW_KV_HEADS), u, gates)

def neighborhood_attention(q, k, v, k_ctx, v_ctx, rpb, rows):
    bsz, n, h, d = q.shape
    n_ctx = k_ctx.shape[1]
    kh = min(NA_WIN_H, rows)
    ncb = GRID_W // NA_QBLK_W
    scale = d ** -0.5
    r = jnp.arange(rows)
    key_rows = jnp.clip(r - kh // 2, 0, rows - kh)[:, None] + jnp.arange(kh)[None]
    j = jnp.arange(ncb)
    blk_c0 = jnp.clip(j * NA_QBLK_W - NA_WIN_W // 2, 0, GRID_W - NA_KBLK_W)
    key_cols = blk_c0[:, None] + jnp.arange(NA_KBLK_W)[None]
    qg = q.reshape(bsz, rows, ncb, NA_QBLK_W, h, d)
    kg = k.reshape(bsz, rows, GRID_W, h, d)
    vg = v.reshape(bsz, rows, GRID_W, h, d)
    idx_r = key_rows[:, None, :, None]
    idx_c = key_cols[None, :, None, :]
    kb = kg[:, idx_r, idx_c]
    vb = vg[:, idx_r, idx_c]
    s_loc = jnp.einsum('brjqhd,brjyxhd->bhrjqyx', qg, kb, preferred_element_type=jnp.float32) * scale
    qcol = j[:, None] * NA_QBLK_W + jnp.arange(NA_QBLK_W)[None]
    win_c0 = jnp.clip(qcol - NA_WIN_W // 2, 0, GRID_W - NA_WIN_W)[..., None]
    kc = key_cols[:, None, :]
    in_win = (kc >= win_c0) & (kc < win_c0 + NA_WIN_W)
    dyi = key_rows - r[:, None] + (NA_WIN_H - 1)
    dxi = jnp.clip(kc - qcol[..., None] + (NA_WIN_W - 1), 0, 2 * NA_WIN_W - 2)
    bias = rpb[:, dyi[:, None, None, :, None], dxi[None, :, :, None, :]]
    s_loc = jnp.where(in_win[None, None, None, :, :, None, :], s_loc + bias.astype(jnp.float32)[None], NEG_INF)
    s_ctx = jnp.einsum('bshd,bchd->bhsc', q, k_ctx, preferred_element_type=jnp.float32) * scale
    s_ctx = s_ctx.reshape(bsz, h, rows, ncb, NA_QBLK_W, n_ctx)
    n_loc = kh * NA_KBLK_W
    p = jax.nn.softmax(jnp.concatenate([s_loc.reshape(bsz, h, rows, ncb, NA_QBLK_W, n_loc), s_ctx], axis=-1), axis=-1)
    p = p.astype(v.dtype)
    p_loc = p[..., :n_loc].reshape(bsz, h, rows, ncb, NA_QBLK_W, kh, NA_KBLK_W)
    o = (jnp.einsum('bhrjqyx,brjyxhd->brjqhd', p_loc, vb)
         + jnp.einsum('bhrjqc,bchd->brjqhd', p[..., n_loc:], v_ctx))
    return o.reshape(bsz, n, h * d)

def window_attention(q, k, v, k_ctx, v_ctx, sink):
    bsz, n, h, d = q.shape
    hkv = k.shape[2]
    g = h // hkv
    nb = n // SW_BLOCK
    scale = d ** -0.5
    pad = ((0, 0), (SW_BLOCK, SW_BLOCK), (0, 0), (0, 0))
    kp, vp = jnp.pad(k, pad), jnp.pad(v, pad)
    blk_idx = jnp.arange(nb)[:, None] * SW_BLOCK + jnp.arange(3 * SW_BLOCK)[None]
    kb, vb = kp[:, blk_idx], vp[:, blk_idx]
    qb = q.reshape(bsz, nb, SW_BLOCK, hkv, g, d)
    s_loc = jnp.einsum('bnqkgd,bnckd->bkgnqc', qb, kb, preferred_element_type=jnp.float32) * scale
    qpos = jnp.arange(n).reshape(nb, SW_BLOCK)
    kpos = blk_idx - SW_BLOCK
    valid = (jnp.abs(qpos[:, :, None] - kpos[:, None, :]) <= SW_WINDOW) & (kpos >= 0)[:, None, :] & (kpos < n)[:, None, :]
    s_loc = jnp.where(valid[None, None, None], s_loc, NEG_INF)
    s_ctx = jnp.einsum('bnqkgd,bmkd->bkgnqm', qb, k_ctx, preferred_element_type=jnp.float32) * scale
    s_sink = jnp.broadcast_to(sink.astype(jnp.float32).reshape(1, hkv, g, 1, 1, 1), s_loc.shape[:-1] + (1,))
    p = jax.nn.softmax(jnp.concatenate([s_loc, s_ctx, s_sink], axis=-1), axis=-1).astype(v.dtype)
    n_loc = 3 * SW_BLOCK
    n_ctx = k_ctx.shape[1]
    o = (jnp.einsum('bkgnqc,bnckd->bnqkgd', p[..., :n_loc], vb)
         + jnp.einsum('bkgnqm,bmkd->bnqkgd', p[..., n_loc:n_loc + n_ctx], v_ctx))
    return o.reshape(bsz, n, h * d)

def context_attention(q, k, v, sink):
    bsz, n_ctx, h, d = q.shape
    hkv = k.shape[2]
    g = h // hkv
    qg = q.reshape(bsz, n_ctx, hkv, g, d)
    s = jnp.einsum('bqkgd,bckd->bkgqc', qg, k, preferred_element_type=jnp.float32) * d ** -0.5
    if sink is None:
        p = jax.nn.softmax(s, axis=-1)
    else:
        s_sink = jnp.broadcast_to(sink.astype(jnp.float32).reshape(1, hkv, g, 1, 1), s.shape[:-1] + (1,))
        p = jax.nn.softmax(jnp.concatenate([s, s_sink], axis=-1), axis=-1)[..., :n_ctx]
    o = jnp.einsum('bkgqc,bckd->bqkgd', p.astype(v.dtype), v)
    return o.reshape(bsz, n_ctx, h * d)

def conformer_conv(u, dw_w, dw_b, ln_g, ln_b):
    a, gt = jnp.split(u, 2, axis=-1)
    h = a * jax.nn.sigmoid(gt)
    h = lax.conv_general_dilated(h, dw_w.astype(h.dtype)[:, None, :], window_strides=(1,),
                                 padding=((CONV_WIDTH // 2, CONV_WIDTH // 2),),
                                 dimension_numbers=('NWC', 'WIO', 'NWC'),
                                 feature_group_count=CONV_DIM) + dw_b
    return jax.nn.silu(layer_norm(h, ln_g, ln_b))

def merge_branches(ya, yb, yc, gate_logits, b_gate, w_oa, w_ob, w_oc, w_o):
    ga, gb, gc = jnp.split(jax.nn.sigmoid(gate_logits + b_gate), N_BRANCH, axis=-1)
    return (ga * (ya @ w_oa) + gb * (yb @ w_ob) + gc * (yc @ w_oc)) @ w_o

def second_inputs(seed: int = 0) -> dict:
    key = jax.random.key(seed)
    ks = jax.random.split(key, 32)
    f32 = jnp.float32
    D = D_MODEL
    nrm = lambda k, shape, fan_in: jax.random.normal(k, shape, f32) * fan_in ** -0.5
    small = lambda k, shape, s: jax.random.normal(k, shape, f32) * s
    return {
        'x': jax.random.normal(ks[0], (BATCH, SEQ, D), f32),
        'c': jax.random.normal(ks[1], (BATCH, D), f32),
        'ctx': jax.random.normal(ks[2], (BATCH, CTX_LEN, D), f32),
        'c_ctx': jax.random.normal(ks[3], (D,), f32),
        'w_ada': nrm(ks[4], (DEPTH, D, N_MOD * D), D),
        'b_ada': small(ks[5], (DEPTH, N_MOD * D), 0.02),
        'norm_g': 1.0 + small(ks[6], (DEPTH, 3, D), 0.05),
        'w_ffn1_gu': nrm(ks[7], (DEPTH, D, 2 * D_FF), D),
        'w_ffn1_down': nrm(ks[8], (DEPTH, D_FF, D), D_FF),
        'w_ffn2_gu': nrm(ks[9], (DEPTH, D, 2 * D_FF), D),
        'w_ffn2_down': nrm(ks[10], (DEPTH, D_FF, D), D_FF),
        'w_in': nrm(ks[11], (DEPTH, D, IN_DIM), D),
        'b_gate': small(ks[12], (DEPTH, N_BRANCH * D), 0.02),
        'na_rpb': small(ks[13], (DEPTH, NA_HEADS, 2 * NA_WIN_H - 1, 2 * NA_WIN_W - 1), 0.1),
        'sw_sink': small(ks[14], (DEPTH, SW_HEADS), 0.5),
        'conv_dw_w': nrm(ks[15], (DEPTH, CONV_WIDTH, CONV_DIM), CONV_WIDTH),
        'conv_dw_b': small(ks[16], (DEPTH, CONV_DIM), 0.02),
        'conv_ln_g': 1.0 + small(ks[17], (DEPTH, CONV_DIM), 0.05),
        'conv_ln_b': small(ks[18], (DEPTH, CONV_DIM), 0.02),
        'w_out_a': nrm(ks[19], (DEPTH, A_DIM, D), A_DIM),
        'w_out_b': nrm(ks[20], (DEPTH, B_Q_DIM, D), B_Q_DIM),
        'w_out_c': nrm(ks[21], (DEPTH, CONV_DIM, D), CONV_DIM),
        'w_out': nrm(ks[22], (DEPTH, D, D), D),
        'final_g': 1.0 + small(ks[23], (D,), 0.05),
    }

def second_block(x, c, ctx, c_ctx, w_ada, b_ada, norm_g, w_ffn1_gu, w_ffn1_down, w_ffn2_gu, w_ffn2_down,
              w_in, b_gate, na_rpb, sw_sink, conv_dw_w, conv_dw_b, conv_ln_g, conv_ln_b,
              w_out_a, w_out_b, w_out_c, w_out, final_g):
    n_tok = x.shape[1]
    rows = n_tok // GRID_W
    cos, sin = axial_rope_tables(n_tok)
    h_ctx = ctx
    silu_c = jax.nn.silu(c)
    silu_cc = jax.nn.silu(c_ctx)
    for l in range(DEPTH):
        last = l == DEPTH - 1
        mx = jnp.split((silu_c @ w_ada[l] + b_ada[l])[:, None, :], N_MOD, axis=-1)
        mc = jnp.split((silu_cc @ w_ada[l] + b_ada[l])[None, None, :], N_MOD, axis=-1)
        x = x + 0.5 * mx[2] * swiglu(modulate(rms_norm(x, norm_g[l, 0]), mx[0], mx[1]), w_ffn1_gu[l], w_ffn1_down[l])
        h_ctx = h_ctx + 0.5 * mc[2] * swiglu(modulate(rms_norm(h_ctx, norm_g[l, 0]), mc[0], mc[1]), w_ffn1_gu[l], w_ffn1_down[l])
        zx = modulate(rms_norm(x, norm_g[l, 1]), mx[3], mx[4]) @ w_in[l]
        zc = modulate(rms_norm(h_ctx, norm_g[l, 1]), mc[3], mc[4]) @ w_in[l]
        qa, ka, va, qb, kb, vb, ux, gx = split_combined(zx)
        qa_c, ka_c, va_c, qb_c, kb_c, vb_c, uc, gc = split_combined(zc)
        qb = apply_axial_rope(qb, cos, sin)
        kb = apply_axial_rope(kb, cos, sin)
        ya = neighborhood_attention(qa, ka, va, ka_c, va_c, na_rpb[l], rows)
        yb = window_attention(qb, kb, vb, kb_c, vb_c, sw_sink[l])
        yc = conformer_conv(ux, conv_dw_w[l], conv_dw_b[l], conv_ln_g[l], conv_ln_b[l])
        x = x + mx[5] * merge_branches(ya, yb, yc, gx, b_gate[l], w_out_a[l], w_out_b[l], w_out_c[l], w_out[l])
        if not last:
            ya_c = context_attention(qa_c, ka_c, va_c, None)
            yb_c = context_attention(qb_c, kb_c, vb_c, sw_sink[l])
            yc_c = conformer_conv(uc, conv_dw_w[l], conv_dw_b[l], conv_ln_g[l], conv_ln_b[l])
            h_ctx = h_ctx + mc[5] * merge_branches(ya_c, yb_c, yc_c, gc, b_gate[l], w_out_a[l], w_out_b[l], w_out_c[l], w_out[l])
        x = x + 0.5 * mx[8] * swiglu(modulate(rms_norm(x, norm_g[l, 2]), mx[6], mx[7]), w_ffn2_gu[l], w_ffn2_down[l])
        if not last:
            h_ctx = h_ctx + 0.5 * mc[8] * swiglu(modulate(rms_norm(h_ctx, norm_g[l, 2]), mc[6], mc[7]), w_ffn2_gu[l], w_ffn2_down[l])
    return rms_norm(x, final_g)


def setup_inputs(seed=0):
    out = dict(first_inputs(seed))
    for name, value in second_inputs(seed + 1).items():
        if name != "x":
            out[name + "_2"] = value
    return out


def reference(
    x, norm_w, w_in, conv_w, conv_b, gate_bias, ret_norm_w, mlstm_norm_w, w_out, final_norm_w,
    c_2, ctx_2, c_ctx_2, w_ada_2, b_ada_2, norm_g_2, w_ffn1_gu_2, w_ffn1_down_2, w_ffn2_gu_2,
    w_ffn2_down_2, w_in_2, b_gate_2, na_rpb_2, sw_sink_2, conv_dw_w_2, conv_dw_b_2, conv_ln_g_2,
    conv_ln_b_2, w_out_a_2, w_out_b_2, w_out_c_2, w_out_2, final_g_2,
):
    x = first_block(
        x, norm_w, w_in, conv_w, conv_b, gate_bias, ret_norm_w, mlstm_norm_w, w_out,
        final_norm_w,
    )
    return second_block(
        x, c_2, ctx_2, c_ctx_2, w_ada_2, b_ada_2, norm_g_2, w_ffn1_gu_2, w_ffn1_down_2,
        w_ffn2_gu_2, w_ffn2_down_2, w_in_2, b_gate_2, na_rpb_2, sw_sink_2, conv_dw_w_2,
        conv_dw_b_2, conv_ln_g_2, conv_ln_b_2, w_out_a_2, w_out_b_2, w_out_c_2, w_out_2,
        final_g_2,
    )


_drawn_inputs = setup_inputs


def setup_inputs(seed=0):
    import zlib

    import numpy as np

    out = dict(_drawn_inputs(seed))
    spreads = {}
    factors = {'conv_b': 4.732,
     'ret_norm_w': 5.351,
     'mlstm_norm_w': 6.667,
     'b_gate_2': 8.0,
     'na_rpb_2': 8.0,
     'sw_sink_2': 8.0,
     'conv_dw_b_2': 6.837,
     'conv_ln_g_2': 3.577,
     'conv_ln_b_2': 8.0}
    for name, (base, spread) in spreads.items():
        noise = np.random.default_rng([zlib.crc32(name.encode()), seed]).standard_normal(out[name].shape)
        drawn = base * np.exp(spread * noise) if base else spread * noise
        out[name] = __import__('jax').numpy.asarray(drawn.astype(out[name].dtype))
    for name, factor in factors.items():
        out[name] = (out[name] * factor).astype(out[name].dtype)
    return out
```

```python
import concourse.bass as bass
from concourse import mybir

DEPTH = 2
D = 1024
NF = 22
STOP = None


def program(nc, t, out):
    f32 = mybir.dt.float32
    f32r = mybir.dt.float32r
    ALU = mybir.AluOpType
    ACT = mybir.ActivationFunctionType
    AX = mybir.AxisListType

    sb = lambda n, s, d=f32: nc.alloc_sbuf_tensor(n, s, d)
    X = sb("X", [128, 8, 512])
    HH = sb("HH", [128, 8, 512], f32r)
    HL = sb("HL", [128, 8, 512], f32r)
    NR = 3
    RAW = sb("RAW", [128, NR, 2048])
    NS = 3
    WH = sb("WH", [128, NS, 1024], f32r)
    WL = sb("WL", [128, NS, 1024], f32r)
    CST = sb("CST", [128, 4 * 128 + 128])
    IDN, TRI, ROT, CAU = (CST[:, 128 * i:128 * i + 128] for i in range(4))
    NAM = CST[:, 512:640]
    ONE = sb("ONE", [128, 128])
    WM = sb("WM", [128, 2, 256])
    CS2 = sb("CS2", [128, 2, 256])
    VEC = sb("VEC", [128, t["vec"].shape[1]])
    SM = sb("SM", [128, 96])
    MOD = sb("MOD", [128, 9, 8, 2])
    R0 = (nc.sbuf_base + 63) // 64 * 64 if not callable(nc.sbuf_base) else (nc.sbuf_base() + 63) // 64 * 64
    REG = {}

    def at(name, off, shape, d=f32):
        if name not in REG:
            REG[name] = nc.alloc_sbuf_tensor_at(name, shape, d, offset=R0 + off)
        return REG[name]

    K = 1024
    GH = at("GH", 0, [128, NF, 512], f32r)
    GL = at("GL", 44 * K, [128, NF, 512], f32r)
    FT = at("FT", 88 * K, [128, 2, 3, 512])
    SQ = at("SQ", 0, [128, 8, 512])
    DG = at("DG", 16 * K, [128, 4, 128])
    NT = at("NT", 18 * K, [128, 4, 512])
    PJ = at("PJ", 0, [128, 24, 256])
    VA = at("VA", 24 * K, [128, 2, 512])
    VB = at("VB", 28 * K, [128, 2, 256])
    VC = at("VC", 30 * K, [128, 2, 4, 66])
    CO = at("CO", 33 * K, [128, 2, 256])
    YH1 = at("YH1", 35 * K, [128, 8, 256], f32r)
    YL1 = at("YL1", 43 * K, [128, 8, 256], f32r)
    DT = at("DT", 51 * K, [128, 4, 384])
    ALI = at("ALI", 57 * K, [128, 2, 256])
    CS1 = at("CS1", 59 * K, [128, 2, 256])
    CP = at("CP", 61 * K, [128, 4, 260])
    W8 = at("W8", 66 * K, [128, 8, 8])
    ST1 = at("ST1", 67 * K, [128, 256])
    P1 = at("P1", 68 * K, [128, 2, 512])
    PT1 = at("PT1", 72 * K, [128, 2, 512])
    O1 = at("O1", 76 * K, [128, 2, 512])
    TM1 = at("TM1", 80 * K, [128, 4, 512])
    MI = at("MI", 88 * K, [128, 6, 512])
    QK = at("QK", 0, [128, 10, 512])
    V2 = at("V2", 20 * K, [128, 4, 512])
    BM = at("BM", 28 * K, [128, 2, 6, 256])
    YH2 = at("YH2", 40 * K, [128, 8, 512], f32r)
    YL2 = at("YL2", 56 * K, [128, 8, 512], f32r)
    HP = at("HP", 72 * K, [128, 2, 2, 288])
    CV = at("CV", 77 * K, [128, 2, 512])
    P2 = at("P2", 81 * K, [128, 2, 512])
    PT2 = at("PT2", 85 * K, [128, 2, 512])
    O2 = at("O2", 89 * K, [128, 2, 384])
    ST2 = at("ST2", 92 * K, [128, 256])
    TM2 = at("TM2", 93 * K, [128, 3, 512])
    MH = at("MH", 0, [128, 8, 512], f32r)
    ML = at("ML", 16 * K, [128, 8, 512], f32r)
    MT = at("MT", 72 * K, [128, 6, 512])

    PS = [nc.alloc_psum_tensor(f"PS{i}", [128, 512], f32) for i in range(8)]
    sems = {n: nc.alloc_semaphore("s_" + n) for n in ("pe", "act", "dve", "pool", "c0", "out", "bm0", "bm1")}
    rsem = [nc.alloc_semaphore(f"s_raw{i}") for i in range(NR)]
    c1 = nc.alloc_semaphore("s_c1")
    scr = nc.dram_tensor("rpb_rows", (DEPTH, 64, 2790), f32, kind="Internal").ap()

    def layout():
        o, v = {}, 0
        for n, w in t["_vec"]:
            o[n] = v
            v += w
        return o
    VO = layout()

    def vec(n, i, w=1):
        return VEC[:, VO[n] + i:VO[n] + i + w]

    class Engine:

        def __init__(self, sem):
            self.sem, self.n, self.q = sem, 0, []

        def do(self, fn, *waits, inc=True):
            self.q.append((waits, fn, inc))
            self.n += inc
            return (self.sem, self.n)

        def now(self):
            return (self.sem, self.n)

        def emit(self, e):
            seen = {}

            def wait(w):
                if w is None:
                    return
                if isinstance(w, list):
                    for x in w:
                        wait(x)
                    return
                s, v = w
                if v > seen.get(id(s), 0):
                    e.wait_ge(s, v)
                    seen[id(s)] = v
            for waits, fn, inc in self.q:
                for w in waits:
                    wait(w)
                if fn is not None:
                    i = fn(e)
                    if inc:
                        i.then_inc(self.sem, 1)

    def trace(plan):
        pe, act, dve, pool = (Engine(sems[n]) for n in ("pe", "act", "dve", "pool"))
        sp = Engine(None)
        engines = (pe, act, dve, pool)

        def dma(dst, src, sem, *waits):
            sp.do(lambda e: e.dma_start(dst, src).then_inc(sem, 16), *waits, inc=False)

        def fence():
            now = [e.now() for e in engines]
            for e in engines:
                e.do(None, now, inc=False)
            return now

        def mm(o, l, r, start, stop, *w, inc=False):
            return pe.do(lambda e: e.matmul(o, l, r, start=start, stop=stop), *w, inc=inc)

        def tp(o, i, *w, inc=False):
            return pe.do(lambda e: e.transpose(o, i, IDN), *w, inc=inc)

        def af(o, i, f, *w, scale=1.0, bias=0.0, acc=None):
            if acc is None:
                return act.do(lambda e: e.activation(o, i, f, bias=bias, scale=scale), *w)
            return act.do(lambda e: e.activation(o, i, f, bias=bias, scale=scale, accum_out=acc), *w)

        def cp(o, i, *w):
            return act.do(lambda e: e.activation(o, i, ACT.Copy), *w)

        def vcp(o, i, *w):
            return dve.do(lambda e: e.tensor_copy(o, i), *w)

        def tt(o, a, b, op, *w, on=None):
            return (on or dve).do(lambda e: e.tensor_tensor(out=o, in0=a, in1=b, op=op), *w)

        def ts(o, a, s1, s2, op0, op1, *w):
            if op1 is None:
                return dve.do(lambda e: e.tensor_scalar(o, a, s1, None, op0), *w)
            return dve.do(lambda e: e.tensor_scalar(o, a, s1, s2, op0, op1), *w)

        def stt(o, a, s, b, op0, op1, *w):
            return dve.do(lambda e: e.scalar_tensor_tensor(out=o, in0=a, scalar=s, in1=b, op0=op0, op1=op1), *w)

        def rmax(o, i, neg, *w):
            return dve.do(lambda e: e.tensor_reduce(o, i, AX.X, ALU.max, negate=neg), *w)

        def recip(o, i, *w):
            return dve.do(lambda e: e.reciprocal(o, i), *w)

        def rpow(o, i, *w):
            return pool.do(lambda e: e.tensor_tensor(out=o, in0=i, in1=MHALF[:, 0:i.shape[-1]], op=ALU.pow), *w)

        MHALF = SM[:, 64:80]

        free = [None] * 8
        turn = [0]

        def bank():
            i = turn[0] % 8
            turn[0] += 1
            return i, PS[i], free[i]

        def done(i, *tok):
            free[i] = list(tok)

        ck = {"load": 0, "n": 0, "unit": 0, "split": 0, "rel": {}, "udone": {}, "stok": {}, "raw": 0}
        chunks, units = [], []

        def load(upto):
            while ck["load"] <= upto:
                c = ck["load"]
                kt, cols, srcs = plan[0][c]
                view = RAW[:, c % NR, 0:kt * cols].rearrange("p (k c) -> p k c", c=cols)
                for c0, c1_, src in srcs:
                    dma(view[:, :, c0:c1_], src, rsem[c % NR], ck["rel"].get(c - NR))
                ck["load"] += 1
                rawcnt[c % NR] += 16 * len(srcs)
                rawval[c] = rawcnt[c % NR]

        rawcnt, rawval = [0] * NR, {}

        def rawview(c):
            kt, cols, _ = plan[0][c] if plan else chunks[c]
            return RAW[:, c % NR, 0:kt * cols].rearrange("p (k c) -> p k c", c=cols)

        def uview(R, u, kt, w):
            return R[:, u % NS, 0:kt * w].rearrange("p (k c) -> p k c", c=w)

        def split(upto):
            while ck["split"] <= upto and ck["split"] < len(plan[1]):
                u = ck["split"]
                c, c0, c1_, last = plan[1][u]
                if c is None or any(r not in ck["rel"] for r in plan[2] if r < c):
                    break
                load(c)
                kt = plan[0][c][0]
                rv = rawview(c)[:, :, c0:c1_]
                h, l = uview(WH, u, kt, c1_ - c0), uview(WL, u, kt, c1_ - c0)
                was = ck["udone"].get(u - NS)
                a = cp(h, rv, (rsem[c % NR], rawval[c]), was)
                b = tt(l, rv, h.bitcast(f32), ALU.subtract, a, was, (rsem[c % NR], rawval[c]))
                ck["stok"][u] = [a, b]
                if last:
                    ck["rel"][c] = [a, b]
                ck["split"] += 1

        def chunk(kt, cols, srcs, us):
            c = ck["n"]
            ck["n"] += 1
            if not plan:
                chunks.append((kt, cols, srcs))
                for j, (a, b) in enumerate(us):
                    units.append((c, a, b, j == len(us) - 1))

        def unit():
            u = ck["unit"]
            ck["unit"] += 1
            if plan:
                split(u + NS - 1)
                c, a, b, _ = plan[1][u]
                kt = plan[0][c][0]
                w = ck["stok"][u]
            else:
                c, a, b, _ = units[u]
                kt = chunks[c][0]
                w = None
            ck["cur"] = u
            return uview(WH, u, kt, b - a), uview(WL, u, kt, b - a), w

        def udone(tok):
            ck["udone"][ck["cur"]] = tok

        raws = []

        def rawchunk(kt, cols, srcs):
            c = ck["n"]
            ck["n"] += 1
            if not plan:
                chunks.append((kt, cols, srcs))
                raws.append(c)
                return c, RAW[:, c % NR, 0:kt * cols].rearrange("p (k c) -> p k c", c=cols), None
            load(c)
            return c, rawview(c), (rsem[c % NR], rawval[c])

        def rawdone(c, tok):
            ck["rel"][c] = tok

        def w3(o, w, h, first, last, *waits, flip=False, inc=False):
            (wh, wl), (hh, hl) = w, h
            pairs = [(wh, hh), (wh, hl), (wl, hh)] if not flip else [(hh, wh), (hh, wl), (hl, wh)]
            for j, (l, r) in enumerate(pairs):
                tok = mm(o, l, r, first and j == 0, last and j == 2, *(waits if j == 0 else ()), inc=inc and j == 2)
            return tok

        def wsrc(w, k0, kt, c0, c1_):
            return w[128 * k0:128 * (k0 + kt), c0:c1_].rearrange("(k p) c -> p k c", p=128)

        def feat(w, c0, nt, n, ev, hin=None, kt=8, koff=0, hw=None, cols=None):
            hin = hin or (HH, HL)
            i = 0
            while i < nt:
                m = min(2, nt - i)
                chunk(kt, 128 * m, [(0, 128 * m, wsrc(w, 0, kt, c0 + 128 * i, c0 + 128 * (i + m)))],
                      [(128 * j, 128 * j + 128) for j in range(m)])
                for j in range(m):
                    wh, wl, w_ = unit()
                    b, P, fr = bank()
                    for k in range(kt):
                        tok = w3(P[:, 0:n], (wh[:, k, :], wl[:, k, :]),
                                 (hin[0][:, koff + k, 0:n], hin[1][:, koff + k, 0:n]), k == 0, k == kt - 1,
                                 w_, fr, hw, inc=k == kt - 1)
                    udone(tok)
                    done(b, *ev(i + j, P, tok))
                i += m

        def tokm(w, c0, nu, ntok, ev, hw=None):
            i = 0
            while i < nu:
                m = min(2, nu - i)
                chunk(8, 128 * m, [(0, 128 * m, wsrc(w, 0, 8, c0 + 128 * i, c0 + 128 * (i + m)))],
                      [(128 * j, 128 * j + 128) for j in range(m)])
                for j in range(m):
                    wh, wl, w_ = unit()
                    b, P, fr = bank()
                    for q in range(ntok):
                        for k in range(8):
                            tok = w3(P[:, 128 * q:128 * q + 128], (wh[:, k, :], wl[:, k, :]),
                                     (HH[:, k, 128 * q:128 * q + 128], HL[:, k, 128 * q:128 * q + 128]),
                                     k == 0, k == 7, w_, fr, hw, flip=True, inc=q == ntok - 1 and k == 7)
                    udone(tok)
                    done(b, *ev(i + j, P, tok))
                i += m

        def rstd(n):
            q = n // 128
            sq = [af(SQ[:, k, 0:n], X[:, k, 0:n], ACT.Square) if k % 2 else
                  tt(SQ[:, k, 0:n], X[:, k, 0:n], X[:, k, 0:n], ALU.mult) for k in range(8)]
            b, P, fr = bank()
            for i in range(q):
                for k in range(8):
                    tok = mm(P[:, i:i + 1], SQ[:, k, 128 * i:128 * i + 128], ONE[:, 0:1], k == 0, k == 7,
                             fr, sq[k], inc=i == q - 1 and k == 7)
            v = ts(SM[:, 0:q], P[:, 0:q], 1.0 / D, 1e-6, ALU.mult, ALU.add, tok)
            done(b, v)
            r = rpow(SM[:, 8:8 + q], SM[:, 0:q], v)
            for i in range(q):
                d = ts(DG[:, i, :], IDN, SM[:, 8 + i:9 + i], None, ALU.mult, None, r)
            b, P, fr = bank()
            tok = mm(P[:, 0:n], ONE[:, :], DG[:, 0:q, :], True, True, fr, d, inc=True)
            return b, P, tok

        def norm_in(n, gs, sh):
            b, P, tok = rstd(n)
            toks = []
            was = [None] * 4
            for k in range(8):
                T = NT[:, k % 4, :]
                for s in range(n // 256):
                    c = slice(256 * s, 256 * s + 256)
                    a = stt(T[:, c], X[:, k, c], gs(k, s), P[:, c], ALU.mult, ALU.mult, tok, was[k % 4])
                    if sh is None:
                        h = cp(HH[:, k, c], T[:, c], a)
                        l = tt(HL[:, k, c], T[:, c], HH[:, k, c].bitcast(f32), ALU.subtract, h)
                    else:
                        h = af(HH[:, k, c], T[:, c], ACT.Identity, a, bias=sh(k, s))
                        l = stt(HL[:, k, c], T[:, c], sh(k, s), HH[:, k, c].bitcast(f32), ALU.add, ALU.subtract, h)
                was[k % 4] = [h, l]
                toks = [h, l]
            done(b, a)
            return toks

        def norm_out(n, g, wr):
            b, P, tok = rstd(n)
            for k in range(8):
                a = stt(wr(k), X[:, k, 0:n], g(k), P[:, 0:n], ALU.mult, ALU.mult, tok)
            done(b, a)
            return a

        def attend(jobs, PB, PTB, ST):
            n = len(jobs)
            st = {}
            for i in range(n + 2):
                if i < n:
                    j = jobs[i]
                    nk = j["nk"]
                    b, P, fr = bank()
                    tok = mm(P[:, 0:nk], j["q"], j["k"], True, True, fr, j.get("w"), inc=True)
                    if "bias" in j:
                        tok = j["bias"](P, tok)
                    nm, sm, rs = ST[:, i:i + 1], ST[:, 64 + i:65 + i], ST[:, 128 + i:129 + i]
                    m = rmax(nm, P[:, 0:nk], True, tok)
                    if j.get("sink") is not None:
                        sk, nsk = j["sink"]
                        m = ts(nm, nm, nsk, None, ALU.min, None, m)
                    e = af(PB[:, i % 2, 0:nk], P[:, 0:nk], ACT.Exp, m, st.get(("t", i - 2)), bias=nm, acc=sm)
                    done(b, e)
                    if j.get("sink") is not None:
                        es = ST[:, 192 + i:193 + i]
                        e2 = af(es, sk, ACT.Exp, m, bias=nm)
                        e3 = tt(sm, sm, es, ALU.add, e, e2)
                        r = recip(rs, sm, e3)
                    else:
                        r = recip(rs, sm, e)
                    st["e", i], st["r", i] = e, r
                i1 = i - 1
                if 0 <= i1 < n:
                    j = jobs[i1]
                    kt = j["nk"] // 128
                    b, P, fr = bank()
                    for x in range(kt):
                        tok = tp(P[:, 128 * x:128 * x + 128], PB[:, i1 % 2, 128 * x:128 * x + 128], fr, st["e", i1],
                                 inc=x == kt - 1)
                    st["t", i1] = tok
                    c = cp(PTB[:, i1 % 2, 0:128 * kt], P[:, 0:128 * kt], tok, st.get(("pv", i1 - 2)))
                    done(b, c)
                    st["c", i1] = c
                i2 = i - 2
                if 0 <= i2 < n:
                    j = jobs[i2]
                    kt = j["nk"] // 128
                    b, P, fr = bank()
                    for x in range(kt):
                        tok = mm(P[:, 0:64], PTB[:, i2 % 2, 128 * x:128 * x + 128], j["v"](x), x == 0, x == kt - 1,
                                 fr, st["c", i2], inc=x == kt - 1)
                    st["pv", i2] = tok
                    o = ts(j["o"], P[:, 0:64], ST[:, 128 + i2:129 + i2], None, ALU.mult, None, tok, st["r", i2],
                           j["ow"]() if "ow" in j else None)
                    done(b, o)
                    if "end" in j:
                        j["end"](o)

        def ysplit(yh, yl, src, tok, scale=None):
            if scale is None:
                a = cp(yh, src, tok)
                return [a, tt(yl, src, yh.bitcast(f32), ALU.subtract, a, tok)]
            a = af(yh, src, ACT.Copy, tok, scale=scale)
            return [a, stt(yl, src, scale, yh.bitcast(f32), ALU.mult, ALU.subtract, a, tok)]

        def head_norm(src, tok, dst):
            S, A = ST1[:, 0:48], ST1[:, 48:64]
            last = None
            for g in range(8):
                a = dve.do(lambda e, g=g, i=src(g): e.bn_stats(S[:, 6 * g:6 * g + 6], i), tok)
                last = dve.do(lambda e, g=g: e.bn_aggr(A[:, 2 * g:2 * g + 2], S[:, 6 * g:6 * g + 6]), a)
            v = ts(SM[:, 16:24], ST1[:, 49:64:2], 1e-5, None, ALU.add, None, last)
            r = rpow(SM[:, 24:32], SM[:, 16:24], v)
            for g in range(8):
                a = ts(dst(g), src(g), A[:, 2 * g:2 * g + 1], SM[:, 24 + g:25 + g], ALU.subtract, ALU.mult, r, last)
            return a

        cload = [(CST[:, :], t["cst"]), (WM[:, :, :], t["wm"]), (CS2[:, :, :], t["cs2"]), (VEC[:, :], t["vec"]),
                 (X[:, :, 0:256], t["xT"].rearrange("(k p) n -> p k n", p=128)),
                 (X[:, :, 256:512], t["ctxT"].rearrange("(k p) n -> p k n", p=128))]
        for o, i in cload:
            act.do(lambda e, o=o, i=i: e.dma_start(o, i).then_inc(sems["c0"], 16), inc=False)
        c0 = (sems["c0"], 16 * len(cload))
        for l in range(DEPTH):
            act.do(lambda e, l=l: e.dma_start(scr[l, :, :], bass.AP(tensor=t["rpb"].tensor, offset=2790 * l,
                   ap=[[0, 64], [1, 2790]])).then_inc(sems["bm0"], 16), inc=False)
        m1 = dve.do(lambda e: e.memset(ONE[:, :], 1.0))
        m1 = dve.do(lambda e: e.memset(MHALF, -0.5))
        for e in engines:
            e.do(None, c0, m1, inc=False)

        for l in range(DEPTH):
            w_in, w_out = t["w_in"][l], t["w_out"][l]
            f = fence()
            c1n = 0
            for o, i in ((DT[:, :, :], t["decay"]), (ALI[:, :, :], t["alibi"]), (CS1[:, :, :], t["cs1"]),
                         (W8[:, :, :], w_in[:, 4352:4360].rearrange("(k p) c -> p k c", p=128))):
                act.do(lambda e, o=o, i=i: e.dma_start(o, i).then_inc(c1, 16), inc=False)
                c1n += 16
            c1t = (c1, c1n * (l + 1))
            hw = norm_in(256, lambda k, s: vec("norm_w", 8 * l + k), None)
            fence()
            N = 256
            z = dve.do(lambda e: e.memset(CP[:, :, 0:3], 0.0))
            z = dve.do(lambda e: e.memset(VC[:, :, :, 64:65], 1.0))

            b, P, fr = bank()
            for q in range(2):
                for k in range(8):
                    for j, hx in enumerate((HH, HL)):
                        tok = mm(P[:, 8 * q:8 * q + 8], hx[:, k, 128 * q:128 * q + 128].bitcast(f32), W8[:, k, :],
                                 k == 0 and j == 0, k == 7 and j == 1, fr, c1t, inc=q == 1 and k == 7 and j == 1)
            IF = MI[:, 0, 0:16].rearrange("p (a b) -> p a b", b=8)
            g = None
            for q in range(2):
                g = tt(IF[:, q, :], P[:, 8 * q:8 * q + 8], vec("gate_bias", 8 * l, 8), ALU.add, tok)
            done(b, g)
            F_, I_ = IF[:, :, 4:8], IF[:, :, 0:4]
            m8 = lambda i: MI[:, 0, 16 + 8 * i:24 + 8 * i].rearrange("p (a b) -> p a b", b=4)
            LS, T1, T2, BB, RR, UU, NU, WI, EM, DN = (m8(i) for i in range(10))
            BL, RH, MS, WS, MX, RHO = (m8(10 + i)[:, 0, :] for i in range(6))
            a = stt(T1, F_, -1.0, F_, ALU.mult, ALU.max, g)
            a = af(T2, T1, ACT.Exp, a, scale=-1.0)
            a = af(T1, T2, ACT.Ln, a, bias=ONE[:, 0:1])
            a = stt(LS, F_, 0.0, T1, ALU.min, ALU.subtract, a)
            b, P, fr = bank()
            mm(P[:, 0:8], TRI, MI[:, 0, 16:24], True, True, fr, a)
            tok = mm(P[:, 8:12], ONE[:, :], MI[:, 0, 16:20], True, True, inc=True)
            b1 = vcp(BB, P[:, 0:8].rearrange("p (a b) -> p a b", b=4), tok)
            b2 = vcp(BL, P[:, 8:12], tok)
            done(b, b2)
            gr = tt(RR, I_, BB, ALU.subtract, b1)

            def to(slot, scale=None):
                def ev(i, P, tok):
                    return [cp(PJ[:, slot + i, :], P[:, 0:N], tok) if scale is None else
                            af(PJ[:, slot + i, :], P[:, 0:N], ACT.Copy, tok, scale=scale)]
                return ev

            def to_silu2(slot):
                def ev(i, P, tok):
                    T = TM1[:, i % 2, 0:N]
                    a = af(T, P[:, 0:N], ACT.Tanh, tok, silu_w[i % 2], scale=0.5)
                    c = stt(PJ[:, slot + i, :], T, 1.0, P[:, 0:N], ALU.add, ALU.mult, a)
                    silu_w[i % 2] = c
                    return [c]
                return ev
            silu_w = [None, None]

            def to_tok(dst):
                def ev(i, P, tok):
                    return [cp(dst(i), P[:, 0:256].rearrange("p (q c) -> p q c", c=128), tok)]
                return ev
            feat(w_in, 0, 4, N, to(0, 0.125))
            feat(w_in, 512, 4, N, to(4))
            tokm(w_in, 1024, 4, 2, to_tok(lambda i: VA[:, :, 128 * i:128 * i + 128]))
            feat(w_in, 1536, 4, N, to_silu2(8))
            feat(w_in, 2048, 4, N, to(12))
            tokm(w_in, 2560, 2, 2, to_tok(lambda i: VB[:, :, 128 * i:128 * i + 128]))
            feat(w_in, 2816, 2, N, to_silu2(16))
            feat(w_in, 3072, 4, N, lambda i, P, tok: [cp(CP[:, i, 3:259], P[:, 0:N], tok)])

            def vc_ev(i, P, tok):
                r = []
                for q in range(2):
                    r.append(cp(VC[:, q, 2 * i:2 * i + 2, 0:64],
                                P[:, 128 * q:128 * q + 128].rearrange("p (h d) -> p h d", d=64), tok))
                return r
            tokm(w_in, 3584, 2, 2, vc_ev)

            def co_ev(i, P, tok):
                v = CO[:, :, 128 * i:128 * i + 128]
                a = af(v, P[:, 0:256].rearrange("p (q c) -> p q c", c=128), ACT.Tanh, tok, scale=0.5)
                ts(v, v, 0.5, 0.5, ALU.mult, ALU.add, a)
                return [a]
            tokm(w_in, 3840, 2, 2, co_ev)
            feat(w_in, 4096, 2, N, to_silu2(18))
            fence()

            hv = ts(SM[:, 32:34], vec("ret_norm_w", 2 * l, 2), 0.5, None, ALU.mult, None)
            hv = ts(SM[:, 34:36], vec("mlstm_norm_w", 2 * l, 2), 0.5, None, ALU.mult, None)

            def half(t_, h):
                return t_[64 * (h % 2):64 * (h % 2) + 64]

            def yout(src, tok, nf, gslot, yslot, sc):
                for i in range(nf):
                    b, P, fr = bank()
                    for q in range(2):
                        tk = tp(P[:, 128 * q:128 * q + 128], src(q, i), tok, fr, inc=q == 1)
                    T = TM1[:, i % 2, 256:512]
                    a = stt(T, PJ[:, gslot + i, :], sc(i), P[:, 0:256], ALU.mult, ALU.mult, tk, yw[i % 2])
                    done(b, a)
                    yw[i % 2] = ysplit(YH1[:, yslot + i, :], YL1[:, yslot + i, :], T, a)
            yw = [None, None]

            jobs = []
            for h in range(8):
                for q in range(2):
                    nk = 128 * (q + 1)

                    def bias(P, tok, h=h, q=q, nk=nk):
                        return stt(P[:, 0:nk], ALI[:, q, 0:nk], 2.0 ** -(h + 1), P[:, 0:nk], ALU.mult, ALU.add, tok, c1t)
                    jobs.append(dict(q=half(PJ, h)[:, h // 2, 128 * q:128 * q + 128], k=half(PJ, h)[:, 4 + h // 2, 0:nk],
                                     nk=nk, bias=bias, v=lambda x, h=h: VA[:, x, 64 * h:64 * h + 64],
                                     o=O1[:, q, 64 * h:64 * h + 64]))
            attend(jobs, P1, PT1, ST1)
            yout(lambda q, i: O1[:, q, 128 * i:128 * i + 128], dve.now(), 4, 8, 0, lambda i: 0.5)

            rt = []
            for i in range(4):
                b, P, fr = bank()
                tok = mm(P[:, 0:256], ROT, PJ[:, 12 + i, :], True, True, fr, inc=True)
                T = TM1[:, 2, 0:256]
                a = tt(T, P[:, 0:256], CS1[:, 1, :], ALU.mult, tok, c1t, rt)
                done(b, a)
                c = tt(PJ[:, 12 + i, :], PJ[:, 12 + i, :], CS1[:, 0, :], ALU.mult, tok, c1t)
                rt = tt(PJ[:, 12 + i, :], PJ[:, 12 + i, :], T, ALU.add, a, c)
            bo, PO, fro = bank()
            pw = {}
            for h in range(4):
                b, P, fr = bank()
                kk, qq = half(PJ, h)[:, 14 + h // 2, :], half(PJ, h)[:, 12 + h // 2, :]
                mm(P[:, 0:256], kk[:, 0:128], qq[:, 0:256], True, True, fr, rt)
                tok = mm(P[:, 256:384], kk[:, 128:256], qq[:, 128:256], True, True, inc=True)
                T = P1[:, h % 2, 0:384]
                a = tt(T, P[:, 0:384], DT[:, h, :], ALU.mult, tok, pw.get(h - 2), pe.now())
                done(b, a)
                vv = lambda x: VB[:, x, 64 * h:64 * h + 64]
                mm(PO[:, 64 * h:64 * h + 64], T[:, 0:128], vv(0), True, True, a, fro)
                mm(PO[:, 256 + 64 * h:320 + 64 * h], T[:, 128:256], vv(0), True, False)
                pw[h] = mm(PO[:, 256 + 64 * h:320 + 64 * h], T[:, 256:384], vv(1), False, True, inc=True)
            YT = TM1[:, 3, :]
            a = head_norm(lambda g: PO[:, 64 * g:64 * g + 64], pw[3], lambda g: YT[:, 64 * g:64 * g + 64])
            done(bo, a)
            yout(lambda q, i: YT[:, 256 * q + 128 * i:256 * q + 128 * i + 128], a, 2, 16, 4, lambda i: SM[:, 32 + i:33 + i])

            hw_ = ts(ST1[:, 64:80], vec("conv_w", 16 * l, 16), 0.5, None, ALU.mult, None)
            hb_ = ts(ST1[:, 80:84], vec("conv_b", 4 * l, 4), 0.5, None, ALU.mult, None)
            cq = []
            for i in range(4):
                A = PJ[:, 20 + i, :]
                a = ts(A, CP[:, i, 0:256], ST1[:, 64 + i:65 + i], ST1[:, 80 + i:81 + i], ALU.mult, ALU.add, hw_, hb_)
                for j in range(1, 4):
                    a = stt(A, CP[:, i, j:j + 256], ST1[:, 64 + 4 * j + i:65 + 4 * j + i], A, ALU.mult, ALU.add, a)
                T = TM1[:, i % 2, 0:256]
                a = af(T, A, ACT.Tanh, a, cq[i - 2] if i > 1 else None)
                cq.append(stt(A, T, 1.0, A, ALU.add, ALU.mult, a))
            NUM = MI[:, 5, 0:260].rearrange("p (h d) -> p h d", d=65)
            HC = TM1[:, 3, :]
            state = None
            for c in range(2):
                b, P, fr = bank()
                for h in range(4):
                    d = ts(MI[:, 1, 128 * h:128 * h + 128], IDN, RR[:, c, h:h + 1], None, ALU.mult, None, gr, pe.now())
                tok = mm(P[:, :], ONE[:, :], MI[:, 1, :], True, True, fr, d, inc=True)
                M1 = MI[:, 2, :]
                for h in range(4):
                    a = tt(M1[:, 128 * h:128 * h + 128], P[:, 128 * h:128 * h + 128], CAU, ALU.add, tok, act.now())
                mx = rmax(MX, M1.rearrange("p (h s) -> p h s", s=128), False, a)
                if c == 0:
                    rho = rmax(RHO, P[:, :].rearrange("p (h s) -> p h s", s=128), False, tok)
                    done(b, rho)
                    rho = ts(RHO, RHO, 0.0, None, ALU.max, None, rho)
                    ms1 = tt(MS, BL, RHO, ALU.add, rho)
                    u = ts(UU[:, c, :], MX, 0.0, None, ALU.max, None, mx)
                else:
                    done(b, a)
                    u = tt(UU[:, c, :], MX, MS, ALU.max, mx, ms1)
                nu = ts(NU[:, c, :], UU[:, c, :], -1.0, None, ALU.mult, None, u)
                W = MI[:, 3, :]
                for h in range(4):
                    w = af(W[:, 128 * h:128 * h + 128], M1[:, 128 * h:128 * h + 128], ACT.Exp, nu, dve.now(),
                           bias=NU[:, c, h:h + 1])
                mt = tt(DN[:, c, :], BB[:, c, :], UU[:, c, :], ALU.add, u)
                em = af(EM[:, c, :], DN[:, c, :], ACT.Exp, mt, scale=-1.0)
                if c == 1:
                    wi = tt(WI[:, c, :], MS, UU[:, c, :], ALU.subtract, u)
                    wi = af(WI[:, c, :], WI[:, c, :], ACT.Exp, wi)
                S = P1[:, 0, :]
                pair = lambda v: v.rearrange("p (a b s) -> p a b s", b=2, s=128)
                for o in range(2):
                    b, P, fr = bank()
                    for x in range(2):
                        tok = mm(P[:, 128 * x:128 * x + 128], half(PJ, o)[:, 20 + x, 128 * c:128 * c + 128],
                                 half(PJ, o)[:, 22 + x, 128 * c:128 * c + 128], True, True, fr, cq[3], inc=x == 1)
                    a = stt(pair(S)[:, :, o, :], P[:, 0:256].rearrange("p (a s) -> p a s", s=128), 0.125,
                            pair(W)[:, :, o, :], ALU.mult, ALU.mult, tok, w, pe.now())
                    done(b, a)
                b, P, fr = bank()
                for h in range(4):
                    tok = tp(P[:, 128 * h:128 * h + 128], S[:, 128 * h:128 * h + 128], fr, a, inc=h == 3)
                PT = PT1[:, 0, :]
                a = cp(PT, P[:, :], tok)
                done(b, a)
                b, P, fr = bank()
                for h in range(4):
                    tok = mm(P[:, 65 * h:65 * h + 65], PT[:, 128 * h:128 * h + 128], VC[:, c, h, 0:65], True, True,
                             fr, a, inc=h == 3)
                a = vcp(NUM, P[:, 0:260].rearrange("p (h d) -> p h d", d=65), tok)
                done(b, a)
                if c == 0:
                    ws = tt(WS, RR[:, 0, :], RHO, ALU.subtract, rho)
                    ws = af(WS, WS, ACT.Exp, ws)
                    b, P, fr = bank()
                    for i in range(2):
                        tok = tp(P[:, 128 * i:128 * i + 128], PJ[:, 22 + i, 0:128], fr, cq[3], inc=i == 1)
                    KT = MI[:, 4, 0:256]
                    for h in range(4):
                        kx = ts(KT[:, 64 * h:64 * h + 64], P[:, 64 * h:64 * h + 64], WS[:, h:h + 1], 0.125, ALU.mult,
                                ALU.mult, tok, ws)
                    done(b, kx)
                    CT = MI[:, 4, 256:256 + 130]
                    b, P, fr = bank()
                    for h in range(4):
                        o = P[64 * (h % 2):64 * (h % 2) + 64, 65 * (h // 2):65 * (h // 2) + 65]
                        tok = mm(o, KT[:, 64 * h:64 * h + 64], VC[:, 0, h, 0:65], True, True, fr, kx, inc=h == 3)
                    state = vcp(CT, P[:, 0:130], tok)
                    done(b, state)
                else:
                    for o in range(2):
                        b, P, fr = bank()
                        for x in range(2):
                            tok = mm(P[:, 65 * x:65 * x + 65], half(PJ, o)[:, 20 + x, 128:256],
                                     half(MI, o)[:, 4, 256 + 65 * x:256 + 65 * x + 65], True, True,
                                     fr, state, inc=x == 1)
                        for x in range(2):
                            h = 2 * x + o
                            a = stt(NUM[:, h, :], P[:, 65 * x:65 * x + 65], WI[:, 1, h:h + 1], NUM[:, h, :], ALU.mult,
                                    ALU.add, tok, wi, a)
                        done(b, a)
                dn = stt(DN[:, c, :], NUM[:, :, 64], -1.0, NUM[:, :, 64], ALU.mult, ALU.max, a, em)
                dn = tt(DN[:, c, :], DN[:, c, :], EM[:, c, :], ALU.max, dn)
                dn = recip(DN[:, c, :], DN[:, c, :], dn)
                for h in range(4):
                    hc = stt(HC[:, 256 * c + 64 * h:256 * c + 64 * h + 64], NUM[:, h, 0:64], DN[:, c, h:h + 1],
                             CO[:, c, 64 * h:64 * h + 64], ALU.mult, ALU.mult, dn, pe.now())
            YC = TM1[:, 2, :]
            a = head_norm(lambda g: HC[:, 64 * g:64 * g + 64], hc, lambda g: YC[:, 64 * g:64 * g + 64])
            yout(lambda q, i: YC[:, 256 * q + 128 * i:256 * q + 128 * i + 128], a, 2, 18, 6, lambda i: SM[:, 34 + i:35 + i])

            ywt = [act.now(), dve.now()]
            feat(w_out, 0, 8, N, lambda i, P, tok: [tt(X[:, i, 0:N], P[:, 0:N], X[:, i, 0:N], ALU.add, tok)],
                 hin=(YH1, YL1), hw=ywt)
        fence()
        if STOP == 1:
            a = norm_out(256, lambda k: vec("final_norm_w", k), lambda k: NT[:, k // 2, 256 * (k % 2):256 * (k % 2) + 256])
            dma(out.rearrange("(k p) n -> p k n", p=128), NT[:, :, :].rearrange("p a (b n) -> p (a b) n", b=2), sems["out"], a)
            sp.do(None, (sems["out"], 16), inc=False)
            return pe, act, dve, pool, sp, (chunks, units, raws)
        norm_out(256, lambda k: vec("final_norm_w", k), lambda k: X[:, k, 0:256])

        a = af(SM[:, 80:96], vec("cc", 0, 16), ACT.Tanh, scale=0.5)
        cc = stt(SM[:, 36:52], SM[:, 80:96], 1.0, vec("cc", 0, 16), ALU.add, ALU.mult, a)
        CC = SM[:, 36:52].rearrange("p (k s) -> p k s", s=2)
        bmn = 0
        for l in range(DEPTH):
            last = l == DEPTH - 1
            w_ada = t["w_ada_2"][l]
            fence()
            for j in range(18):
                b, P, fr = bank()
                for m in range(2):
                    c, rv, rw = rawchunk(8, 256, [(0, 256, wsrc(w_ada, 0, 8, 512 * j + 256 * m, 512 * j + 256 * m + 256))])
                    for x in range(2):
                        o = P[:, 4 * m + 2 * x:4 * m + 2 * x + 2]
                        for k in range(8):
                            tok = mm(o, rv[:, k, 128 * x:128 * x + 128], CC[:, k, :], k == 0, k == 7, fr, rw, cc,
                                     inc=k == 7 and x == 1)
                    rawdone(c, tok)
                i0, k0 = (4 * j) // 8, (4 * j) % 8
                ba = vec("b_ada", 72 * l + 4 * j, 4)
                for s in range(2):
                    a = stt(MOD[:, i0, k0:k0 + 4, s], P[:, s:8:2], 0.5, ba, ALU.mult, ALU.add, tok)
                done(b, a)
            for i in (2, 8):
                a = ts(MOD[:, i, :, :], MOD[:, i, :, :], 0.5, None, ALU.mult, None, a)
            for i, n in ((1, 0), (4, 1), (7, 2)):
                for s in range(2):
                    a = stt(MOD[:, i, :, s], MOD[:, i, :, s], 1.0, vec("norm_g", 24 * l + 8 * n, 8), ALU.add, ALU.mult, a)
            fence()

            def ffn(gu, dn, n, i0):
                norm_in(n, lambda k, s: MOD[:, i0 + 1, k, s:s + 1], lambda k, s: MOD[:, i0, k, s:s + 1])
                fence()
                ft = [None, None]
                for j in range(11):
                    ab = []
                    for x in range(2):
                        col = 2816 * x + 256 * j
                        chunk(8, 256, [(0, 256, wsrc(gu, 0, 8, col, col + 256))], [(0, 128), (128, 256)])
                        for m in range(2):
                            wh, wl, w_ = unit()
                            b, P, fr = bank()
                            for k in range(8):
                                tok = w3(P[:, 0:n], (wh[:, k, :], wl[:, k, :]), (HH[:, k, 0:n], HL[:, k, 0:n]),
                                         k == 0, k == 7, w_, fr, inc=k == 7)
                            udone(tok)
                            ab.append((b, P, tok))
                            if x == 1:
                                (ba_, PA, ta), (bb, PB_, tb) = ab[m], ab[2 + m]
                                i = 2 * j + m
                                T, M_, G_ = (FT[:, m, y, 0:n] for y in range(3))
                                a = af(T, PA[:, 0:n], ACT.Tanh, ta, ft[m], scale=0.5)
                                c = stt(M_, T, 1.0, PA[:, 0:n], ALU.add, ALU.mult, a)
                                g = stt(G_, M_, 0.5, PB_[:, 0:n], ALU.mult, ALU.mult, c, tb)
                                done(ba_, c)
                                done(bb, g)
                                ft[m] = ysplit(GH[:, i, 0:n], GL[:, i, 0:n], G_, g)
                gt = [act.now(), dve.now()]
                for j in range(4):
                    bk = [bank(), bank()]
                    for k0, kt in ((0, 8), (8, 8), (16, 6)):
                        chunk(kt, 256, [(0, 256, wsrc(dn, k0, kt, 256 * j, 256 * j + 256))], [(0, 128), (128, 256)])
                        for m in range(2):
                            wh, wl, w_ = unit()
                            b, P, fr = bk[m]
                            for k in range(kt):
                                kk = k0 + k
                                tok = w3(P[:, 0:n], (wh[:, k, :], wl[:, k, :]), (GH[:, kk, 0:n], GL[:, kk, 0:n]),
                                         kk == 0, kk == 21, w_, fr, gt, inc=k == kt - 1)
                            udone(tok)
                            if k0 == 16:
                                i = 2 * j + m
                                for s in range(n // 256):
                                    c = slice(256 * s, 256 * s + 256)
                                    a = stt(X[:, i, c], P[:, c], MOD[:, i0 + 2, i, s:s + 1], X[:, i, c], ALU.mult,
                                            ALU.add, tok)
                                done(b, a)
                fence()

            def mixer():
                n = 512
                nq = 256 if last else 512
                w_in, bg = t["w_in_2"][l], "b_gate"
                nb = 0
                fw = [e.now() for e in engines]
                for r in range(4):
                    for h in range(6):
                        src = bass.AP(tensor=scr.tensor, offset=(l * 64) * 2790 + 465 * h + (7 - r) * 31 + 15,
                                      ap=[[2789, 64], [31, 4], [1, 64]])
                        pp = 64 * (r % 2)
                        act.do(lambda e, src=src, pp=pp, r=r, h=h: e.dma_start(
                            BM[pp:pp + 64, r // 2, h, :].rearrange("p (y x) -> p y x", x=64), src)
                            .then_inc(sems["bm1"], 16), fw, (sems["bm0"], 32), inc=False)
                        nb += 16
                bmt = (sems["bm1"], nb * (l + 1))
                norm_in(n, lambda k, s: MOD[:, 4, k, s:s + 1], lambda k, s: MOD[:, 3, k, s:s + 1])
                f = fence()
                z = dve.do(lambda e: e.memset(HP[:, :, :, :], 0.0))

                def to(slot, w, scale=1.0):
                    return lambda i, P, tok: [af(QK[:, slot + i, 0:w], P[:, 0:w], ACT.Copy, tok, scale=scale)]

                def tov(c):
                    return lambda i, P, tok: [cp(V2[:, :, c + 128 * i:c + 128 * i + 128],
                                                 P[:, :].rearrange("p (q c) -> p q c", c=128), tok)]
                for h in range(6):
                    for q in range(2):
                        v = BM[:, q, h, :].rearrange("p (y x) -> p y x", x=64)
                        mul = bass.AP(tensor=NAM.tensor, offset=NAM.offset, ap=[list(NAM.ap[0]), [0, 4], [1, 64]])
                        add = bass.AP(tensor=NAM.tensor, offset=NAM.offset + 64, ap=[list(NAM.ap[0]), [0, 4], [1, 64]])
                        a = tt(v, v, mul, ALU.mult, bmt)
                        bmr = tt(v, v, add, ALU.add, a)
                feat(w_in, 0, 3, nq, to(0, nq, 0.125))
                feat(w_in, 384, 3, n, to(3, n))
                tokm(w_in, 768, 3, 4, tov(0))
                for j in range(3):
                    c_ = 1152 + 64 * j
                    chunk(8, 128, [(0, 64, wsrc(w_in, 0, 8, c_, c_ + 64)),
                                   (64, 128, wsrc(w_in, 0, 8, c_ + 192, c_ + 256))], [(0, 128)])
                    wh, wl, w_ = unit()
                    b, P, fr = bank()
                    for k in range(8):
                        tok = w3(P[:, 0:nq], (wh[:, k, :], wl[:, k, :]), (HH[:, k, 0:nq], HL[:, k, 0:nq]),
                                 k == 0, k == 7, w_, fr, inc=k == 7)
                    udone(tok)
                    done(b, *to(6 + j, nq, 0.125)(0, P, tok))
                feat(w_in, 1536, 1, n, to(9, n))
                tokm(w_in, 1664, 1, 4, tov(384))
                ub = []

                def uev(i, P, tok):
                    if i < 2:
                        ub.append((P, tok))
                        return [cp(TM2[:, i, 0:nq], P[:, 0:nq], tok)]
                    T = TM2[:, 2, 0:nq]
                    a = af(T, P[:, 0:nq], ACT.Tanh, tok, dve.now(), scale=0.5)
                    b_ = ts(T, T, 0.5, 0.5, ALU.mult, ALU.add, a)
                    tt(HP[:, i - 2, 0:nq // 256, 15:271], T.rearrange("p (s n) -> p s n", n=256),
                       TM2[:, i - 2, 0:nq].rearrange("p (s n) -> p s n", n=256), ALU.mult, b_, z)
                    return [a]
                feat(w_in, 1792, 4, nq, uev)
                fence()
                rt = None
                for i in (6, 7, 8, 9):
                    w = 256 if i < 9 else 256
                    b, P, fr = bank()
                    tok = mm(P[:, 0:256], ROT, QK[:, i, 0:256], True, True, fr, inc=True)
                    T = TM2[:, 0, 0:256]
                    a = tt(T, P[:, 0:256], CS2[:, 1, 0:256], ALU.mult, tok, rt)
                    done(b, a)
                    c = tt(QK[:, i, 0:256], QK[:, i, 0:256], CS2[:, 0, 0:256], ALU.mult, tok)
                    rt = tt(QK[:, i, 0:256], QK[:, i, 0:256], T, ALU.add, a, c)
                ns = ts(SM[:, 52:58], vec("sink", 6 * l, 6), -1.0, None, ALU.mult, None)
                nq_t = nq // 128
                cnt = [0]

                def ytile(o, yslot, q, ob):
                    b, P, fr = bank()
                    for i in range(3):
                        tok = tp(P[:, 128 * i:128 * i + 128], O2[:, ob, 128 * i:128 * i + 128], fr, o, inc=i == 2)
                    yh = YH2[:, yslot:yslot + 3, 128 * q:128 * q + 128]
                    yl = YL2[:, yslot:yslot + 3, 128 * q:128 * q + 128]
                    Pv = P[:, 0:384].rearrange("p (i n) -> p i n", n=128)
                    a = cp(yh, Pv, tok)
                    c = tt(yl, Pv, yh.bitcast(f32), ALU.subtract, a)
                    done(b, c)
                    ow[ob] = tok
                ow = [None, None]
                for br in range(2):
                    jobs = []
                    for q in range(nq_t):
                        ctx_q = q >= 2
                        k0, nk = (256, 256) if ctx_q else (0, 512)
                        for h in range(6):
                            if br == 0:
                                hs, qt, kt = h % 2, h // 2, 3 + h // 2
                            else:
                                hs, qt, kt = h // 3, 6 + h % 3, 9
                            r0 = slice(64 * hs, 64 * hs + 64)
                            vc = 64 * h if br == 0 else 384 + 64 * (h // 3)
                            ob = cnt[0] % 2
                            job = dict(q=QK[r0, qt, 128 * q:128 * q + 128], k=QK[r0, kt, k0:k0 + nk], nk=nk,
                                       v=lambda x, vc=vc, k0=k0: V2[:, k0 // 128 + x, vc:vc + 64],
                                       o=O2[:, ob, 64 * h:64 * h + 64], w=rt)
                            if not ctx_q:
                                tab = BM[:, q, h, :] if br == 0 else WM[:, q, :]

                                def bias(P, tok, tab=tab):
                                    return tt(P[:, 0:256], P[:, 0:256], tab, ALU.add, tok, bmr)
                                job["bias"] = bias
                            if br == 1:
                                job["sink"] = (vec("sink", 6 * l + h, 1), SM[:, 52 + h:53 + h])
                            if h == 0:
                                job["ow"] = lambda ob=ob: ow[ob]
                            if h == 5:
                                job["end"] = lambda o, q=q, ob=ob, br=br: ytile(o, 3 * br, q, ob)
                            jobs.append(job)
                        cnt[0] += 1
                    attend(jobs, P2, PT2, ST2)
                for i in range(2):
                    A = CV[:, i, 0:nq].rearrange("p (s n) -> p s n", n=256)
                    a = None
                    for j in range(31):
                        x = HP[:, i, 0:nq // 256, j:j + 256]
                        wv = vec("dw_w", 62 * l + 2 * j + i)
                        if j == 0:
                            a = ts(A, x, wv, vec("dw_b", 2 * l + i), ALU.mult, ALU.add)
                        else:
                            a = stt(A, x, wv, A, ALU.mult, ALU.add, a)
                for q in range(nq_t):
                    b, P, fr = bank()
                    for i in range(2):
                        tok = tp(P[:, 128 * i:128 * i + 128], CV[:, i, 128 * q:128 * q + 128], fr, a, inc=i == 1)
                    S6 = ST2[:, 240:246]
                    s = dve.do(lambda e, P=P: e.bn_stats(S6, P[:, 0:256]), tok)
                    s = dve.do(lambda e: e.bn_aggr(ST2[:, 246:248], S6), s)
                    v = ts(SM[:, 16:17], ST2[:, 247:248], 1e-6, None, ALU.add, None, s)
                    r = rpow(SM[:, 24:25], SM[:, 16:17], v)
                    T = TM2[:, q % 2, 0:256]
                    y = ts(T, P[:, 0:256], ST2[:, 246:247], SM[:, 24:25], ALU.subtract, ALU.mult, r, s, pe.now())
                    done(b, y)
                    b, P, fr = bank()
                    for i in range(2):
                        tok = tp(P[:, 128 * i:128 * i + 128], T[:, 128 * i:128 * i + 128], fr, y, inc=i == 1)
                    for i in range(2):
                        U = TM2[:, 2, 128 * i:128 * i + 128]
                        V_ = TM2[:, 2, 256 + 128 * i:384 + 128 * i]
                        u = ts(U, P[:, 128 * i:128 * i + 128], vec("ln_g", 2 * l + i), vec("ln_b", 2 * l + i), ALU.mult,
                               ALU.add, tok, act.now())
                        w = af(V_, U, ACT.Tanh, u, dve.now(), scale=0.5)
                        w = stt(V_, V_, 1.0, U, ALU.add, ALU.mult, w)
                        ysplit(YH2[:, 6 + i, 128 * q:128 * q + 128], YL2[:, 6 + i, 128 * q:128 * q + 128], V_, w, 0.5)
                    done(b, u)
                fence()
                hb = ts(ST2[:, 0:24], vec("b_gate", 24 * l, 24), 0.5, None, ALU.mult, None)
                mw = [None] * 2
                for mp in range(4):
                    acc = [None, None]
                    for br, (wo, kb, kn) in enumerate((("w_out_a_2", 0, 3), ("w_out_b_2", 3, 3), ("w_out_c_2", 6, 2))):
                        col = 2304 + 1024 * br + 256 * mp
                        chunk(8, 256, [(0, 256, wsrc(w_in, 0, 8, col, col + 256))], [(0, 128), (128, 256)])
                        gb = []
                        for m in range(2):
                            wh, wl, w_ = unit()
                            b, P, fr = bank()
                            for k in range(8):
                                tok = w3(P[:, 0:nq], (wh[:, k, :], wl[:, k, :]), (HH[:, k, 0:nq], HL[:, k, 0:nq]),
                                         k == 0, k == 7, w_, fr, inc=k == 7)
                            udone(tok)
                            T = MT[:, m, 0:nq]
                            a = af(T, P[:, 0:nq], ACT.Tanh, tok, hb, mw[m], scale=0.5,
                                   bias=ST2[:, 8 * br + 2 * mp + m:8 * br + 2 * mp + m + 1])
                            done(b, a)
                            gb.append(a)
                        chunk(kn, 256, [(0, 256, wsrc(t[wo][l], 0, kn, 256 * mp, 256 * mp + 256))], [(0, 256)])
                        wh, wl, w_ = unit()
                        for m in range(2):
                            b, P, fr = bank()
                            for k in range(kn):
                                tok = w3(P[:, 0:nq], (wh[:, k, 128 * m:128 * m + 128], wl[:, k, 128 * m:128 * m + 128]),
                                         (YH2[:, kb + k, 0:nq], YL2[:, kb + k, 0:nq]), k == 0, k == kn - 1, w_, fr,
                                         inc=k == kn - 1)
                            A = MT[:, 2 + m, 0:nq]
                            if br == 0:
                                acc[m] = stt(A, MT[:, m, 0:nq], 1.0, P[:, 0:nq], ALU.add, ALU.mult, tok, gb[m])
                                mw[m] = acc[m]
                            else:
                                B_ = MT[:, 4 + m, 0:nq]
                                x = stt(B_, MT[:, m, 0:nq], 1.0, P[:, 0:nq], ALU.add, ALU.mult, tok, gb[m])
                                mw[m] = x
                                acc[m] = tt(A, A, B_, ALU.add, x, acc[m])
                            done(b, mw[m])
                        udone(tok)
                    for m in range(2):
                        i = 2 * mp + m
                        ysplit(MH[:, i, 0:nq], ML[:, i, 0:nq], MT[:, 2 + m, 0:nq], acc[m], 0.5)
                        mw[m] = [act.now(), dve.now()]
                mt_ = [act.now(), dve.now()]

                def xev(i, P, tok):
                    for s in range(nq // 256):
                        c = slice(256 * s, 256 * s + 256)
                        a = stt(X[:, i, c], P[:, c], MOD[:, 5, i, s:s + 1], X[:, i, c], ALU.mult, ALU.add, tok)
                    return [a]
                feat(t["w_out_2"][l], 0, 8, nq, xev, hin=(MH, ML), hw=mt_)
                fence()

            ffn(t["w_ffn1_gu_2"][l], t["w_ffn1_down_2"][l], 512, 0)
            mixer()
            ffn(t["w_ffn2_gu_2"][l], t["w_ffn2_down_2"][l], 256 if last else 512, 6)
        OUT = at("OUT", 20 * K, [128, 8, 256])
        fence()
        a = norm_out(256, lambda k: vec("final_g", k), lambda k: OUT[:, k, :])
        dma(out.rearrange("(k p) n -> p k n", p=128), OUT[:, :, :], sems["out"], a)
        sp.do(None, (sems["out"], 16), inc=False)
        return pe, act, dve, pool, sp, (chunks, units, raws)

    plan = trace(None)[5]
    pe, act, dve, pool, sp, _ = trace(plan)
    with nc.Block() as block:
        @block.sync
        def _(e):
            sp.emit(e)

        @block.scalar
        def _(e):
            act.emit(e)

        @block.vector
        def _(e):
            dve.emit(e)

        @block.gpsimd
        def _(e):
            pool.emit(e)

        @block.tensor
        def _(e):
            pe.emit(e)


_WEIGHTS = ["w_in", "w_out", "w_ada_2", "w_ffn1_gu_2", "w_ffn1_down_2", "w_ffn2_gu_2", "w_ffn2_down_2", "w_in_2",
            "w_out_a_2", "w_out_b_2", "w_out_c_2", "w_out_2"]


def constants():
    import numpy as np
    f = np.float32
    i = np.arange(128)
    ident = np.eye(128, dtype=f)
    tri = (i[:, None] <= i[None, :]).astype(f)
    rot = np.zeros((128, 128), f)
    for h in (0, 64):
        for d in range(32):
            rot[h + 32 + d, h + d] = -1.0
            rot[h + d, h + 32 + d] = 1.0
    cau = np.where(i[None, :] <= i[:, None], 0.0, -1e30).astype(f)
    qc = i % 64
    w0 = np.clip(qc - 8, 0, 48)[:, None]
    x = np.arange(64)[None, :]
    inw = (x >= w0) & (x < w0 + 16)
    cst = np.concatenate([ident, tri, rot, cau, inw.astype(f), np.where(inw, 0.0, -1e30).astype(f)], axis=1)
    q = (np.arange(2)[None, :, None] * 128 + i[:, None, None])
    k = np.arange(256)[None, None, :]
    alibi = np.where(k <= q, -(q - k).astype(f), f(-1e32)).astype(f)
    wm = np.where(np.abs(q - k) <= 128, 0.0, -1e30).astype(f)
    lg = np.log(f(1.0) - np.exp2(f(-5.0) - np.arange(4, dtype=f))).astype(f)
    dec = np.zeros((128, 4, 384), f)
    for h in range(4):
        d = (np.arange(256)[None, :] - i[:, None]).astype(f)
        full = np.where(d >= 0, np.exp((lg[h] * np.maximum(d, f(0.0))).astype(f)), f(0.0)).astype(f) * f(0.125)
        dec[:, h, 0:256] = full
        dec[:, h, 256:384] = full[:, 0:128]
    pos = np.arange(256, dtype=f)
    th = (f(1.0) / (f(10000.0) ** np.linspace(0.0, 1.0, 32, dtype=f))).astype(f)
    ang = (pos[:, None] * th[None, :]).astype(f).T
    cs1 = np.stack([np.tile(np.cos(ang), (4, 1)), np.tile(np.sin(ang), (4, 1))], axis=1).astype(f)
    inv = (f(10000.0) ** (-np.arange(16, dtype=f) / f(16))).astype(f)
    tk = np.arange(256)
    a2 = np.concatenate([(tk // 64).astype(f)[:, None] * inv, (tk % 64).astype(f)[:, None] * inv], axis=1).astype(f).T
    cs2 = np.stack([np.tile(np.cos(a2), (4, 1)), np.tile(np.sin(a2), (4, 1))], axis=1).astype(f)
    return {"cst": cst, "wm": wm, "alibi": alibi, "decay": dec, "cs1": cs1, "cs2": cs2}


def kernel(**inputs):
    import numpy as _np
    import concourse.bacc as _bacc
    from concourse import mybir as _mybir
    from concourse.bass_utils import run_bass_kernel_spmd as _run

    nc = _bacc.Bacc("TRN2", target_bir_lowering=False, num_devices=1)
    a = {n: _np.asarray(v) for n, v in inputs.items()}

    def col(v):
        v = v.reshape(-1, v.shape[-1] // 128, 128)
        return v.transpose(2, 0, 1).reshape(128, -1)

    def row(v):
        return _np.broadcast_to(v.reshape(1, -1), (128, v.size))
    parts = [("norm_w", col(a["norm_w"])), ("conv_w", col(a["conv_w"].reshape(8, 512))), ("conv_b", col(a["conv_b"])),
             ("ret_norm_w", col(a["ret_norm_w"])), ("mlstm_norm_w", col(a["mlstm_norm_w"])),
             ("final_norm_w", col(a["final_norm_w"][None])), ("gate_bias", row(a["gate_bias"])),
             ("cc", col(_np.stack([a["c_2"][0], a["c_ctx_2"]])).reshape(128, 2, 8).transpose(0, 2, 1).reshape(128, 16)),
             ("b_ada", col(a["b_ada_2"])), ("norm_g", col(a["norm_g_2"].reshape(6, 1024))),
             ("b_gate", col(a["b_gate_2"])), ("sink", row(a["sw_sink_2"])),
             ("dw_w", col(a["conv_dw_w_2"].reshape(62, 256))), ("dw_b", col(a["conv_dw_b_2"])),
             ("ln_g", col(a["conv_ln_g_2"])), ("ln_b", col(a["conv_ln_b_2"])), ("final_g", col(a["final_g_2"][None]))]
    arrays = {"vec": _np.ascontiguousarray(_np.concatenate([p for _, p in parts], axis=1)),
              "xT": _np.ascontiguousarray(a["x"][0].T), "ctxT": _np.ascontiguousarray(a["ctx_2"][0].T),
              "rpb": _np.ascontiguousarray(a["na_rpb_2"].reshape(2, 2790))}
    for n in _WEIGHTS:
        arrays[n] = _np.ascontiguousarray(a[n])
    arrays.update(constants())
    t = {n: nc.dram_tensor(f"in_{n}", v.shape, _mybir.dt.from_np(v.dtype), kind="ExternalInput").ap()
         for n, v in arrays.items()}
    t["_vec"] = [(n, p.shape[1]) for n, p in parts]
    out = nc.dram_tensor("out_0_dram", (1024, 256), _mybir.dt.from_np(_np.dtype("float32")), kind="ExternalOutput").ap()
    program(nc, t, out)
    r = _run(nc, [{f"in_{n}": v for n, v in arrays.items()}], core_ids=[0])
    return _np.ascontiguousarray(r.results[0]["out_0_dram"].T)[None]
```

```python
import concourse.bass as bass
from concourse import mybir

DEPTH = 2
D = 1024
NF = 22
STOP = None


def program(nc, t, out):
    f32 = mybir.dt.float32
    f32r = mybir.dt.float32r
    ALU = mybir.AluOpType
    ACT = mybir.ActivationFunctionType
    AX = mybir.AxisListType

    sb = lambda n, s, d=f32: nc.alloc_sbuf_tensor(n, s, d)
    X = sb("X", [128, 8, 512])
    NR = 3
    RAW = sb("RAW", [128, NR, 2048])
    NS = 3
    WH = sb("WH", [128, NS, 1024], f32r)
    WL = sb("WL", [128, NS, 1024], f32r)
    CST = sb("CST", [128, 5 * 128 + 64 + 2])
    IDN, TRI, ROT, CAU, CAT = (CST[:, 128 * i:128 * i + 128] for i in range(5))
    WIN = CST[:, 640:704]
    SEL = CST[:, 704:706]
    ONE = sb("ONE", [128, 128])
    CS2 = sb("CS2", [128, 2, 256])
    VEC = sb("VEC", [128, t["vec"].shape[1]])
    SM = sb("SM", [128, 112])
    MOD = sb("MOD", [128, DEPTH, 9, 8, 2])
    R0 = (nc.sbuf_base + 63) // 64 * 64
    K = 1024

    def at(name, off, shape, d=f32):
        return nc.alloc_sbuf_tensor_at(name, shape, d, offset=R0 + int(off * K))

    HH = at("HH", 0, [128, 8, 512], f32r)
    HL = at("HL", 16, [128, 8, 512], f32r)
    H1H = at("H1H", 0, [128, 8, 256], f32r)
    H1L = at("H1L", 8, [128, 8, 256], f32r)
    NA = 3
    AR = at("AR", 16, [128, NA, 2, 512])
    AS = at("AS", 28, [128, 512])
    AC = at("AC", 30, [128, 8, 32])
    B0 = 32
    GH = at("GH", B0, [128, NF, 512], f32r)
    GL = at("GL", B0 + 44, [128, NF, 512], f32r)
    FT = at("FT", B0 + 88, [128, 2, 512])
    SS = at("SS", B0 + 92, [128, 512])
    SQ = at("SQ", B0 + 94, [128, 2, 512])
    DG = at("DG", B0 + 98, [128, 4, 128])
    NT = at("NT", B0 + 88, [128, 2, 512])
    PJ = at("PJ", B0, [128, 24, 256])
    SS1 = at("SS1", B0, [128, 256])
    SQ1 = at("SQ1", B0 + 1, [128, 2, 256])
    DG1 = at("DG1", B0 + 3, [128, 2, 128])
    NT1 = at("NT1", B0 + 4, [128, 4, 256])
    VA = at("VA", B0 + 24, [128, 2, 512])
    VB = at("VB", B0 + 28, [128, 2, 256])
    VC = at("VC", B0 + 30, [128, 2, 4, 66])
    CO = at("CO", B0 + 33, [128, 2, 256])
    YH1 = at("YH1", B0 + 35, [128, 8, 256], f32r)
    YL1 = at("YL1", B0 + 43, [128, 8, 256], f32r)
    DT = at("DT", B0 + 51, [128, 4, 384])
    ALI = at("ALI", B0 + 57, [128, 2, 256])
    CS1 = at("CS1", B0 + 59, [128, 2, 256])
    CP = at("CP", B0 + 61, [128, 4, 260])
    W8 = at("W8", B0 + 65.25, [128, 8, 8])
    ST1 = at("ST1", B0 + 66, [128, 256])
    P1 = at("P1", B0 + 67, [128, 3, 256])
    PT1 = at("PT1", B0 + 70, [128, 3, 256])
    O1 = at("O1", B0 + 73, [128, 2, 2, 128])
    TM1 = at("TM1", B0 + 75, [128, 2, 512])
    RT = at("RT", B0 + 79, [128, 256])
    PR = at("PR", B0 + 80, [128, 2, 384])
    YT = at("YT", B0 + 83, [128, 512])
    HC = at("HC", B0 + 85, [128, 512])
    MA = at("MA", B0 + 87, [128, 192])
    NU1 = at("NU1", B0 + 87.75, [128, 264])
    MI = at("MI", B0 + 89, [128, 4, 512])
    HN = at("HN", B0 + 99, [128, 2, 80])
    QA = at("QA", B0, [128, 6, 512])
    BM = at("BM", B0 + 12, [128, 2, 6, 256])
    QB = at("QB", B0 + 24, [128, 4, 512])
    V2 = at("V2", B0 + 32, [128, 4, 512])
    YH2 = at("YH2", B0 + 40, [128, 8, 512], f32r)
    YL2 = at("YL2", B0 + 56, [128, 8, 512], f32r)
    HP = at("HP", B0 + 72, [128, 2, 2, 288])
    CV = at("CV", B0 + 76.5, [128, 2, 512])
    P2 = at("P2", B0 + 80.5, [128, 3, 512])
    PT2 = at("PT2", B0 + 86.5, [128, 3, 512])
    O2 = at("O2", B0 + 92.5, [128, 2, 384])
    ST2 = at("ST2", B0 + 95.5, [128, 256])
    TM2 = at("TM2", B0 + 96.5, [128, 3, 512])
    ACC = at("ACC", B0, [128, 8, 512])
    MT = at("MT", B0 + 16, [128, 4, 512])
    MH = at("MH", B0 + 24, [128, 8, 512], f32r)
    ML = at("ML", B0 + 72, [128, 8, 512], f32r)
    OUT = at("OUT", B0, [128, 8, 256])

    PS = [nc.alloc_psum_tensor(f"PS{i}", [128, 512], f32) for i in range(8)]
    sems = {n: nc.alloc_semaphore("s_" + n) for n in ("pe", "act", "dve", "pool", "c0", "out", "bm0", "bm1")}
    rsem = [nc.alloc_semaphore(f"s_raw{i}") for i in range(NR)]
    asem = [nc.alloc_semaphore(f"s_ada{i}") for i in range(NA)]
    c1 = nc.alloc_semaphore("s_c1")
    scr = nc.dram_tensor("rpb_rows", (DEPTH, 64, 2790), f32, kind="Internal").ap()

    def layout():
        o, v = {}, 0
        for n, w in t["_vec"]:
            o[n] = v
            v += w
        return o
    VO = layout()

    def vec(n, i, w=1):
        return VEC[:, VO[n] + i:VO[n] + i + w]

    class Engine:

        def __init__(self, sem):
            self.sem, self.n, self.q = sem, 0, []

        def do(self, fn, *waits, inc=True):
            self.q.append((waits, fn, inc))
            self.n += inc
            return (self.sem, self.n)

        def now(self):
            return (self.sem, self.n)

        def emit(self, e):
            seen = {}

            def wait(w):
                if w is None:
                    return
                if isinstance(w, list):
                    for x in w:
                        wait(x)
                    return
                s, v = w
                if v > seen.get(id(s), 0):
                    e.wait_ge(s, v)
                    seen[id(s)] = v
            for waits, fn, inc in self.q:
                for w in waits:
                    wait(w)
                if fn is not None:
                    i = fn(e)
                    if inc:
                        i.then_inc(self.sem, 1)

    def trace(plan):
        pe, act, dve, pool = (Engine(sems[n]) for n in ("pe", "act", "dve", "pool"))
        sp = Engine(None)
        engines = (pe, act, dve, pool)

        def dma(dst, src, sem, *waits):
            sp.do(lambda e: e.dma_start(dst, src).then_inc(sem, 16), *waits, inc=False)

        def fence():
            now = [e.now() for e in engines]
            for e in engines:
                e.do(None, now, inc=False)
            return now

        def mm(o, l, r, start, stop, *w, inc=False):
            return pe.do(lambda e: e.matmul(o, l, r, start=start, stop=stop), *w, inc=inc)

        def tp(o, i, *w, inc=False):
            return pe.do(lambda e: e.transpose(o, i, IDN), *w, inc=inc)

        def af(o, i, f, *w, scale=1.0, bias=0.0, acc=None):
            if acc is None:
                return act.do(lambda e: e.activation(o, i, f, bias=bias, scale=scale), *w)
            return act.do(lambda e: e.activation(o, i, f, bias=bias, scale=scale, accum_out=acc), *w)

        def cp(o, i, *w):
            return act.do(lambda e: e.activation(o, i, ACT.Copy), *w)

        def vcp(o, i, *w):
            return dve.do(lambda e: e.tensor_copy(o, i), *w)

        def tt(o, a, b, op, *w, on=None):
            return (on or dve).do(lambda e: e.tensor_tensor(out=o, in0=a, in1=b, op=op), *w)

        def ts(o, a, s1, s2, op0, op1, *w):
            if op1 is None:
                return dve.do(lambda e: e.tensor_scalar(o, a, s1, None, op0), *w)
            return dve.do(lambda e: e.tensor_scalar(o, a, s1, s2, op0, op1), *w)

        def stt(o, a, s, b, op0, op1, *w):
            return dve.do(lambda e: e.scalar_tensor_tensor(out=o, in0=a, scalar=s, in1=b, op0=op0, op1=op1), *w)

        def rmax(o, i, neg, *w):
            return dve.do(lambda e: e.tensor_reduce(o, i, AX.X, ALU.max, negate=neg), *w)

        def recip(o, i, *w):
            return dve.do(lambda e: e.reciprocal(o, i), *w)

        def rpow(o, i, *w):
            return pool.do(lambda e: e.tensor_tensor(out=o, in0=i, in1=MHALF[:, 0:i.shape[-1]], op=ALU.pow), *w)

        MHALF = SM[:, 96:112]

        free, held = [None] * 7, [False] * 7
        turn = [0]

        def bank():
            while held[turn[0] % 7]:
                turn[0] += 1
                assert not all(held)
            i = turn[0] % 7
            turn[0] += 1
            held[i] = True
            return i, PS[i], free[i]

        def done(i, *tok):
            free[i], held[i] = list(tok), False

        def run(*gens):
            for g in gens:
                for _ in g:
                    pass

        class Part:

            def __init__(self, gen, cost):
                self.gen, self.cost, self.spent, self.over = gen, cost, 0.0, False

            def step(self):
                self.spent += self.cost
                try:
                    next(self.gen)
                except StopIteration:
                    self.over = True

        def weave(*parts, until=None):
            low = min(p.spent for p in parts)
            for p in parts:
                p.spent -= low
            while True:
                live = [p for p in parts if not p.over]
                if not live or (until is not None and until.over):
                    return
                min(live, key=lambda p: p.spent).step()

        ck = dict(load=0, chunk=0, unit=0, split=0, cur=0)
        rel, ended, ready, arrived, count = {}, {}, {}, {}, [0] * NR
        chunks, units = [], []

        def load(c):
            while ck["load"] <= c:
                i = ck["load"]
                kt, cols, srcs = plan[0][i]
                view = RAW[:, i % NR, 0:kt * cols].rearrange("p (k c) -> p k c", c=cols)
                for c0, c1_, src in srcs:
                    dma(view[:, :, c0:c1_], src, rsem[i % NR], rel.get(i - NR))
                count[i % NR] += 16 * len(srcs)
                arrived[i] = (rsem[i % NR], count[i % NR])
                ck["load"] += 1

        def uview(R, u, kt, w):
            return R[:, u % NS, 0:kt * w].rearrange("p (k c) -> p k c", c=w)

        def split(upto):
            while ck["split"] <= min(upto, len(plan[1]) - 1):
                u = ck["split"]
                c, a, b, last = plan[1][u]
                load(c)
                kt, cols, _ = plan[0][c]
                raw = RAW[:, c % NR, 0:kt * cols].rearrange("p (k c) -> p k c", c=cols)[:, :, a:b]
                h, l = uview(WH, u, kt, b - a), uview(WL, u, kt, b - a)
                was = ended.get(u - NS)
                x = cp(h, raw, arrived[c], was)
                y = tt(l, raw, h.bitcast(f32), ALU.subtract, x, was, arrived[c])
                ready[u] = [x, y]
                if last:
                    rel[c] = [x, y]
                    for n in range(c + 1, min(c + NR, len(plan[0]) - 1) + 1):
                        if n < NR or n - NR in rel:
                            load(n)
                ck["split"] += 1

        def chunk(kt, cols, srcs, us):
            if not plan:
                c = len(chunks)
                chunks.append((kt, cols, srcs))
                units.extend((c, a, b, j == len(us) - 1) for j, (a, b) in enumerate(us))

        def unit(n=1):
            r = []
            for _ in range(n):
                u = ck["unit"]
                ck["unit"] += 1
                if plan:
                    split(u + NS - n)
                c, a, b, _ = (plan[1] if plan else units)[u]
                kt = (plan[0] if plan else chunks)[c][0]
                r.append((uview(WH, u, kt, b - a), uview(WL, u, kt, b - a), ready.get(u), u))
            return r

        def w3(o, w, h, first, last, *waits, flip=False, inc=False):
            (wh, wl), (hh, hl) = w, h
            pairs = [(wh, hh), (wh, hl), (wl, hh)] if not flip else [(hh, wh), (hh, wl), (hl, wh)]
            for j, (l, r) in enumerate(pairs):
                tok = mm(o, l, r, first and j == 0, last and j == 2, *(waits if j == 0 else ()), inc=inc and j == 2)
            return tok

        def wsrc(w, k0, kt, c0, c1_):
            return w[128 * k0:128 * (k0 + kt), c0:c1_].rearrange("(k p) c -> p k c", p=128)

        def columns(w, c0, m, kt, n, hin, k0, ev, i, hw):
            chunk(kt, 128 * m, [(0, 128 * m, wsrc(w, 0, kt, c0, c0 + 128 * m))],
                  [(128 * j, 128 * j + 128) for j in range(m)])
            if hw is not None:
                us = unit(m)
                bk = [bank() for _ in us]
                for k in range(kt):
                    for (wh, wl, w_, _), (b, P, fr) in zip(us, bk):
                        tok = w3(P[:, 0:n], (wh[:, k, :], wl[:, k, :]),
                                 (hin[0][:, k0 + k, 0:n], hin[1][:, k0 + k, 0:n]), k == 0, k == kt - 1,
                                 w_, fr, hw[k], inc=k == kt - 1)
                for j, ((_, _, _, u), (b, P, fr)) in enumerate(zip(us, bk)):
                    ended[u] = tok
                    done(b, *ev(i + j, P, tok))
                yield
                return
            for j in range(m):
                (wh, wl, w_, u), = unit()
                b, P, fr = bank()
                for k in range(kt):
                    if k == 4 and n == 512:
                        yield
                    tok = w3(P[:, 0:n], (wh[:, k, :], wl[:, k, :]),
                             (hin[0][:, k0 + k, 0:n], hin[1][:, k0 + k, 0:n]), k == 0, k == kt - 1,
                             w_, fr, inc=k == kt - 1)
                ended[u] = tok
                done(b, *ev(i + j, P, tok))
                yield

        def feat(w, c0, nt, n, ev, hin=None, hw=None):
            hin = hin or (HH, HL)
            for i in range(0, nt, 2):
                m = min(2, nt - i)
                yield from columns(w, c0 + 128 * i, m, 8, n, hin, 0, ev, i, hw if i == 0 else None)

        def tokm(w, c0, nu, ntok, ev, hin, VT, was):
            n = 128 * ntok
            pend = []

            def flip(i, c):
                b, P, fr = bank()
                for q in range(ntok):
                    tok = tp(P[:, 128 * q:128 * q + 128], VT[:, i % 2, 128 * q:128 * q + 128], fr, c, inc=q == ntok - 1)
                was[i % 2] = tok
                done(b, *ev(i, P, tok))

            def fev(i, P, tok):
                c = cp(VT[:, i % 2, 0:n], P[:, 0:n], tok, was[i % 2])
                pend.append((i, c))
                return [c]
            for _ in feat(w, c0, nu, n, fev, hin):
                yield
                if len(pend) > 1:
                    flip(*pend.pop(0))
            yield
            for p in pend:
                flip(*p)

        class Norm:

            def __init__(self, n, S, Q, G):
                self.n, self.S, self.Q, self.G, self.was, self.tok = n, S, Q, G, [None, None], None

            def add(self, i, tok):
                n = self.n
                if i == 0:
                    self.tok = af(self.S[:, 0:n], X[:, 0, 0:n], ACT.Square, tok)
                    return
                a = af(self.Q[:, i % 2, 0:n], X[:, i, 0:n], ACT.Square, tok, self.was[i % 2])
                self.tok = tt(self.S[:, 0:n], self.S[:, 0:n], self.Q[:, i % 2, 0:n], ALU.add, a, self.tok, on=pool)
                self.was[i % 2] = self.tok

            def rstd(self):
                q = self.n // 128
                b, P, fr = bank()
                for i in range(q):
                    tok = mm(P[:, i:i + 1], self.S[:, 128 * i:128 * i + 128], ONE[:, 0:1], True, True, fr, self.tok,
                             inc=i == q - 1)
                v = ts(SM[:, 0:q], P[:, 0:q], 1.0 / D, 1e-6, ALU.mult, ALU.add, tok)
                done(b, v)
                r = rpow(SM[:, 8:8 + q], SM[:, 0:q], v)
                for i in range(q):
                    d = ts(self.G[:, i, :], IDN, SM[:, 8 + i:9 + i], None, ALU.mult, None, r)
                b, P, fr = bank()
                tok = mm(P[:, 0:self.n], ONE[:, :], self.G[:, 0:q, :], True, True, fr, d, inc=True)
                return b, P, tok

        def norm_in(nm, gs, sh, hin, T_, fill=lambda: None):
            n = nm.n
            fill()
            b, P, tok = nm.rstd()
            fill()
            r = []
            nb = T_.shape[1]
            was = [None] * nb
            for k in range(8):
                T = T_[:, k % nb, :]
                r.append([])
                for s in range(n // 256):
                    c = slice(256 * s, 256 * s + 256)
                    H, L = hin[0][:, k, c], hin[1][:, k, c]
                    a = stt(T[:, c], X[:, k, c], gs(k, s), P[:, c], ALU.mult, ALU.mult, tok, was[k % nb])
                    if sh is None:
                        h = cp(H, T[:, c], a)
                        l = tt(L, T[:, c], H.bitcast(f32), ALU.subtract, h)
                    else:
                        h = af(H, T[:, c], ACT.Identity, a, bias=sh(k, s))
                        l = stt(L, T[:, c], sh(k, s), H.bitcast(f32), ALU.add, ALU.subtract, h)
                    r[k] += [h, l]
                was[k % nb] = r[k]
            done(b, a)
            return r

        def norm_out(nm, g, wr, after=None):
            b, P, tok = nm.rstd()
            for k in range(8):
                a = stt(wr(k), X[:, k, 0:nm.n], g(k), P[:, 0:nm.n], ALU.mult, ALU.mult, tok)
                if after:
                    after(k, a)
            done(b, a)
            return a

        LAG, NB = 2, 3

        def attend(jobs, PB, PTB, ST):
            n = len(jobs)
            st = {}
            for i in range(n + 2 * LAG):
                if i < n:
                    j = jobs[i]
                    nk = j["nk"]
                    b, P, fr = bank()
                    tok = mm(P[:, 0:nk], j["q"], j["k"], True, True, fr, j.get("w"), inc=True)
                    if "bias" in j:
                        tok = j["bias"](P, tok)
                    nm, sm, rs = ST[:, i:i + 1], ST[:, 64 + i:65 + i], ST[:, 128 + i:129 + i]
                    m = rmax(nm, P[:, 0:nk], True, tok)
                    if j.get("sink") is not None:
                        sk, nsk = j["sink"]
                        m = ts(nm, nm, nsk, None, ALU.min, None, m)
                    e = af(PB[:, i % NB, 0:nk], P[:, 0:nk], ACT.Exp, m, st.get(("t", i - NB)), bias=nm, acc=sm)
                    done(b, e)
                    e2 = None
                    if j.get("sink") is not None:
                        e2 = af(ST[:, 192 + i:193 + i], sk, ACT.Exp, m, bias=nm)
                    st["e", i] = [e, e2]
                i1 = i - LAG
                if 0 <= i1 < n:
                    j = jobs[i1]
                    kt = j["nk"] // 128
                    sm, rs = ST[:, 64 + i1:65 + i1], ST[:, 128 + i1:129 + i1]
                    b, P, fr = bank()
                    for x in range(kt):
                        tok = tp(P[:, 128 * x:128 * x + 128], PB[:, i1 % NB, 128 * x:128 * x + 128], fr, st["e", i1],
                                 inc=x == kt - 1)
                    st["t", i1] = tok
                    c = cp(PTB[:, i1 % NB, 0:128 * kt], P[:, 0:128 * kt], tok, st.get(("pv", i1 - NB)))
                    done(b, c)
                    st["c", i1] = c
                    e3 = st["e", i1]
                    if j.get("sink") is not None:
                        e3 = tt(sm, sm, ST[:, 192 + i1:193 + i1], ALU.add, e3)
                    st["r", i1] = recip(rs, sm, e3)
                i2 = i - 2 * LAG
                if 0 <= i2 < n:
                    j = jobs[i2]
                    kt = j["nk"] // 128
                    b, P, fr = bank()
                    for x in range(kt):
                        tok = mm(P[:, 0:64], PTB[:, i2 % NB, 128 * x:128 * x + 128], j["v"](x), x == 0, x == kt - 1,
                                 fr, st["c", i2], inc=x == kt - 1)
                    st["pv", i2] = tok
                    o = ts(j["o"], P[:, 0:64], ST[:, 128 + i2:129 + i2], None, ALU.mult, None, tok, st["r", i2],
                           j["ow"]() if "ow" in j else None)
                    done(b, o)
                    if "end" in j:
                        j["end"](o)
                yield

        def ysplit(yh, yl, src, tok, scale=None):
            if scale is None:
                a = cp(yh, src, tok)
                return [a, tt(yl, src, yh.bitcast(f32), ALU.subtract, a, tok)]
            a = af(yh, src, ACT.Copy, tok, scale=scale)
            return [a, stt(yl, src, scale, yh.bitcast(f32), ALU.mult, ALU.subtract, a, tok)]

        def head_norm(x, src, tok, dst, res):
            S, A, V, R = HN[:, x, 0:48], HN[:, x, 48:64], HN[:, x, 64:72], HN[:, x, 72:80]
            for g in range(8):
                a = dve.do(lambda e, g=g, i=src(g): e.bn_stats(S[:, 6 * g:6 * g + 6], i), tok)
                last = dve.do(lambda e, g=g: e.bn_aggr(A[:, 2 * g:2 * g + 2], S[:, 6 * g:6 * g + 6]), a)
                if g % 2:
                    yield
            v = ts(V, HN[:, x, 49:64:2], 1e-5, None, ALU.add, None, last)
            r = rpow(R, V, v)
            yield
            for g in range(8):
                a = ts(dst(g), src(g), A[:, 2 * g:2 * g + 1], R[:, g:g + 1], ALU.subtract, ALU.mult, r, last)
            res.append(a)
            yield

        cload = [(X[:, :, 0:256], t["xT"].rearrange("(k p) n -> p k n", p=128)), (CST[:, :], t["cst"]),
                 (VEC[:, :], t["vec"]), (CS2[:, :, :], t["cs2"]),
                 (X[:, :, 256:512], t["ctxT"].rearrange("(k p) n -> p k n", p=128))]
        for o, i in cload:
            act.do(lambda e, o=o, i=i: e.dma_start(o, i).then_inc(sems["c0"], 16), inc=False)
        c0 = (sems["c0"], 16 * len(cload))
        for l in range(DEPTH):
            act.do(lambda e, l=l: e.dma_start(scr[l, :, :], bass.AP(tensor=t["rpb"].tensor, offset=2790 * l,
                   ap=[[0, 64], [1, 2790]])).then_inc(sems["bm0"], 16), inc=False)
        c1n = 64
        for o, i in ((DT[:, :, :], t["decay"]), (ALI[:, :, :], t["alibi"]), (CS1[:, :, :], t["cs1"]),
                     (W8[:, :, :], t["w_in"][0][:, 4352:4360].rearrange("(k p) c -> p k c", p=128))):
            act.do(lambda e, o=o, i=i: e.dma_start(o, i).then_inc(c1, 16), inc=False)
        m1 = dve.do(lambda e: e.memset(ONE[:, :], 1.0))
        m2 = dve.do(lambda e: e.memset(MHALF, -0.5))
        m3 = dve.do(lambda e: e.memset(AC[:, :, :], 0.0))
        for e in engines:
            e.do(None, c0, m2, inc=False)
        z1 = dve.do(lambda e: e.memset(CP[:, :, 0:3], 0.0))
        z2 = dve.do(lambda e: e.memset(VC[:, :, :, 64:65], 1.0))

        a = af(SM[:, 80:96], vec("cc", 0, 16), ACT.Tanh, scale=0.5)
        cc = stt(AC[:, :, 0:2], SM[:, 80:96].rearrange("p (k s) -> p k s", s=2), 1.0,
                 vec("cc", 0, 16).rearrange("p (k s) -> p k s", s=2), ALU.add, ALU.mult, a, m3)
        acnt = [0] * NA

        def aload(n, tok):
            if n >= 72 * DEPTH:
                return
            l, j, q = n // 72, n // 4 % 18, n % 4
            src = t["w_ada_2"][l][256 * q:256 * q + 256, 512 * j:512 * j + 512].rearrange("(k p) c -> p k c", p=128)
            dma(AR[:, n % NA, :, :], src, asem[n % NA], tok)

        def ada():
            for n in range(NA):
                aload(n, None)
            fr = was = None
            P = PS[7]
            for l in range(DEPTH):
                for j in range(18):
                    for q in range(4):
                        n = 72 * l + 4 * j + q
                        for x in range(2):
                            g = 2 * (q % 2) + x
                            tok = mm(P[32 * g:32 * g + 32, :], AC[:, 2 * q + x, :], AR[:, n % NA, x, :], q < 2, q > 1,
                                     (asem[n % NA], 16 * (n // NA + 1)), cc, fr, inc=x == 1)
                        aload(n + NA, tok)
                        yield
                    a = cp(AS[:, :], P[:, :], tok, was)
                    fr = a
                    yield
                    b, P2_, f2 = bank()
                    for x in range(4):
                        was = mm(P2_[:, 2 * x:2 * x + 2], AS[:, 128 * x:128 * x + 128], SEL, True, True, a, f2, inc=x == 3)
                    i0, k0 = (4 * j) // 8, (4 * j) % 8
                    for s in range(2):
                        a = stt(MOD[:, l, i0, k0:k0 + 4, s], P2_[:, s:8:2], 0.5, vec("b_ada", 72 * l + 4 * j, 4),
                                ALU.mult, ALU.add, was)
                    done(b, a)
                    yield
                for i in (2, 8):
                    ts(MOD[:, l, i, :, :], MOD[:, l, i, :, :], 0.5, None, ALU.mult, None, a)
                for i, n in ((1, 0), (4, 1), (7, 2)):
                    for s in range(2):
                        stt(MOD[:, l, i, :, s], MOD[:, l, i, :, s], 1.0, vec("norm_g", 24 * l + 8 * n, 8), ALU.add,
                            ALU.mult, a)
        adag = ada()
        adap = Part(adag, 0.5)

        def afill(n):
            for _ in range(n):
                next(adag, None)

        N = 256
        H1 = (H1H, H1L)
        nm = Norm(N, SS1, SQ1, DG1)
        for k in range(8):
            nm.add(k, None)
        for l in range(DEPTH):
            w_in, w_out = t["w_in"][l], t["w_out"][l]
            if l:
                c1n += 16
                act.do(lambda e, i=w_in[:, 4352:4360].rearrange("(k p) c -> p k c", p=128):
                       e.dma_start(W8[:, :, :], i).then_inc(c1, 16), pe.now(), inc=False)
            c1t = (c1, c1n)
            hw = norm_in(nm, lambda k, s: vec("norm_w", 8 * l + k), None, H1, NT1, lambda: afill(4))

            def to(slot, scale=None):
                def ev(i, P, tok):
                    return [cp(PJ[:, slot + i, :], P[:, 0:N], tok) if scale is None else
                            af(PJ[:, slot + i, :], P[:, 0:N], ACT.Copy, tok, scale=scale)]
                return ev
            silu_w = [None, None]

            def to_silu2(slot):
                def ev(i, P, tok):
                    T = TM1[:, i % 2, 0:N]
                    a = af(T, P[:, 0:N], ACT.Tanh, tok, silu_w[i % 2], scale=0.5)
                    c = stt(PJ[:, slot + i, :], T, 1.0, P[:, 0:N], ALU.add, ALU.mult, a)
                    silu_w[i % 2] = c
                    return [c]
                return ev

            def to_tok(dst):
                def ev(i, P, tok):
                    return [cp(dst(i), P[:, 0:256].rearrange("p (q c) -> p q c", c=128), tok)]
                return ev

            def vc_ev(i, P, tok):
                for q in range(2):
                    r = cp(VC[:, q, 2 * i:2 * i + 2, 0:64], P[:, 128 * q:128 * q + 128].rearrange("p (h d) -> p h d", d=64),
                           tok)
                return [r]
            cot = []

            def co_ev(i, P, tok):
                v = CO[:, :, 128 * i:128 * i + 128]
                a = af(v, P[:, 0:256].rearrange("p (q c) -> p q c", c=128), ACT.Tanh, tok, scale=0.5)
                cot.append(ts(v, v, 0.5, 0.5, ALU.mult, ALU.add, a))
                return [a]

            def half(t_, h):
                return t_[64 * (h % 2):64 * (h % 2) + 64]

            hv1 = ts(SM[:, 32:34], vec("ret_norm_w", 2 * l, 2), 0.5, None, ALU.mult, None)
            hv2 = ts(SM[:, 34:36], vec("mlstm_norm_w", 2 * l, 2), 0.5, None, ALU.mult, None)
            yw = [None, None]
            yt2 = [None, None]
            YT2 = YT[:, :].rearrange("p (a n) -> p a n", n=256)

            def yout(src, tok, i, gslot, yslot, sc):
                b, P, fr = bank()
                for q in range(2):
                    tk = tp(P[:, 128 * q:128 * q + 128], src(q), tok, fr, inc=q == 1)
                T = TM1[:, yslot % 2, 256:512]
                a = stt(T, PJ[:, gslot + i, :], sc, P[:, 0:256], ALU.mult, ALU.mult, tk, yw[yslot % 2], hv1, hv2)
                done(b, a)
                yw[yslot % 2] = ysplit(YH1[:, yslot, :], YL1[:, yslot, :], T, a)
                return tk

            def gates(res):
                b, P, fr = bank()
                for q in range(2):
                    for k in range(8):
                        for j, hx in enumerate(H1):
                            tok = mm(P[:, 8 * q:8 * q + 8], hx[:, k, 128 * q:128 * q + 128].bitcast(f32), W8[:, k, :],
                                     k == 0 and j == 0, k == 7 and j == 1, fr, c1t, inc=q == 1 and k == 7 and j == 1)
                for q in range(2):
                    g = tt(IF[:, q, :], P[:, 8 * q:8 * q + 8], vec("gate_bias", 8 * l, 8), ALU.add, tok)
                done(b, g)
                yield
                a = stt(T1, F_, -1.0, F_, ALU.mult, ALU.max, g)
                a = af(T2, T1, ACT.Exp, a, scale=-1.0)
                yield
                a = af(T1, T2, ACT.Ln, a, bias=ONE[:, 0:1])
                a = stt(LS, F_, 0.0, T1, ALU.min, ALU.subtract, a)
                yield
                b, P, fr = bank()
                mm(P[:, 0:8], TRI, MA[:, 16:24], True, True, fr, a)
                tok = mm(P[:, 8:12], ONE[:, :], MA[:, 16:20], True, True, inc=True)
                b1 = vcp(BB, P[:, 0:8].rearrange("p (a b) -> p a b", b=4), tok)
                b2 = vcp(BL, P[:, 8:12], tok)
                done(b, b2)
                res.append([tt(RR, I_, BB, ALU.subtract, b1), b2])
                yield
            IF = MA[:, 0:16].rearrange("p (a b) -> p a b", b=8)
            F_, I_ = IF[:, :, 4:8], IF[:, :, 0:4]
            m8 = lambda i: MA[:, 16 + 8 * i:24 + 8 * i].rearrange("p (a b) -> p a b", b=4)
            LS, T1, T2, BB, RR, UU, NU, WI, EM, DN = (m8(i) for i in range(10))
            BL, MS, WS, MX, RHO = (m8(10 + i)[:, 0, :] for i in range(5))

            def attention():
                jobs = []
                ow = [None, None]
                for h in range(8):
                    for q in range(2):
                        nk = 128 * (q + 1)

                        def bias(P, tok, h=h, q=q, nk=nk):
                            return stt(P[:, 0:nk], ALI[:, q, 0:nk], 2.0 ** -(h + 1), P[:, 0:nk], ALU.mult, ALU.add, tok,
                                       c1t)
                        i, ob = h // 2, h // 2 % 2
                        job = dict(q=half(PJ, h)[:, i, 128 * q:128 * q + 128], k=half(PJ, h)[:, 4 + i, 0:nk],
                                   nk=nk, bias=bias, v=lambda x, h=h: VA[:, x, 64 * h:64 * h + 64],
                                   o=O1[:, ob, q, 64 * (h % 2):64 * (h % 2) + 64], ow=lambda ob=ob: ow[ob])
                        if h % 2 and q:
                            def end(o, i=i, ob=ob):
                                pend.append((i, ob, o))
                                assert len(pend) < 2
                            job["end"] = end
                        jobs.append(job)
                pend = []
                gen = attend(jobs, P1, PT1, ST1)
                for _ in gen:
                    yield
                    while pend and len(gated) > 0:
                        i, ob, o = pend.pop(0)
                        ow[ob] = yout(lambda q: O1[:, ob, q, :], o, i, 8, 0 + i, 0.5)
                for i, ob, o in pend:
                    ow[ob] = yout(lambda q: O1[:, ob, q, :], o, i, 8, 0 + i, 0.5)
                    yield
            gated = []

            def flag(lst):
                lst.append(1)
                return
                yield

            def retention():
                rt = []
                for i in range(4):
                    b, P, fr = bank()
                    tok = mm(P[:, 0:256], ROT, PJ[:, 12 + i, :], True, True, fr, inc=True)
                    a = tt(RT[:, :], P[:, 0:256], CS1[:, 1, :], ALU.mult, tok, c1t, rt)
                    done(b, a)
                    c = tt(PJ[:, 12 + i, :], PJ[:, 12 + i, :], CS1[:, 0, :], ALU.mult, tok, c1t)
                    rt = tt(PJ[:, 12 + i, :], PJ[:, 12 + i, :], RT[:, :], ALU.add, a, c)
                    yield
                bo, PO, fro = bank()
                pw = {}
                T = {}
                for h in range(5):
                    if h < 4:
                        b, P, fr = bank()
                        kk, qq = half(PJ, h)[:, 14 + h // 2, :], half(PJ, h)[:, 12 + h // 2, :]
                        mm(P[:, 0:256], kk[:, 0:128], qq[:, 0:256], True, True, fr, rt)
                        tok = mm(P[:, 256:384], kk[:, 128:256], qq[:, 128:256], True, True, inc=True)
                        T[h] = PR[:, h % 2, :]
                        a_ = tt(T[h], P[:, 0:384], DT[:, h, :], ALU.mult, tok, pw.get(h - 2), c1t)
                        done(b, a_)
                    if h > 0:
                        g = h - 1
                        vv = lambda x: VB[:, x, 64 * g:64 * g + 64]
                        mm(PO[:, 64 * g:64 * g + 64], T[g][:, 0:128], vv(0), True, True, a, fro)
                        mm(PO[:, 256 + 64 * g:320 + 64 * g], T[g][:, 128:256], vv(0), True, False)
                        pw[g] = mm(PO[:, 256 + 64 * g:320 + 64 * g], T[g][:, 256:384], vv(1), False, True, inc=True)
                    a = a_
                    yield
                res = []
                yield from head_norm(0, lambda g: PO[:, 64 * g:64 * g + 64], pw[3], lambda g: YT[:, 64 * g:64 * g + 64],
                                     res)
                done(bo, res[0])
                for i in range(2):
                    yout(lambda q: YT[:, 256 * q + 128 * i:256 * q + 128 * i + 128], res[0], i, 16, 4 + i,
                         SM[:, 32 + i:33 + i])
                    yield

            def mlstm(gr):
                hw_ = ts(SM[:, 36:52], vec("conv_w", 16 * l, 16), 0.5, None, ALU.mult, None)
                hb_ = ts(SM[:, 52:56], vec("conv_b", 4 * l, 4), 0.5, None, ALU.mult, None)
                cq = []
                for i in range(4):
                    A = PJ[:, 20 + i, :]
                    a = ts(A, CP[:, i, 0:256], SM[:, 36 + i:37 + i], SM[:, 52 + i:53 + i], ALU.mult, ALU.add, hw_, hb_,
                           cpt[i], z1)
                    for j in range(1, 4):
                        a = stt(A, CP[:, i, j:j + 256], SM[:, 36 + 4 * j + i:37 + 4 * j + i], A, ALU.mult, ALU.add, a)
                    T = CP[:, i, 3:259]
                    a = af(T, A, ACT.Tanh, a)
                    cq.append(stt(A, T, 1.0, A, ALU.add, ALU.mult, a))
                    yield
                NUM = NU1[:, 0:260].rearrange("p (h d) -> p h d", d=65)
                pv = w = tpt = hc = None
                for c in range(2):
                    b, P, fr = bank()
                    for h in range(4):
                        d = ts(MI[:, 0, 128 * h:128 * h + 128], IDN, RR[:, c, h:h + 1], None, ALU.mult, None, gr, pv)
                    tok = mm(P[:, :], ONE[:, :], MI[:, 0, :], True, True, fr, d, inc=True)
                    yield
                    M1 = MI[:, 1, :]
                    for h in range(4):
                        a = tt(M1[:, 128 * h:128 * h + 128], P[:, 128 * h:128 * h + 128], CAU, ALU.add, tok, w)
                    mx = rmax(MX, M1.rearrange("p (h s) -> p h s", s=128), False, a)
                    yield
                    if c == 0:
                        rho = rmax(RHO, P[:, :].rearrange("p (h s) -> p h s", s=128), False, tok)
                        done(b, rho)
                        rho = ts(RHO, RHO, 0.0, None, ALU.max, None, rho)
                        ms1 = tt(MS, BL, RHO, ALU.add, rho)
                        u = ts(UU[:, c, :], MX, 0.0, None, ALU.max, None, mx)
                    else:
                        done(b, a)
                        u = tt(UU[:, c, :], MX, MS, ALU.max, mx, ms1)
                    nu = ts(NU[:, c, :], UU[:, c, :], -1.0, None, ALU.mult, None, u)
                    yield
                    W = MI[:, 2, :]
                    for h in range(4):
                        w = af(W[:, 128 * h:128 * h + 128], M1[:, 128 * h:128 * h + 128], ACT.Exp, nu, tpt,
                               bias=NU[:, c, h:h + 1])
                    mt = tt(DN[:, c, :], BB[:, c, :], UU[:, c, :], ALU.add, u)
                    em = af(EM[:, c, :], DN[:, c, :], ACT.Exp, mt, scale=-1.0)
                    if c == 1:
                        wi = tt(WI[:, c, :], MS, UU[:, c, :], ALU.subtract, u)
                        wi = af(WI[:, c, :], WI[:, c, :], ACT.Exp, wi)
                    yield
                    pair = lambda v: v.rearrange("p (a b s) -> p a b s", b=2, s=128)
                    for o in range(2):
                        b, P, fr = bank()
                        for x in range(2):
                            tok = mm(P[:, 128 * x:128 * x + 128], half(PJ, o)[:, 20 + x, 128 * c:128 * c + 128],
                                     half(PJ, o)[:, 22 + x, 128 * c:128 * c + 128], True, True, fr, cq[3], inc=x == 1)
                        a = stt(pair(W)[:, :, o, :], P[:, 0:256].rearrange("p (a s) -> p a s", s=128), 0.125,
                                pair(W)[:, :, o, :], ALU.mult, ALU.mult, tok, w)
                        done(b, a)
                    yield
                    b, P, fr = bank()
                    for h in range(4):
                        tpt = tp(P[:, 128 * h:128 * h + 128], W[:, 128 * h:128 * h + 128], fr, a, inc=h == 3)
                    PT = MI[:, 0, :]
                    a = cp(PT, P[:, :], tpt)
                    done(b, a)
                    yield
                    b, P, fr = bank()
                    for h in range(4):
                        pv = mm(P[:, 65 * h:65 * h + 65], PT[:, 128 * h:128 * h + 128], VC[:, c, h, 0:65], True, True,
                                fr, a, z2, inc=h == 3)
                    a = vcp(NUM, P[:, 0:260].rearrange("p (h d) -> p h d", d=65), pv)
                    done(b, a)
                    yield
                    if c == 0:
                        ws = tt(WS, RR[:, 0, :], RHO, ALU.subtract, rho)
                        ws = af(WS, WS, ACT.Exp, ws)
                        b, P, fr = bank()
                        for i in range(2):
                            tok = tp(P[:, 128 * i:128 * i + 128], PJ[:, 22 + i, 0:128], fr, cq[3], inc=i == 1)
                        KT = MI[:, 3, 0:256]
                        for h in range(4):
                            kx = ts(KT[:, 64 * h:64 * h + 64], P[:, 64 * h:64 * h + 64], WS[:, h:h + 1], 0.125, ALU.mult,
                                    ALU.mult, tok, ws)
                        done(b, kx)
                        yield
                        b, P, fr = bank()
                        for h in range(4):
                            o = P[64 * (h % 2):64 * (h % 2) + 64, 65 * (h // 2):65 * (h // 2) + 65]
                            tok = mm(o, KT[:, 64 * h:64 * h + 64], VC[:, 0, h, 0:65], True, True, fr, kx, inc=h == 3)
                        state = vcp(MI[:, 3, 256:386], P[:, 0:130], tok)
                        done(b, state)
                        yield
                    else:
                        for o in range(2):
                            b, P, fr = bank()
                            for x in range(2):
                                tok = mm(P[:, 65 * x:65 * x + 65], half(PJ, o)[:, 20 + x, 128:256],
                                         half(MI, o)[:, 3, 256 + 65 * x:256 + 65 * x + 65], True, True,
                                         fr, state, inc=x == 1)
                            for x in range(2):
                                h = 2 * x + o
                                a = stt(NUM[:, h, :], P[:, 65 * x:65 * x + 65], WI[:, 1, h:h + 1], NUM[:, h, :],
                                        ALU.mult, ALU.add, tok, wi, a)
                            done(b, a)
                        yield
                    dn = stt(DN[:, c, :], NUM[:, :, 64], -1.0, NUM[:, :, 64], ALU.mult, ALU.max, a, em)
                    dn = tt(DN[:, c, :], DN[:, c, :], EM[:, c, :], ALU.max, dn)
                    dn = recip(DN[:, c, :], DN[:, c, :], dn)
                    for h in range(4):
                        hc = stt(HC[:, 256 * c + 64 * h:256 * c + 64 * h + 64], NUM[:, h, 0:64], DN[:, c, h:h + 1],
                                 CO[:, c, 64 * h:64 * h + 64], ALU.mult, ALU.mult, dn, cot)
                    yield
                res = []
                g_ = lambda g: HC[:, 64 * g:64 * g + 64]
                yield from head_norm(1, g_, hc, g_, res)
                for i in range(2):
                    yout(lambda q: HC[:, 256 * q + 128 * i:256 * q + 128 * i + 128], res[0], i, 18, 6 + i,
                         SM[:, 34 + i:35 + i])
                    yield

            def outp(part, hw, ev):
                for i in range(0, 8, 4):
                    chunk(4, 512, [(0, 512, wsrc(w_out, 4 * part, 4, 128 * i, 128 * i + 512))], [(0, 256), (256, 512)])
                    for j in range(2):
                        (wh, wl, w_, u), = unit()
                        for m in range(2):
                            b, P, fr = bank()
                            for k in range(4):
                                tok = w3(P[:, 0:N], (wh[:, k, 128 * m:128 * m + 128], wl[:, k, 128 * m:128 * m + 128]),
                                         (YH1[:, 4 * part + k, :], YL1[:, 4 * part + k, :]), k == 0, k == 3, w_, fr, hw,
                                         inc=k == 3)
                            x = i + 2 * j + m
                            a = tt(X[:, x, 0:N], P[:, 0:N], X[:, x, 0:N], ALU.add, tok)
                            done(b, a)
                            if ev:
                                ev(x, a)
                        ended[u] = tok
                        yield

            def chain(*gens):
                for g in gens:
                    yield from g
            cpt = {}

            def cp_ev(i, P, tok):
                cpt[i] = cp(CP[:, i, 3:259], P[:, 0:N], tok)
                return [cpt[i]]
            gr = []
            run(feat(w_in, 0, 4, N, to(0, 0.125), H1, hw), feat(w_in, 512, 4, N, to(4), H1),
                tokm(w_in, 1024, 4, 2, to_tok(lambda i: VA[:, :, 128 * i:128 * i + 128]), H1, YT2, yt2))
            att = Part(attention(), 1.0)
            cpr = Part(chain(feat(w_in, 1536, 4, N, to_silu2(8), H1), flag(gated), feat(w_in, 3072, 4, N, cp_ev, H1), gates(gr), tokm(w_in, 3584, 2, 2, vc_ev, H1, YT2, yt2),
                             tokm(w_in, 3840, 2, 2, co_ev, H1, YT2, yt2)), 1.2)
            weave(att, cpr, until=cpr)
            mls = Part(mlstm(gr[0]), 1.0)
            rest = Part(chain(feat(w_in, 2048, 4, N, to(12), H1),
                              tokm(w_in, 2560, 2, 2, to_tok(lambda i: VB[:, :, 128 * i:128 * i + 128]), H1, YT2, yt2),
                              feat(w_in, 2816, 2, N, to_silu2(16), H1), feat(w_in, 4096, 2, N, to_silu2(18), H1)), 1.4)
            weave(att, rest, mls, until=rest)
            weave(att, mls, adap, until=att)
            at_ = [act.now(), dve.now()]
            ret, op = Part(retention(), 1.0), Part(outp(0, at_, None), 4.0)
            weave(mls, ret, op, adap, until=mls)
            weave(ret, op, adap, until=ret)
            weave(op)
            ywt = [act.now(), dve.now()]
            nm = Norm(N, SS1, SQ1, DG1)
            run(outp(1, ywt, nm.add))
        if STOP == 1:
            a = norm_out(nm, lambda k: vec("final_norm_w", k), lambda k: PJ[:, 8 + k, :])
            dma(out.rearrange("(k p) n -> p k n", p=128), PJ[:, 8:16, :], sems["out"], a)
            sp.do(None, (sems["out"], 16), inc=False)
            return pe, act, dve, pool, sp, (chunks, units)
        nm1, nm = nm, Norm(512, SS, SQ, DG)
        norm_out(nm1, lambda k: vec("final_norm_w", k), lambda k: X[:, k, 0:256], nm.add)
        run(adag)

        def ffn(nm, l, gu, dn, n, i0, nxt):
            hw = norm_in(nm, lambda k, s: MOD[:, l, i0 + 1, k, s:s + 1], lambda k, s: MOD[:, l, i0, k, s:s + 1],
                         (HH, HL), NT)
            ft = [None, None]
            ab = {}

            def ev(i, P, tok):
                x, m = divmod(i, 2)
                if x == 0:
                    T = FT[:, m, 0:n]
                    a = af(T, P[:, 0:n], ACT.Tanh, tok, ft[m], scale=0.5)
                    ab[m] = stt(T, T, 1.0, P[:, 0:n], ALU.add, ALU.mult, a)
                    return [ab[m]]
                T = FT[:, m, 0:n]
                g = stt(T, T, 0.5, P[:, 0:n], ALU.mult, ALU.mult, ab[m], tok)
                ft[m] = ysplit(GH[:, 2 * j + m, 0:n], GL[:, 2 * j + m, 0:n], T, g)
                return [g]
            for j in range(11):
                for x in range(2):
                    run(columns(gu, 2816 * x + 256 * j, 2, 8, n, (HH, HL), 0, ev, 2 * x, hw if j == 0 and x == 0 else None))
            gt = [act.now(), dve.now()]
            for j in range(4):
                bk = [bank(), bank()]
                for k0, kt in ((0, 8), (8, 8), (16, 6)):
                    chunk(kt, 256, [(0, 256, wsrc(dn, k0, kt, 256 * j, 256 * j + 256))], [(0, 128), (128, 256)])
                    for m in range(2):
                        (wh, wl, w_, u), = unit()
                        b, P, fr = bk[m]
                        for k in range(kt):
                            kk = k0 + k
                            tok = w3(P[:, 0:n], (wh[:, k, :], wl[:, k, :]), (GH[:, kk, 0:n], GL[:, kk, 0:n]),
                                     kk == 0, kk == 21, w_, fr, gt if kk >= 20 else None, inc=k == kt - 1)
                        ended[u] = tok
                        if k0 == 16:
                            i = 2 * j + m
                            for s in range(n // 256):
                                c = slice(256 * s, 256 * s + 256)
                                a = stt(X[:, i, c], P[:, c], MOD[:, l, i0 + 2, i, s:s + 1], X[:, i, c], ALU.mult,
                                        ALU.add, tok)
                            done(b, a)
                            nxt.add(i, a)

        def mixer(nm, l, last, nxt):
            n = 512
            nq = 256 if last else 512
            nt = nq // 128
            w_in = t["w_in_2"][l]
            fw = [e.now() for e in engines]
            nb = 0
            for r in range(4):
                for h in range(6):
                    src = bass.AP(tensor=scr.tensor, offset=(l * 64) * 2790 + 465 * h + (7 - r) * 31 + 15,
                                  ap=[[2789, 64], [31, 4], [1, 64]])
                    pp = 64 * (r % 2)
                    pool.do(lambda e, src=src, pp=pp, r=r, h=h: e.dma_start(
                        BM[pp:pp + 64, r // 2, h, :].rearrange("p (y x) -> p y x", x=64), src)
                        .then_inc(sems["bm1"], 16), fw, (sems["bm0"], 32), inc=False)
                    nb += 16
            bmt = (sems["bm1"], nb * (l + 1))
            hw = norm_in(nm, lambda k, s: MOD[:, l, 4, k, s:s + 1], lambda k, s: MOD[:, l, 3, k, s:s + 1], (HH, HL), NT)
            z = dve.do(lambda e: e.memset(HP[:, :, :, :], 0.0), fw)
            hb = None

            def to(T, slot, w, scale=1.0):
                return lambda i, P, tok: [af(T[:, slot + i, 0:w], P[:, 0:w], ACT.Copy, tok, scale=scale)]

            def tov(c):
                return lambda i, P, tok: [cp(V2[:, :, c + 128 * i:c + 128 * i + 128],
                                             P[:, :].rearrange("p (q c) -> p q c", c=128), tok)]
            vt2 = [None, None]
            run(feat(w_in, 0, 3, nq, to(QA, 0, nq, 0.125), None, hw), feat(w_in, 384, 3, n, to(QA, 3, n)),
                tokm(w_in, 768, 3, 4, tov(0), None, TM2, vt2))
            bmr = None
            for q in range(2):
                v = BM[:, q, :, :].rearrange("p h (y x) -> p (h y) x", x=64)
                lim = bass.AP(tensor=WIN.tensor, offset=WIN.offset, ap=[list(WIN.ap[0]), [0, 24], [1, 64]])
                bmr = tt(v, v, lim, ALU.min, bmt)
            hb = ts(ST2[:, 216:240], vec("b_gate", 24 * l, 24), 0.5, None, ALU.mult, None)
            ns = ts(SM[:, 56:62], vec("sink", 6 * l, 6), -1.0, None, ALU.mult, None)
            ut = [None] * 2
            hp = [None, None]

            def uev(i, P, tok):
                if i < 2:
                    ut[i] = cp(TM2[:, i, 0:nq], P[:, 0:nq], tok, vt2[i])
                    return [ut[i]]
                T = TM2[:, 2, 0:nq]
                a = af(T, P[:, 0:nq], ACT.Tanh, tok, hp[0], scale=0.5)
                b_ = ts(T, T, 0.5, 0.5, ALU.mult, ALU.add, a)
                hp[i - 2] = tt(HP[:, i - 2, 0:nq // 256, 15:271], T.rearrange("p (s n) -> p s n", n=256),
                               TM2[:, i - 2, 0:nq].rearrange("p (s n) -> p s n", n=256), ALU.mult, b_, z, ut[i - 2])
                return [a]

            def projb():
                for j in range(3):
                    c_ = 1152 + 64 * j
                    chunk(8, 128, [(0, 64, wsrc(w_in, 0, 8, c_, c_ + 64)),
                                   (64, 128, wsrc(w_in, 0, 8, c_ + 192, c_ + 256))], [(0, 128)])
                    (wh, wl, w_, u), = unit()
                    b, P, fr = bank()
                    for k in range(8):
                        if k == 4:
                            yield
                        tok = w3(P[:, 0:nq], (wh[:, k, :], wl[:, k, :]), (HH[:, k, 0:nq], HL[:, k, 0:nq]),
                                 k == 0, k == 7, w_, fr, inc=k == 7)
                    ended[u] = tok
                    done(b, *to(QB, j, nq, 0.125)(0, P, tok))
                    yield
                yield from feat(w_in, 1536, 1, n, to(QB, 3, n))
                yield from tokm(w_in, 1664, 1, 4, tov(384), None, TM2, [hp[0], hp[1]])
                rt = None
                for i in range(4):
                    b, P, fr = bank()
                    tok = mm(P[:, 0:256], ROT, QB[:, i, 0:256], True, True, fr, act.now(), inc=True)
                    T = TM2[:, 0, 0:256]
                    a = tt(T, P[:, 0:256], CS2[:, 1, :], ALU.mult, tok, rt)
                    done(b, a)
                    c = tt(QB[:, i, 0:256], QB[:, i, 0:256], CS2[:, 0, :], ALU.mult, tok)
                    rt = tt(QB[:, i, 0:256], QB[:, i, 0:256], T, ALU.add, a, c)
                    yield
                rtt.append(rt)
            rtt = []
            ow = [None, None]
            cnt = [0]

            def ytile(o, yslot, q, ob):
                b, P, fr = bank()
                for i in range(3):
                    tok = tp(P[:, 128 * i:128 * i + 128], O2[:, ob, 128 * i:128 * i + 128], fr, o, inc=i == 2)
                yh = YH2[:, yslot:yslot + 3, 128 * q:128 * q + 128]
                yl = YL2[:, yslot:yslot + 3, 128 * q:128 * q + 128]
                Pv = P[:, 0:384].rearrange("p (i n) -> p i n", n=128)
                a = cp(yh, Pv, tok)
                c = tt(yl, Pv, yh.bitcast(f32), ALU.subtract, a)
                done(b, c)
                ow[ob] = tok

            def attn(br):
                jobs = []
                pend = []
                for q in range(nt):
                    ctx_q = q >= 2
                    k0, nk = (256, 256) if ctx_q else (0, 512)
                    for h in range(6):
                        if br == 0:
                            hs, Q_, K_ = h % 2, QA[:, h // 2, :], QA[:, 3 + h // 2, :]
                        else:
                            hs, Q_, K_ = h // 3, QB[:, h % 3, :], QB[:, 3, :]
                        r0 = slice(64 * hs, 64 * hs + 64)
                        vc = 64 * h if br == 0 else 384 + 64 * (h // 3)
                        ob = cnt[0] % 2
                        job = dict(q=Q_[r0, 128 * q:128 * q + 128], k=K_[r0, k0:k0 + nk], nk=nk,
                                   v=lambda x, vc=vc, k0=k0: V2[:, k0 // 128 + x, vc:vc + 64],
                                   o=O2[:, ob, 64 * h:64 * h + 64], w=rtt if br else None)
                        if not ctx_q:
                            if br == 0:
                                def bias(P, tok, tab=BM[:, q, h, :]):
                                    return tt(P[:, 0:256], P[:, 0:256], tab, ALU.add, tok, bmr)
                            else:
                                def bias(P, tok, c=slice(128, 256) if q == 0 else slice(0, 128), m=CAU if q == 0 else CAT):
                                    return tt(P[:, c], P[:, c], m, ALU.add, tok)
                            job["bias"] = bias
                        if br == 1:
                            job["sink"] = (vec("sink", 6 * l + h, 1), SM[:, 56 + h:57 + h])
                        if h == 0:
                            job["ow"] = lambda ob=ob: ow[ob]
                        if h == 5:
                            job["end"] = lambda o, q=q, ob=ob: pend.append((o, 3 * br, q, ob))
                        jobs.append(job)
                    cnt[0] += 1
                for _ in attend(jobs, P2, PT2, ST2):
                    yield
                    while pend:
                        ytile(*pend.pop(0))
                for p in pend:
                    ytile(*p)

            def conv():
                a = [None, None]
                for j in range(31):
                    for i in range(2):
                        A = CV[:, i, 0:nq].rearrange("p (s n) -> p s n", n=256)
                        x = HP[:, i, 0:nq // 256, j:j + 256]
                        wv = vec("dw_w", 62 * l + 2 * j + i)
                        if j == 0:
                            a[i] = ts(A, x, wv, vec("dw_b", 2 * l + i), ALU.mult, ALU.add, hp[i])
                        else:
                            a[i] = stt(A, x, wv, A, ALU.mult, ALU.add, a[i])
                        yield
                cvt.append(a)
            cvt = []

            def lnorm():
                w = yt = tt_ = None
                S6 = ST2[:, 240:246]
                tw = [None, None]
                for q in range(nt):
                    b, P, fr = bank()
                    for i in range(2):
                        tok = tp(P[:, 128 * i:128 * i + 128], CV[:, i, 128 * q:128 * q + 128], fr, cvt, inc=i == 1)
                    s = dve.do(lambda e, P=P: e.bn_stats(S6, P[:, 0:256]), tok)
                    s = dve.do(lambda e: e.bn_aggr(ST2[:, 246:248], S6), s)
                    v = ts(SM[:, 16:17], ST2[:, 247:248], 1e-6, None, ALU.add, None, s)
                    r = rpow(SM[:, 24:25], SM[:, 16:17], v)
                    yield
                    T = TM2[:, q % 2, 0:256]
                    y = ts(T, P[:, 0:256], ST2[:, 246:247], SM[:, 24:25], ALU.subtract, ALU.mult, r, s, tw[q % 2])
                    done(b, y)
                    b, P, fr = bank()
                    for i in range(2):
                        tok = tp(P[:, 128 * i:128 * i + 128], T[:, 128 * i:128 * i + 128], fr, y, inc=i == 1)
                    tw[q % 2] = tok
                    yield
                    for i in range(2):
                        U = TM2[:, 2, 128 * i:128 * i + 128]
                        V_ = TM2[:, 2, 256 + 128 * i:384 + 128 * i]
                        u = ts(U, P[:, 128 * i:128 * i + 128], vec("ln_g", 2 * l + i), vec("ln_b", 2 * l + i), ALU.mult,
                               ALU.add, tok, yt)
                        w = af(V_, U, ACT.Tanh, u, yt, scale=0.5)
                        w = stt(V_, V_, 1.0, U, ALU.add, ALU.mult, w)
                        yt2 = ysplit(YH2[:, 6 + i, 128 * q:128 * q + 128], YL2[:, 6 + i, 128 * q:128 * q + 128], V_, w, 0.5)
                    done(b, u)
                    yt = yt2
                    yield

            mw, bw = [None] * 2, [None] * 2
            accs = {}
            mtok = []

            def merge(br, wo, kb, kn):
                yt = [act.now(), dve.now()]
                for mp in range(4):
                    ga = [None, None]

                    def gev(m, P, tok):
                        i = 8 * br + 2 * mp + m
                        ga[m] = af(MT[:, m, 0:nq], P[:, 0:nq], ACT.Tanh, tok, hb, mw[m], scale=0.5,
                                   bias=ST2[:, 216 + i:217 + i])
                        return [ga[m]]
                    yield from columns(w_in, 2304 + 1024 * br + 256 * mp, 2, 8, nq, (HH, HL), 0, gev, 0, None)
                    chunk(kn, 256, [(0, 256, wsrc(t[wo][l], 0, kn, 256 * mp, 256 * mp + 256))], [(0, 256)])
                    (wh, wl, w_, u), = unit()
                    for m in range(2):
                        i = 2 * mp + m
                        b, P, fr = bank()
                        for k in range(kn):
                            tok = w3(P[:, 0:nq], (wh[:, k, 128 * m:128 * m + 128], wl[:, k, 128 * m:128 * m + 128]),
                                     (YH2[:, kb + k, 0:nq], YL2[:, kb + k, 0:nq]), k == 0, k == kn - 1, w_, fr, yt,
                                     inc=k == kn - 1)
                        A = ACC[:, i, 0:nq]
                        if br == 0:
                            accs[i] = mw[m] = stt(A, MT[:, m, 0:nq], 1.0, P[:, 0:nq], ALU.add, ALU.mult, tok, ga[m])
                        else:
                            B_ = MT[:, 2 + m, 0:nq]
                            mw[m] = stt(B_, MT[:, m, 0:nq], 1.0, P[:, 0:nq], ALU.add, ALU.mult, tok, ga[m], bw[m])
                            accs[i] = bw[m] = tt(A, A, B_, ALU.add, mw[m], accs[i], on=pool)
                            if br == 2:
                                mtok.append(ysplit(MH[:, i, 0:nq], ML[:, i, 0:nq], A, accs[i], 0.5))
                        done(b, mw[m])
                    ended[u] = tok
                    yield

            cvp = Part(conv(), 1.0)

            def pj2():
                yield from feat(w_in, 1792, 4, nq, uev)
                yield from projb()
            att = Part(attn(0), 1.0)
            pj = Part(pj2(), 1.2)

            while hp[1] is None:
                att.step()
                pj.step()
            weave(att, pj, cvp, until=pj)
            weave(att, cvp, until=att)
            att = Part(attn(1), 1.0)
            weave(att, Part(merge(0, "w_out_a_2", 0, 3), 24 / 20), cvp)
            weave(Part(lnorm(), 1.0), Part(merge(1, "w_out_b_2", 3, 3), 12 / 20))
            run(merge(2, "w_out_c_2", 6, 2))

            def xev(i, P, tok):
                for s in range(nq // 256):
                    c = slice(256 * s, 256 * s + 256)
                    a = stt(X[:, i, c], P[:, c], MOD[:, l, 5, i, s:s + 1], X[:, i, c], ALU.mult, ALU.add, tok)
                nxt.add(i, a)
                return [a]
            run(feat(t["w_out_2"][l], 0, 8, nq, xev, (MH, ML), mtok))

        for l in range(DEPTH):
            last = l == DEPTH - 1
            nn = Norm(512, SS, SQ, DG)
            ffn(nm, l, t["w_ffn1_gu_2"][l], t["w_ffn1_down_2"][l], 512, 0, nn)
            nq = 256 if last else 512
            n2 = Norm(nq, SS, SQ, DG)
            mixer(nn, l, last, n2)
            nm = Norm(nq, SS, SQ, DG)
            ffn(n2, l, t["w_ffn2_gu_2"][l], t["w_ffn2_down_2"][l], nq, 6, nm)
        a = norm_out(nm, lambda k: vec("final_g", k), lambda k: OUT[:, k, :])
        dma(out.rearrange("(k p) n -> p k n", p=128), OUT[:, :, :], sems["out"], a)
        sp.do(None, (sems["out"], 16), inc=False)
        return pe, act, dve, pool, sp, (chunks, units)

    plan = trace(None)[5]
    pe, act, dve, pool, sp, _ = trace(plan)
    with nc.Block() as block:
        @block.sync
        def _(e):
            sp.emit(e)

        @block.scalar
        def _(e):
            act.emit(e)

        @block.vector
        def _(e):
            dve.emit(e)

        @block.gpsimd
        def _(e):
            pool.emit(e)

        @block.tensor
        def _(e):
            pe.emit(e)


_WEIGHTS = ["w_in", "w_out", "w_ada_2", "w_ffn1_gu_2", "w_ffn1_down_2", "w_ffn2_gu_2", "w_ffn2_down_2", "w_in_2",
            "w_out_a_2", "w_out_b_2", "w_out_c_2", "w_out_2"]


def constants():
    import numpy as np
    f = np.float32
    i = np.arange(128)
    ident = np.eye(128, dtype=f)
    tri = (i[:, None] <= i[None, :]).astype(f)
    rot = np.zeros((128, 128), f)
    for h in (0, 64):
        for d in range(32):
            rot[h + 32 + d, h + d] = -1.0
            rot[h + d, h + 32 + d] = 1.0
    cau = np.where(i[None, :] <= i[:, None], 0.0, -1e30).astype(f)
    qc = i % 64
    w0 = np.clip(qc - 8, 0, 48)[:, None]
    x = np.arange(64)[None, :]
    inw = (x >= w0) & (x < w0 + 16)
    sel = np.zeros((128, 2), f)
    for g in range(4):
        sel[32 * g, 0] = sel[32 * g + 1, 1] = 1.0
    cst = np.concatenate([ident, tri, rot, cau, cau.T, np.where(inw, 3e38, -1e30).astype(f), sel], axis=1)
    q = (np.arange(2)[None, :, None] * 128 + i[:, None, None])
    k = np.arange(256)[None, None, :]
    alibi = np.where(k <= q, -(q - k).astype(f), f(-1e32)).astype(f)
    lg = np.log(f(1.0) - np.exp2(f(-5.0) - np.arange(4, dtype=f))).astype(f)
    dec = np.zeros((128, 4, 384), f)
    for h in range(4):
        d = (np.arange(256)[None, :] - i[:, None]).astype(f)
        full = np.where(d >= 0, np.exp((lg[h] * np.maximum(d, f(0.0))).astype(f)), f(0.0)).astype(f) * f(0.125)
        dec[:, h, 0:256] = full
        dec[:, h, 256:384] = full[:, 0:128]
    pos = np.arange(256, dtype=f)
    th = (f(1.0) / (f(10000.0) ** np.linspace(0.0, 1.0, 32, dtype=f))).astype(f)
    ang = (pos[:, None] * th[None, :]).astype(f).T
    cs1 = np.stack([np.tile(np.cos(ang), (4, 1)), np.tile(np.sin(ang), (4, 1))], axis=1).astype(f)
    inv = (f(10000.0) ** (-np.arange(16, dtype=f) / f(16))).astype(f)
    tk = np.arange(256)
    a2 = np.concatenate([(tk // 64).astype(f)[:, None] * inv, (tk % 64).astype(f)[:, None] * inv], axis=1).astype(f).T
    cs2 = np.stack([np.tile(np.cos(a2), (4, 1)), np.tile(np.sin(a2), (4, 1))], axis=1).astype(f)
    return {"cst": cst, "alibi": alibi, "decay": dec, "cs1": cs1, "cs2": cs2}


def kernel(**inputs):
    import numpy as _np
    import concourse.bacc as _bacc
    from concourse import mybir as _mybir
    from concourse.bass_utils import run_bass_kernel_spmd as _run

    nc = _bacc.Bacc("TRN2", target_bir_lowering=False, num_devices=1)
    a = {n: _np.asarray(v) for n, v in inputs.items()}

    def col(v):
        v = v.reshape(-1, v.shape[-1] // 128, 128)
        return v.transpose(2, 0, 1).reshape(128, -1)

    def row(v):
        return _np.broadcast_to(v.reshape(1, -1), (128, v.size))
    parts = [("norm_w", col(a["norm_w"])), ("conv_w", col(a["conv_w"].reshape(8, 512))), ("conv_b", col(a["conv_b"])),
             ("ret_norm_w", col(a["ret_norm_w"])), ("mlstm_norm_w", col(a["mlstm_norm_w"])),
             ("final_norm_w", col(a["final_norm_w"][None])), ("gate_bias", row(a["gate_bias"])),
             ("cc", col(_np.stack([a["c_2"][0], a["c_ctx_2"]])).reshape(128, 2, 8).transpose(0, 2, 1).reshape(128, 16)),
             ("b_ada", col(a["b_ada_2"])), ("norm_g", col(a["norm_g_2"].reshape(6, 1024))),
             ("b_gate", col(a["b_gate_2"])), ("sink", row(a["sw_sink_2"])),
             ("dw_w", col(a["conv_dw_w_2"].reshape(62, 256))), ("dw_b", col(a["conv_dw_b_2"])),
             ("ln_g", col(a["conv_ln_g_2"])), ("ln_b", col(a["conv_ln_b_2"])), ("final_g", col(a["final_g_2"][None]))]
    arrays = {"vec": _np.ascontiguousarray(_np.concatenate([p for _, p in parts], axis=1)),
              "xT": _np.ascontiguousarray(a["x"][0].T), "ctxT": _np.ascontiguousarray(a["ctx_2"][0].T),
              "rpb": _np.ascontiguousarray(a["na_rpb_2"].reshape(2, 2790))}
    for n in _WEIGHTS:
        arrays[n] = _np.ascontiguousarray(a[n])
    arrays.update(constants())
    t = {n: nc.dram_tensor(f"in_{n}", v.shape, _mybir.dt.from_np(v.dtype), kind="ExternalInput").ap()
         for n, v in arrays.items()}
    t["_vec"] = [(n, p.shape[1]) for n, p in parts]
    out = nc.dram_tensor("out_0_dram", (1024, 256), _mybir.dt.from_np(_np.dtype("float32")), kind="ExternalOutput").ap()
    program(nc, t, out)
    r = _run(nc, [{f"in_{n}": v for n, v in arrays.items()}], core_ids=[0])
    return _np.ascontiguousarray(r.results[0]["out_0_dram"].T)[None]
```

```python
import concourse.bass as bass
from concourse import mybir

DEPTH = 2
KC, KP, KM, KL = 0.7, 1.2, 1.2, 0.6
CM, CU, CA, CR, CG, EV = 2.0, 3.0, 2.0, 1.5, 3.0, 2
D = 1024
NF = 22


def program(nc, t, out):
    f32 = mybir.dt.float32
    f32r = mybir.dt.float32r
    ALU = mybir.AluOpType
    ACT = mybir.ActivationFunctionType
    AX = mybir.AxisListType

    sb = lambda n, s, d=f32: nc.alloc_sbuf_tensor(n, s, d)
    X = sb("X", [128, 8, 512])
    NR = 3
    RAW = sb("RAW", [128, NR, 2048])
    NS = 3
    WH = sb("WH", [128, NS, 1024], f32r)
    WL = sb("WL", [128, NS, 1024], f32r)
    CST = sb("CST", [128, 5 * 128 + 64 + 2])
    IDN, TRI, ROT, CAU, CAT = (CST[:, 128 * i:128 * i + 128] for i in range(5))
    WIN = CST[:, 640:704]
    SEL = CST[:, 704:706]
    ONE = sb("ONE", [128, 128])
    CS2 = sb("CS2", [128, 2, 256])
    VEC = sb("VEC", [128, t["vec"].shape[1]])
    SM = sb("SM", [128, 112])
    MOD = sb("MOD", [128, DEPTH, 9, 8, 2])
    AS = sb("AS", [128, 512])
    AC = sb("AC", [128, 8, 32])
    R0 = (nc.sbuf_base + 63) // 64 * 64
    K = 1024

    def at(name, off, shape, d=f32):
        return nc.alloc_sbuf_tensor_at(name, shape, d, offset=R0 + int(off * K))

    HH = at("HH", 0, [128, 8, 512], f32r)
    HL = at("HL", 16, [128, 8, 512], f32r)
    H1H = at("H1H", 0, [128, 8, 256], f32r)
    H1L = at("H1L", 8, [128, 8, 256], f32r)
    B0 = 32
    GH = at("GH", B0, [128, NF, 512], f32r)
    GL = at("GL", B0 + 44, [128, NF, 512], f32r)
    FT = at("FT", B0 + 88, [128, 2, 512])
    SS = at("SS", B0 + 92, [128, 512])
    SQ = at("SQ", B0 + 94, [128, 2, 512])
    DG = at("DG", B0 + 98, [128, 4, 128])
    NT = at("NT", B0 + 88, [128, 2, 512])
    PJ = at("PJ", B0, [128, 24, 256])
    SS1 = at("SS1", B0, [128, 256])
    SQ1 = at("SQ1", B0 + 1, [128, 2, 256])
    DG1 = at("DG1", B0 + 3, [128, 2, 128])
    NT1 = at("NT1", B0 + 4, [128, 4, 256])
    VA = at("VA", B0 + 24, [128, 2, 512])
    VB = at("VB", B0 + 28, [128, 2, 256])
    VC = at("VC", B0 + 30, [128, 2, 4, 66])
    CO = at("CO", B0 + 33, [128, 2, 256])
    YH1 = at("YH1", B0 + 35, [128, 8, 256], f32r)
    YL1 = at("YL1", B0 + 43, [128, 8, 256], f32r)
    DT = at("DT", B0 + 51, [128, 4, 384])
    ALI = at("ALI", B0 + 57, [128, 2, 256])
    CS1 = at("CS1", B0 + 59, [128, 2, 256])
    CP = at("CP", B0 + 61, [128, 4, 260])
    W8 = at("W8", B0 + 65.25, [128, 8, 8])
    W8H = at("W8H", B0 + 65.5, [128, 8, 8], f32r)
    W8L = at("W8L", B0 + 65.75, [128, 8, 8], f32r)
    ST1 = at("ST1", B0 + 66, [128, 256])
    P1 = at("P1", B0 + 67, [128, 3, 256])
    PT1 = at("PT1", B0 + 70, [128, 3, 256])
    O1 = at("O1", B0 + 73, [128, 2, 2, 128])
    TM1 = at("TM1", B0 + 75, [128, 2, 512])
    RT = at("RT", B0 + 79, [128, 256])
    PR = at("PR", B0 + 80, [128, 2, 384])
    YV = at("YV", 16, [128, 2, 256])
    YT = at("YT", B0 + 83, [128, 512])
    HC = at("HC", B0 + 85, [128, 512])
    MA = at("MA", B0 + 87, [128, 192])
    NU1 = at("NU1", B0 + 87.75, [128, 264])
    MI = at("MI", B0 + 89, [128, 4, 512])
    HN = at("HN", B0 + 99, [128, 2, 80])
    QA = at("QA", B0, [128, 6, 512])
    BM = at("BM", B0 + 12, [128, 2, 6, 256])
    QB = at("QB", B0 + 24, [128, 4, 512])
    V2 = at("V2", B0 + 32, [128, 4, 512])
    YH2 = at("YH2", B0 + 40, [128, 8, 512], f32r)
    YL2 = at("YL2", B0 + 56, [128, 8, 512], f32r)
    HP = at("HP", B0 + 72, [128, 2, 2, 288])
    CV = at("CV", B0 + 76.5, [128, 2, 512])
    P2 = at("P2", B0 + 80.5, [128, 2, 512])
    PT2 = at("PT2", B0 + 84.5, [128, 2, 512])
    O2 = at("O2", B0 + 88.5, [128, 2, 384])
    ST2 = at("ST2", B0 + 91.5, [128, 256])
    TM2 = at("TM2", B0 + 92.5, [128, 3, 512])
    ACC = at("ACC", B0, [128, 8, 512])
    MT = at("MT", B0 + 16, [128, 4, 512])
    MH = at("MH", B0 + 24, [128, 8, 512], f32r)
    ML = at("ML", B0 + 72, [128, 8, 512], f32r)
    OUT = at("OUT", B0, [128, 8, 256])

    PS = [nc.alloc_psum_tensor(f"PS{i}", [128, 512], f32) for i in range(8)]
    sems = {n: nc.alloc_semaphore("s_" + n) for n in ("pe", "act", "dve", "pool", "c0", "out", "bm0", "bm1")}
    rsem = [nc.alloc_semaphore(f"s_raw{i}") for i in range(NR)]
    c1 = nc.alloc_semaphore("s_c1")
    c2 = nc.alloc_semaphore("s_c2")
    c3 = nc.alloc_semaphore("s_c3")
    cx = nc.alloc_semaphore("s_cx")
    scr = nc.dram_tensor("rpb_rows", (DEPTH, 64, 2790), f32, kind="Internal").ap()

    def layout():
        o, v = {}, 0
        for n, w in t["_vec"]:
            o[n] = v
            v += w
        return o
    VO = layout()

    def vec(n, i, w=1):
        return VEC[:, VO[n] + i:VO[n] + i + w]

    class Engine:

        def __init__(self, sem):
            self.sem, self.n, self.q = sem, 0, []

        def do(self, fn, *waits, inc=True):
            self.q.append((waits, fn, inc))
            self.n += inc
            return (self.sem, self.n)

        def now(self):
            return (self.sem, self.n)

        def emit(self, e):
            seen = {}

            def wait(w):
                if w is None:
                    return
                if isinstance(w, list):
                    for x in w:
                        wait(x)
                    return
                s, v = w
                if v > seen.get(id(s), 0):
                    e.wait_ge(s, v)
                    seen[id(s)] = v
            for waits, fn, inc in self.q:
                for w in waits:
                    wait(w)
                if fn is not None:
                    i = fn(e)
                    if inc:
                        i.then_inc(self.sem, 1)

    def trace(plan):
        pe, act, dve, pool = (Engine(sems[n]) for n in ("pe", "act", "dve", "pool"))
        sp = Engine(None)
        engines = (pe, act, dve, pool)

        def dma(dst, src, sem, *waits):
            sp.do(lambda e: e.dma_start(dst, src).then_inc(sem, 16), *waits, inc=False)

        def fence():
            now = [e.now() for e in engines]
            for e in engines:
                e.do(None, now, inc=False)
            return now

        def mm(o, l, r, start, stop, *w, inc=False):
            return pe.do(lambda e: e.matmul(o, l, r, start=start, stop=stop), *w, inc=inc)

        def tp(o, i, *w, inc=False):
            return pe.do(lambda e: e.transpose(o, i, IDN), *w, inc=inc)

        def af(o, i, f, *w, scale=1.0, bias=0.0, acc=None):
            if acc is None:
                return act.do(lambda e: e.activation(o, i, f, bias=bias, scale=scale), *w)
            return act.do(lambda e: e.activation(o, i, f, bias=bias, scale=scale, accum_out=acc), *w)

        def cp(o, i, *w):
            return act.do(lambda e: e.activation(o, i, ACT.Copy), *w)

        def vcp(o, i, *w):
            return dve.do(lambda e: e.tensor_copy(o, i), *w)

        def tt(o, a, b, op, *w, on=None):
            return (on or dve).do(lambda e: e.tensor_tensor(out=o, in0=a, in1=b, op=op), *w)

        def ts(o, a, s1, s2, op0, op1, *w):
            if op1 is None:
                return dve.do(lambda e: e.tensor_scalar(o, a, s1, None, op0), *w)
            return dve.do(lambda e: e.tensor_scalar(o, a, s1, s2, op0, op1), *w)

        def stt(o, a, s, b, op0, op1, *w):
            return dve.do(lambda e: e.scalar_tensor_tensor(out=o, in0=a, scalar=s, in1=b, op0=op0, op1=op1), *w)

        def rmax(o, i, neg, *w):
            return dve.do(lambda e: e.tensor_reduce(o, i, AX.X, ALU.max, negate=neg), *w)

        def recip(o, i, *w):
            return dve.do(lambda e: e.reciprocal(o, i), *w)

        def rpow(o, i, *w):
            return pool.do(lambda e: e.tensor_tensor(out=o, in0=i, in1=MHALF[:, 0:i.shape[-1]], op=ALU.pow), *w)

        MHALF = SM[:, 96:112]

        free, held = [None] * 7, [False] * 7
        turn = [0]

        def bank():
            while held[turn[0] % 7]:
                turn[0] += 1
                assert not all(held)
            i = turn[0] % 7
            turn[0] += 1
            held[i] = True
            return i, PS[i], free[i]

        def done(i, *tok):
            free[i], held[i] = list(tok), False

        def run(*gens):
            for g in gens:
                for _ in g:
                    pass

        class Part:

            def __init__(self, gen, cost):
                self.gen, self.cost, self.spent, self.over = gen, cost, 0.0, False

            def step(self):
                try:
                    self.spent += self.cost * (next(self.gen) or 1.0)
                except StopIteration:
                    self.over = True

        def weave(*parts, until=None):
            low = min(p.spent for p in parts)
            for p in parts:
                p.spent -= low
            while True:
                live = [p for p in parts if not p.over]
                if not live or (until is not None and until.over):
                    return
                min(live, key=lambda p: p.spent).step()

        ck = dict(load=0, chunk=0, unit=0, split=0, cur=0)
        rel, ended, ready, arrived, count = {}, {}, {}, {}, [0] * NR
        chunks, units = [], []

        def load(c):
            while ck["load"] <= c:
                i = ck["load"]
                assert i < NR or i - NR in rel
                kt, cols, srcs = plan[0][i]
                view = RAW[:, i % NR, 0:kt * cols].rearrange("p (k c) -> p k c", c=cols)
                for c0, c1_, src in srcs:
                    dma(view[:, :, c0:c1_], src, rsem[i % NR], rel.get(i - NR))
                count[i % NR] += 16 * len(srcs)
                arrived[i] = (rsem[i % NR], count[i % NR])
                ck["load"] += 1

        def ahead():
            while ck["load"] < len(plan[0]) and (ck["load"] < NR or ck["load"] - NR in rel):
                load(ck["load"])

        def rawchunk(kt, cols, src, use):
            c = ck["chunk"]
            ck["chunk"] += 1
            if not plan:
                chunks.append((kt, cols, [(0, cols, src)]))
            else:
                load(c)
            rel[c] = [use(RAW[:, c % NR, 0:kt * cols].rearrange("p (k c) -> p k c", c=cols), arrived.get(c))]
            if plan:
                ahead()

        def uview(R, u, kt, w):
            return R[:, u % NS, 0:kt * w].rearrange("p (k c) -> p k c", c=w)

        def split(need, upto):
            while ck["split"] <= min(upto, len(plan[1]) - 1):
                u = ck["split"]
                c, a, b, last = plan[1][u]
                if u > need and ((u >= NS and u - NS not in ended) or
                                 any(i >= NR and i - NR not in rel for i in range(ck["load"], c + 1))):
                    return
                load(c)
                kt, cols, _ = plan[0][c]
                raw = RAW[:, c % NR, 0:kt * cols].rearrange("p (k c) -> p k c", c=cols)[:, :, a:b]
                h, l = uview(WH, u, kt, b - a), uview(WL, u, kt, b - a)
                was = ended.get(u - NS)
                x = cp(h, raw, arrived[c], was)
                y = tt(l, raw, h.bitcast(f32), ALU.subtract, x, was, arrived[c])
                ready[u] = [x, y]
                if last:
                    rel[c] = [x, y]
                    ahead()
                ck["split"] += 1

        def chunk(kt, cols, srcs, us):
            c = ck["chunk"]
            ck["chunk"] += 1
            if not plan:
                chunks.append((kt, cols, srcs))
                units.extend((c, a, b, j == len(us) - 1) for j, (a, b) in enumerate(us))

        def unit(n=1):
            r = []
            for _ in range(n):
                u = ck["unit"]
                ck["unit"] += 1
                if plan:
                    split(u, u + NS - n)
                c, a, b, _ = (plan[1] if plan else units)[u]
                kt = (plan[0] if plan else chunks)[c][0]
                r.append((uview(WH, u, kt, b - a), uview(WL, u, kt, b - a), ready.get(u), u))
            return r

        def w3(o, w, h, first, last, *waits, flip=False, inc=False):
            (wh, wl), (hh, hl) = w, h
            pairs = [(wh, hh), (wh, hl), (wl, hh)] if not flip else [(hh, wh), (hh, wl), (hl, wh)]
            for j, (l, r) in enumerate(pairs):
                tok = mm(o, l, r, first and j == 0, last and j == 2, *(waits if j == 0 else ()), inc=inc and j == 2)
            return tok

        def wsrc(w, k0, kt, c0, c1_):
            return w[128 * k0:128 * (k0 + kt), c0:c1_].rearrange("(k p) c -> p k c", p=128)

        def columns(w, c0, m, kt, n, hin, k0, ev, i, hw):
            chunk(kt, 128 * m, [(0, 128 * m, wsrc(w, 0, kt, c0, c0 + 128 * m))],
                  [(128 * j, 128 * j + 128) for j in range(m)])
            if hw is not None:
                us = unit(m)
                bk = [bank() for _ in us]
                for k in range(kt):
                    for (wh, wl, w_, _), (b, P, fr) in zip(us, bk):
                        tok = w3(P[:, 0:n], (wh[:, k, :], wl[:, k, :]),
                                 (hin[0][:, k0 + k, 0:n], hin[1][:, k0 + k, 0:n]), k == 0, k == kt - 1,
                                 w_, fr, hw[k], inc=k == kt - 1)
                for j, ((_, _, _, u), (b, P, fr)) in enumerate(zip(us, bk)):
                    ended[u] = tok
                    done(b, *ev(i + j, P, tok))
                yield
                return
            for j in range(m):
                (wh, wl, w_, u), = unit()
                b, P, fr = bank()
                for k in range(kt):
                    if k == 4 and n == 512:
                        yield
                    tok = w3(P[:, 0:n], (wh[:, k, :], wl[:, k, :]),
                             (hin[0][:, k0 + k, 0:n], hin[1][:, k0 + k, 0:n]), k == 0, k == kt - 1,
                             w_, fr, inc=k == kt - 1)
                ended[u] = tok
                done(b, *ev(i + j, P, tok))
                yield

        def feat(w, c0, nt, n, ev, hin=None, hw=None):
            hin = hin or (HH, HL)
            for i in range(0, nt, 2):
                m = min(2, nt - i)
                yield from columns(w, c0 + 128 * i, m, 8, n, hin, 0, ev, i, hw if i == 0 else None)

        def tokm(w, c0, nu, ntok, ev, hin, VT, was):
            n = 128 * ntok
            pend = []

            def flip(i, c):
                b, P, fr = bank()
                for q in range(ntok):
                    tok = tp(P[:, 128 * q:128 * q + 128], VT[:, i % 2, 128 * q:128 * q + 128], fr, c, inc=q == ntok - 1)
                was[i % 2] = tok
                done(b, *ev(i, P, tok))

            def fev(i, P, tok):
                c = cp(VT[:, i % 2, 0:n], P[:, 0:n], tok, was[i % 2])
                pend.append((i, c))
                return [c]
            for _ in feat(w, c0, nu, n, fev, hin):
                yield
                if len(pend) > 1:
                    flip(*pend.pop(0))
            yield
            for p in pend:
                flip(*p)

        class Norm:

            def __init__(self, n, S, Q, G):
                self.n, self.S, self.Q, self.G, self.was, self.tok = n, S, Q, G, [None, None], None
                self.last = []

            def add(self, i, tok):
                n = self.n
                if i == 0:
                    self.tok = af(self.S[:, 0:n], X[:, 0, 0:n], ACT.Square, tok)
                    return
                a = af(self.Q[:, i % 2, 0:n], X[:, i, 0:n], ACT.Square, tok, self.was[i % 2])
                if i >= 6:
                    self.last.append(a)
                    return
                self.tok = tt(self.S[:, 0:n], self.S[:, 0:n], self.Q[:, i % 2, 0:n], ALU.add, a, self.tok, on=pool)
                self.was[i % 2] = self.tok

            def rstd(self):
                q = self.n // 128
                b, P, fr = bank()
                for i in range(q):
                    c = slice(128 * i, 128 * i + 128)
                    mm(P[:, i:i + 1], self.S[:, c], ONE[:, 0:1], True, False, fr, self.tok)
                    mm(P[:, i:i + 1], self.Q[:, 0, c], ONE[:, 0:1], False, False, self.last[0])
                    tok = mm(P[:, i:i + 1], self.Q[:, 1, c], ONE[:, 0:1], False, True, self.last[1], inc=i == q - 1)
                v = ts(SM[:, 0:q], P[:, 0:q], 1.0 / D, 1e-6, ALU.mult, ALU.add, tok)
                done(b, v)
                r = rpow(SM[:, 8:8 + q], SM[:, 0:q], v)
                for i in range(q):
                    d = ts(self.G[:, i, :], IDN, SM[:, 8 + i:9 + i], None, ALU.mult, None, r)
                b, P, fr = bank()
                tok = mm(P[:, 0:self.n], ONE[:, :], self.G[:, 0:q, :], True, True, fr, d, inc=True)
                return b, P, tok

        def norm_in(nm, gs, sh, hin, T_, fill=lambda: None):
            n = nm.n
            fill()
            b, P, tok = nm.rstd()
            fill()
            if plan:
                split(-1, ck["unit"] + NS - 2)
            r = [[] for _ in range(8)]
            nb = T_.shape[1]
            pend = []

            def low(k, s, T, H, L, h):
                if sh is None:
                    l = tt(L, T, H.bitcast(f32), ALU.subtract, h)
                else:
                    l = stt(L, T, sh(k, s), H.bitcast(f32), ALU.add, ALU.subtract, h)
                r[k] += [h, l]
            for k in range(8):
                for s in range(n // 256):
                    c = slice(256 * s, 256 * s + 256)
                    H, L, T = hin[0][:, k, c], hin[1][:, k, c], T_[:, k % nb, c]
                    if len(pend) == 2:
                        low(*pend.pop(0))
                    a = stt(T, X[:, k, c], gs(k, s), P[:, c], ALU.mult, ALU.mult, tok, r[k - nb] if k >= nb else None)
                    h = cp(H, T, a) if sh is None else af(H, T, ACT.Identity, a, bias=sh(k, s))
                    pend.append((k, s, T, H, L, h))
            for p in pend:
                low(*p)
            done(b, a)
            return r

        def norm_out(nm, g, wr, after=None):
            b, P, tok = nm.rstd()
            for k in range(8):
                a = stt(wr(k), X[:, k, 0:nm.n], g(k), P[:, 0:nm.n], ALU.mult, ALU.mult, tok)
                if after:
                    after(k, a)
            done(b, a)
            return a

        def attend(jobs, PB, PTB, ST, LAG, NB):
            n = len(jobs)
            st = {}
            for i in range(n + 2 * LAG):
                if i < n:
                    j = jobs[i]
                    nk = j["nk"]
                    b, P, fr = bank()
                    tok = mm(P[:, 0:nk], j["q"], j["k"], True, True, fr, j.get("w"), inc=True)
                    if "bias" in j:
                        tok = j["bias"](P, tok)
                    nm, sm, rs = ST[:, i:i + 1], ST[:, 64 + i:65 + i], ST[:, 128 + i:129 + i]
                    m = rmax(nm, P[:, 0:nk], True, tok)
                    if j.get("sink") is not None:
                        sk, nsk = j["sink"]
                        m = ts(nm, nm, nsk, None, ALU.min, None, m)
                    e = af(PB[:, i % NB, 0:nk], P[:, 0:nk], ACT.Exp, m, st.get(("t", i - NB)), bias=nm, acc=sm)
                    done(b, e)
                    e2 = None
                    if j.get("sink") is not None:
                        e2 = af(ST[:, 192 + i:193 + i], sk, ACT.Exp, m, bias=nm)
                    st["e", i] = [e, e2]
                i1 = i - LAG
                if 0 <= i1 < n:
                    j = jobs[i1]
                    kt = j["nk"] // 128
                    sm, rs = ST[:, 64 + i1:65 + i1], ST[:, 128 + i1:129 + i1]
                    b, P, fr = bank()
                    for x in range(kt):
                        tok = tp(P[:, 128 * x:128 * x + 128], PB[:, i1 % NB, 128 * x:128 * x + 128], fr, st["e", i1],
                                 inc=x == kt - 1)
                    st["t", i1] = tok
                    c = cp(PTB[:, i1 % NB, 0:128 * kt], P[:, 0:128 * kt], tok, st.get(("pv", i1 - NB)))
                    done(b, c)
                    st["c", i1] = c
                    e3 = st["e", i1]
                    if j.get("sink") is not None:
                        e3 = tt(sm, sm, ST[:, 192 + i1:193 + i1], ALU.add, e3)
                    st["r", i1] = recip(rs, sm, e3)
                i2 = i - 2 * LAG
                if 0 <= i2 < n:
                    j = jobs[i2]
                    kt = j["nk"] // 128
                    b, P, fr = bank()
                    for x in range(kt):
                        tok = mm(P[:, 0:64], PTB[:, i2 % NB, 128 * x:128 * x + 128], j["v"](x), x == 0, x == kt - 1,
                                 fr, st["c", i2], inc=x == kt - 1)
                    st["pv", i2] = tok
                    o = ts(j["o"], P[:, 0:64], ST[:, 128 + i2:129 + i2], None, ALU.mult, None, tok, st["r", i2],
                           j["ow"]() if "ow" in j else None)
                    done(b, o)
                    if "end" in j:
                        j["end"](o)
                yield

        def ysplit(yh, yl, src, tok, scale=None):
            if scale is None:
                a = cp(yh, src, tok)
                return [a, tt(yl, src, yh.bitcast(f32), ALU.subtract, a, tok)]
            a = af(yh, src, ACT.Copy, tok, scale=scale)
            return [a, stt(yl, src, scale, yh.bitcast(f32), ALU.mult, ALU.subtract, a, tok)]

        def head_norm(x, src, tok, dst, res):
            S, A, V, R = HN[:, x, 0:48], HN[:, x, 48:64], HN[:, x, 64:72], HN[:, x, 72:80]
            for g in range(8):
                a = dve.do(lambda e, g=g, i=src(g): e.bn_stats(S[:, 6 * g:6 * g + 6], i), tok)
                last = dve.do(lambda e, g=g: e.bn_aggr(A[:, 2 * g:2 * g + 2], S[:, 6 * g:6 * g + 6]), a)
                if g % 2:
                    yield
            v = ts(V, HN[:, x, 49:64:2], 1e-5, None, ALU.add, None, last)
            r = rpow(R, V, v)
            yield
            for g in range(8):
                a = ts(dst(g), src(g), A[:, 2 * g:2 * g + 1], R[:, g:g + 1], ALU.subtract, ALU.mult, r, last)
            res.append(a)
            yield

        cload = [(VEC[:, :], t["vec"]), (CST[:, :], t["cst"])]
        for o, i in cload:
            act.do(lambda e, o=o, i=i: e.dma_start(o, i).then_inc(sems["c0"], 16), inc=False)
        c0 = (sems["c0"], 16 * len(cload))
        act.do(lambda e: e.dma_start(X[:, :, 0:256], t["xT"].rearrange("(k p) n -> p k n", p=128)).then_inc(cx, 16),
               inc=False)
        late = []
        for l in range(DEPTH):
            late.append(lambda e, l=l: e.dma_start(scr[l, :, :], bass.AP(tensor=t["rpb"].tensor, offset=2790 * l,
                   ap=[[0, 64], [1, 2790]])).then_inc(sems["bm0"], 16))
        for o, i in ((CS2[:, :, :], t["cs2"]), (X[:, :, 256:512], t["ctxT"].rearrange("(k p) n -> p k n", p=128))):
            late.append(lambda e, o=o, i=i: e.dma_start(o, i).then_inc(c2, 16))
        act.do(lambda e, i=t["w_in"][0][:, 4352:4360].rearrange("(k p) c -> p k c", p=128):
               e.dma_start(W8[:, :, :], i).then_inc(c3, 16), inc=False)
        for o, i in ((CS1[:, :, :], t["cs1"]), (DT[:, :, :], t["decay"]), (ALI[:, :, :], t["alibi"])):
            late.insert(0, lambda e, o=o, i=i: e.dma_start(o, i).then_inc(c1, 16))
        c1t = (c1, 48)
        m1 = dve.do(lambda e: e.memset(ONE[:, :], 1.0))
        m2 = dve.do(lambda e: e.memset(MHALF, -0.5))
        m3 = dve.do(lambda e: e.memset(AC[:, :, :], 0.0))
        for e in engines:
            e.do(None, c0, m2, inc=False)
        z1 = dve.do(lambda e: e.memset(CP[:, :, 0:3], 0.0))
        z2 = dve.do(lambda e: e.memset(VC[:, :, :, 64:65], 1.0))

        a = af(SM[:, 80:96], vec("cc", 0, 16), ACT.Tanh, scale=0.5)
        cc = stt(AC[:, :, 0:2], SM[:, 80:96].rearrange("p (k s) -> p k s", s=2), 1.0,
                 vec("cc", 0, 16).rearrange("p (k s) -> p k s", s=2), ALU.add, ALU.mult, a, m3)
        def ada(l):
            fr = was = None
            P = PS[7]
            for j in range(18):
                for hf in range(2):
                    def use(view, w):
                        for g in range(4):
                            tok = mm(P[32 * g:32 * g + 32, :], AC[:, 4 * hf + g, :], view[:, g, :], hf == 0, hf == 1,
                                     w, cc, fr, inc=g == 3)
                        return tok
                    rawchunk(4, 512, wsrc(t["w_ada_2"][l], 4 * hf, 4, 512 * j, 512 * j + 512), use)
                    tok = pe.now()
                    yield
                a = cp(AS[:, :], P[:, :], tok, was)
                fr = a
                yield
                b, P2_, f2 = bank()
                for x in range(4):
                    was = mm(P2_[:, 2 * x:2 * x + 2], AS[:, 128 * x:128 * x + 128], SEL, True, True, a, f2, inc=x == 3)
                i0, k0 = (4 * j) // 8, (4 * j) % 8
                for s in range(2):
                    a = stt(MOD[:, l, i0, k0:k0 + 4, s], P2_[:, s:8:2], 0.5, vec("b_ada", 72 * l + 4 * j, 4),
                            ALU.mult, ALU.add, was)
                done(b, a)
                yield
            for i in (2, 8):
                ts(MOD[:, l, i, :, :], MOD[:, l, i, :, :], 0.5, None, ALU.mult, None, a)
            for i, n in ((1, 0), (4, 1), (7, 2)):
                for s in range(2):
                    stt(MOD[:, l, i, :, s], MOD[:, l, i, :, s], 1.0, vec("norm_g", 24 * l + 8 * n, 8), ALU.add,
                        ALU.mult, a)

        class Filler:

            def __init__(self, l):
                self.gen, self.over = ada(l), False

            def fill(self, n=1):
                for _ in range(n):
                    if next(self.gen, 1) is not None:
                        self.over = True
                        return

            def mixed(self, gen, every=1, n=1):
                for i, x in enumerate(gen):
                    if i % every == every - 1:
                        self.fill(n)
                    yield x
        adas = [Filler(l) for l in range(DEPTH)]

        N = 256
        H1 = (H1H, H1L)
        adas[0].fill(4)
        nm = Norm(N, SS1, SQ1, DG1)
        for k in range(8):
            nm.add(k, (cx, 16))
        for l in range(DEPTH):
            w_in, w_out = t["w_in"][l], t["w_out"][l]
            if l:
                act.do(lambda e, i=w_in[:, 4352:4360].rearrange("(k p) c -> p k c", p=128):
                       e.dma_start(W8[:, :, :], i).then_inc(c3, 16), dve.now(), inc=False)
            c3t = (c3, 16 * (l + 1))
            hw = norm_in(nm, lambda k, s: vec("norm_w", 8 * l + k), None, H1, NT1, lambda: adas[0].fill(4))


            def to(slot, scale=None):
                def ev(i, P, tok):
                    return [cp(PJ[:, slot + i, :], P[:, 0:N], tok) if scale is None else
                            af(PJ[:, slot + i, :], P[:, 0:N], ACT.Copy, tok, scale=scale)]
                return ev
            silu_w = [None, None]

            def to_silu2(slot):
                def ev(i, P, tok):
                    T = TM1[:, i % 2, 0:N]
                    a = af(T, P[:, 0:N], ACT.Tanh, tok, silu_w[i % 2], scale=0.5)
                    c = stt(PJ[:, slot + i, :], T, 1.0, P[:, 0:N], ALU.add, ALU.mult, a)
                    silu_w[i % 2] = c
                    return [c]
                return ev

            def to_tok(dst):
                def ev(i, P, tok):
                    return [cp(dst(i), P[:, 0:256].rearrange("p (q c) -> p q c", c=128), tok)]
                return ev

            def vc_ev(i, P, tok):
                for q in range(2):
                    r = cp(VC[:, q, 2 * i:2 * i + 2, 0:64], P[:, 128 * q:128 * q + 128].rearrange("p (h d) -> p h d", d=64),
                           tok)
                vct.append(r)
                return [r]
            vct, cot = [], []

            def co_ev(i, P, tok):
                v = CO[:, :, 128 * i:128 * i + 128]
                a = af(v, P[:, 0:256].rearrange("p (q c) -> p q c", c=128), ACT.Tanh, tok, scale=0.5)
                cot.append(ts(v, v, 0.5, 0.5, ALU.mult, ALU.add, a))
                return [a]

            def half(t_, h):
                return t_[64 * (h % 2):64 * (h % 2) + 64]

            hv1 = ts(SM[:, 32:34], vec("ret_norm_w", 2 * l, 2), 0.5, None, ALU.mult, None)
            hv2 = ts(SM[:, 34:36], vec("mlstm_norm_w", 2 * l, 2), 0.5, None, ALU.mult, None)
            yw = [None, None]
            yt2 = [None, None]

            def yout(src, tok, i, gslot, yslot, sc):
                b, P, fr = bank()
                for q in range(2):
                    tk = tp(P[:, 128 * q:128 * q + 128], src(q), tok, fr, inc=q == 1)
                T = TM1[:, yslot % 2, 256:512]
                a = stt(T, PJ[:, gslot + i, :], sc, P[:, 0:256], ALU.mult, ALU.mult, tk, yw[yslot % 2], hv1, hv2)
                done(b, a)
                yw[yslot % 2] = ysplit(YH1[:, yslot, :], YL1[:, yslot, :], T, a)
                return tk

            def gates(res):
                a = cp(W8H[:, :, :], W8[:, :, :], c3t)
                w = tt(W8L[:, :, :], W8[:, :, :], W8H[:, :, :].bitcast(f32), ALU.subtract, a)
                b, P, fr = bank()
                for k in range(8):
                    tok = w3(P[0:8, 0:256], (W8H[:, k, :], W8L[:, k, :]), (H1H[:, k, :], H1L[:, k, :]), k == 0, k == 7,
                             fr, a, w, inc=k == 7)
                a = cp(RT[0:8, :], P[0:8, 0:256], tok)
                done(b, a)
                yield
                b, P, fr = bank()
                for q in range(2):
                    tok = pe.do(lambda e, o=P[:, 8 * q:8 * q + 8], i=RT[0:8, 128 * q:128 * q + 128]:
                                e.transpose(o, i, IDN[0:8, 0:8]), fr, a, inc=q == 1)
                for q in range(2):
                    g = tt(IF[:, q, :], P[:, 8 * q:8 * q + 8], vec("gate_bias", 8 * l, 8), ALU.add, tok)
                done(b, g)
                yield
                a = stt(T1, F_, -1.0, F_, ALU.mult, ALU.max, g)
                a = af(T2, T1, ACT.Exp, a, scale=-1.0)
                yield
                a = af(T1, T2, ACT.Ln, a, bias=ONE[:, 0:1])
                a = stt(LS, F_, 0.0, T1, ALU.min, ALU.subtract, a)
                yield
                b, P, fr = bank()
                mm(P[:, 0:8], TRI, MA[:, 16:24], True, True, fr, a)
                tok = mm(P[:, 8:12], ONE[:, :], MA[:, 16:20], True, True, inc=True)
                b1 = vcp(BB, P[:, 0:8].rearrange("p (a b) -> p a b", b=4), tok)
                b2 = vcp(BL, P[:, 8:12], tok)
                done(b, b2)
                res.append([tt(RR, I_, BB, ALU.subtract, b1), b2])
                yield
            IF = MA[:, 0:16].rearrange("p (a b) -> p a b", b=8)
            F_, I_ = IF[:, :, 4:8], IF[:, :, 0:4]
            m8 = lambda i: MA[:, 16 + 8 * i:24 + 8 * i].rearrange("p (a b) -> p a b", b=4)
            LS, T1, T2, BB, RR, UU, NU, WI, EM, DN = (m8(i) for i in range(10))
            BL, MS, WS, MX, RHO = (m8(10 + i)[:, 0, :] for i in range(5))

            def attention():
                jobs = []
                ow = [None, None]
                for h in range(8):
                    for q in range(2):
                        nk = 128 * (q + 1)

                        def bias(P, tok, h=h, q=q, nk=nk):
                            return stt(P[:, 0:nk], ALI[:, q, 0:nk], 2.0 ** -(h + 1), P[:, 0:nk], ALU.mult, ALU.add, tok,
                                       c1t)
                        i, ob = h // 2, h // 2 % 2
                        job = dict(q=half(PJ, h)[:, i, 128 * q:128 * q + 128], k=half(PJ, h)[:, 4 + i, 0:nk],
                                   nk=nk, bias=bias, v=lambda x, h=h: VA[:, x, 64 * h:64 * h + 64],
                                   o=O1[:, ob, q, 64 * (h % 2):64 * (h % 2) + 64], ow=lambda ob=ob: ow[ob])
                        if h % 2 and q:
                            def end(o, i=i, ob=ob):
                                pend.append((i, ob, o))
                                assert len(pend) < 2
                            job["end"] = end
                        jobs.append(job)
                pend = []
                gen = attend(jobs, P1, PT1, ST1, 2, 3)
                for _ in gen:
                    yield
                    while pend and not gated:
                        yield
                    while pend and len(gated) > 0:
                        i, ob, o = pend.pop(0)
                        ow[ob] = yout(lambda q: O1[:, ob, q, :], o, i, 8, 0 + i, 0.5)
                for i, ob, o in pend:
                    ow[ob] = yout(lambda q: O1[:, ob, q, :], o, i, 8, 0 + i, 0.5)
                    yield
            gated, mgated = [], []

            def flag(lst):
                lst.append(1)
                return
                yield

            def retention():
                rt = []
                for i in range(4):
                    b, P, fr = bank()
                    tok = mm(P[:, 0:256], ROT, PJ[:, 12 + i, :], True, True, fr, inc=True)
                    a = tt(RT[:, :], P[:, 0:256], CS1[:, 1, :], ALU.mult, tok, c1t, rt)
                    done(b, a)
                    c = tt(PJ[:, 12 + i, :], PJ[:, 12 + i, :], CS1[:, 0, :], ALU.mult, tok, c1t)
                    rt = tt(PJ[:, 12 + i, :], PJ[:, 12 + i, :], RT[:, :], ALU.add, a, c)
                    yield
                bo, PO, fro = bank()
                pw = {}
                T = {}
                for h in range(5):
                    if h < 4:
                        b, P, fr = bank()
                        kk, qq = half(PJ, h)[:, 14 + h // 2, :], half(PJ, h)[:, 12 + h // 2, :]
                        mm(P[:, 0:256], kk[:, 0:128], qq[:, 0:256], True, True, fr, rt)
                        tok = mm(P[:, 256:384], kk[:, 128:256], qq[:, 128:256], True, True, inc=True)
                        T[h] = PR[:, h % 2, :]
                        a_ = tt(T[h], P[:, 0:384], DT[:, h, :], ALU.mult, tok, pw.get(h - 2), c1t)
                        done(b, a_)
                    if h > 0:
                        g = h - 1
                        vv = lambda x: VB[:, x, 64 * g:64 * g + 64]
                        mm(PO[:, 64 * g:64 * g + 64], T[g][:, 0:128], vv(0), True, True, a, fro)
                        mm(PO[:, 256 + 64 * g:320 + 64 * g], T[g][:, 128:256], vv(0), True, False)
                        pw[g] = mm(PO[:, 256 + 64 * g:320 + 64 * g], T[g][:, 256:384], vv(1), False, True, inc=True)
                    a = a_
                    yield
                res = []
                yield from head_norm(0, lambda g: PO[:, 64 * g:64 * g + 64], pw[3], lambda g: YT[:, 64 * g:64 * g + 64],
                                     res)
                done(bo, res[0])
                for i in range(2):
                    yout(lambda q: YT[:, 256 * q + 128 * i:256 * q + 128 * i + 128], res[0], i, 16, 4 + i,
                         SM[:, 32 + i:33 + i])
                    yield

            def mlstm(grs):
                hw_ = ts(SM[:, 36:52], vec("conv_w", 16 * l, 16), 0.5, None, ALU.mult, None)
                hb_ = ts(SM[:, 52:56], vec("conv_b", 4 * l, 4), 0.5, None, ALU.mult, None)
                cq = []
                for i in range(4):
                    A = PJ[:, 20 + i, :]
                    a = ts(A, CP[:, i, 0:256], SM[:, 36 + i:37 + i], SM[:, 52 + i:53 + i], ALU.mult, ALU.add, hw_, hb_,
                           cpt[i], z1)
                    for j in range(1, 4):
                        a = stt(A, CP[:, i, j:j + 256], SM[:, 36 + 4 * j + i:37 + 4 * j + i], A, ALU.mult, ALU.add, a)
                    T = CP[:, i, 3:259]
                    a = af(T, A, ACT.Tanh, a)
                    cq.append(stt(A, T, 1.0, A, ALU.add, ALU.mult, a))
                    yield 1.3
                while not grs or len(cot) < 2:
                    yield
                gr = grs[0]
                NUM = NU1[:, 0:260].rearrange("p (h d) -> p h d", d=65)
                pv = w = tpt = hc = None
                for c in range(2):
                    b, P, fr = bank()
                    for h in range(4):
                        d = ts(MI[:, 0, 128 * h:128 * h + 128], IDN, RR[:, c, h:h + 1], None, ALU.mult, None, gr, pv)
                    tok = mm(P[:, :], ONE[:, :], MI[:, 0, :], True, True, fr, d, inc=True)
                    yield
                    M1 = MI[:, 1, :]
                    for h in range(4):
                        a = tt(M1[:, 128 * h:128 * h + 128], P[:, 128 * h:128 * h + 128], CAU, ALU.add, tok, w)
                    mx = rmax(MX, M1.rearrange("p (h s) -> p h s", s=128), False, a)
                    yield
                    if c == 0:
                        rho = rmax(RHO, P[:, :].rearrange("p (h s) -> p h s", s=128), False, tok)
                        done(b, rho)
                        rho = ts(RHO, RHO, 0.0, None, ALU.max, None, rho)
                        ms1 = tt(MS, BL, RHO, ALU.add, rho)
                        u = ts(UU[:, c, :], MX, 0.0, None, ALU.max, None, mx)
                    else:
                        done(b, a)
                        u = tt(UU[:, c, :], MX, MS, ALU.max, mx, ms1)
                    nu = ts(NU[:, c, :], UU[:, c, :], -1.0, None, ALU.mult, None, u)
                    yield
                    W = MI[:, 2, :]
                    for h in range(4):
                        w = af(W[:, 128 * h:128 * h + 128], M1[:, 128 * h:128 * h + 128], ACT.Exp, nu, tpt,
                               bias=NU[:, c, h:h + 1])
                    mt = tt(DN[:, c, :], BB[:, c, :], UU[:, c, :], ALU.add, u)
                    em = af(EM[:, c, :], DN[:, c, :], ACT.Exp, mt, scale=-1.0)
                    if c == 1:
                        wi = tt(WI[:, c, :], MS, UU[:, c, :], ALU.subtract, u)
                        wi = af(WI[:, c, :], WI[:, c, :], ACT.Exp, wi)
                    yield
                    pair = lambda v: v.rearrange("p (a b s) -> p a b s", b=2, s=128)
                    for o in range(2):
                        b, P, fr = bank()
                        for x in range(2):
                            tok = mm(P[:, 128 * x:128 * x + 128], half(PJ, o)[:, 20 + x, 128 * c:128 * c + 128],
                                     half(PJ, o)[:, 22 + x, 128 * c:128 * c + 128], True, True, fr, cq[3], inc=x == 1)
                        a = stt(pair(W)[:, :, o, :], P[:, 0:256].rearrange("p (a s) -> p a s", s=128), 0.125,
                                pair(W)[:, :, o, :], ALU.mult, ALU.mult, tok, w)
                        done(b, a)
                    yield
                    b, P, fr = bank()
                    for h in range(4):
                        tpt = tp(P[:, 128 * h:128 * h + 128], W[:, 128 * h:128 * h + 128], fr, a, inc=h == 3)
                    PT = MI[:, 0, :]
                    a = cp(PT, P[:, :], tpt)
                    done(b, a)
                    yield
                    b, P, fr = bank()
                    for h in range(4):
                        pv = mm(P[:, 65 * h:65 * h + 65], PT[:, 128 * h:128 * h + 128], VC[:, c, h, 0:65], True, True,
                                fr, a, z2, vct, inc=h == 3)
                    a = vcp(NUM, P[:, 0:260].rearrange("p (h d) -> p h d", d=65), pv)
                    done(b, a)
                    yield
                    if c == 0:
                        ws = tt(WS, RR[:, 0, :], RHO, ALU.subtract, rho)
                        ws = af(WS, WS, ACT.Exp, ws)
                        b, P, fr = bank()
                        for i in range(2):
                            tok = tp(P[:, 128 * i:128 * i + 128], PJ[:, 22 + i, 0:128], fr, cq[3], inc=i == 1)
                        KT = MI[:, 3, 0:256]
                        for h in range(4):
                            kx = ts(KT[:, 64 * h:64 * h + 64], P[:, 64 * h:64 * h + 64], WS[:, h:h + 1], 0.125, ALU.mult,
                                    ALU.mult, tok, ws)
                        done(b, kx)
                        yield
                        b, P, fr = bank()
                        for h in range(4):
                            o = P[64 * (h % 2):64 * (h % 2) + 64, 65 * (h // 2):65 * (h // 2) + 65]
                            tok = mm(o, KT[:, 64 * h:64 * h + 64], VC[:, 0, h, 0:65], True, True, fr, kx, inc=h == 3)
                        state = vcp(MI[:, 3, 256:386], P[:, 0:130], tok)
                        done(b, state)
                        yield
                    else:
                        for o in range(2):
                            b, P, fr = bank()
                            for x in range(2):
                                tok = mm(P[:, 65 * x:65 * x + 65], half(PJ, o)[:, 20 + x, 128:256],
                                         half(MI, o)[:, 3, 256 + 65 * x:256 + 65 * x + 65], True, True,
                                         fr, state, inc=x == 1)
                            for x in range(2):
                                h = 2 * x + o
                                a = stt(NUM[:, h, :], P[:, 65 * x:65 * x + 65], WI[:, 1, h:h + 1], NUM[:, h, :],
                                        ALU.mult, ALU.add, tok, wi, a)
                            done(b, a)
                        yield
                    dn = stt(DN[:, c, :], NUM[:, :, 64], -1.0, NUM[:, :, 64], ALU.mult, ALU.max, a, em)
                    dn = tt(DN[:, c, :], DN[:, c, :], EM[:, c, :], ALU.max, dn)
                    dn = recip(DN[:, c, :], DN[:, c, :], dn)
                    for h in range(4):
                        hc = stt(HC[:, 256 * c + 64 * h:256 * c + 64 * h + 64], NUM[:, h, 0:64], DN[:, c, h:h + 1],
                                 CO[:, c, 64 * h:64 * h + 64], ALU.mult, ALU.mult, dn, cot)
                    yield
                res = []
                g_ = lambda g: HC[:, 64 * g:64 * g + 64]
                yield from head_norm(1, g_, hc, g_, res)
                while not mgated:
                    yield
                for i in range(2):
                    yout(lambda q: HC[:, 256 * q + 128 * i:256 * q + 128 * i + 128], res[0], i, 18, 6 + i,
                         SM[:, 34 + i:35 + i])
                    yield

            def outp(part, hw, ev):
                for i in range(0, 8, 4):
                    chunk(4, 512, [(0, 512, wsrc(w_out, 4 * part, 4, 128 * i, 128 * i + 512))], [(0, 256), (256, 512)])
                    for j in range(2):
                        (wh, wl, w_, u), = unit()
                        for m in range(2):
                            b, P, fr = bank()
                            for k in range(4):
                                tok = w3(P[:, 0:N], (wh[:, k, 128 * m:128 * m + 128], wl[:, k, 128 * m:128 * m + 128]),
                                         (YH1[:, 4 * part + k, :], YL1[:, 4 * part + k, :]), k == 0, k == 3, w_, fr, hw,
                                         inc=k == 3)
                            x = i + 2 * j + m
                            a = tt(X[:, x, 0:N], P[:, 0:N], X[:, x, 0:N], ALU.add, tok)
                            done(b, a)
                            if ev:
                                ev(x, a)
                        ended[u] = tok
                        yield

            def chain(*gens):
                for g in gens:
                    yield from g
            cpt = {}

            def cp_ev(i, P, tok):
                cpt[i] = cp(CP[:, i, 3:259], P[:, 0:N], tok)
                return [cpt[i]]
            gr = []
            mx = lambda g: adas[0].mixed(g, EV - l)
            run(mx(feat(w_in, 3072, 4, N, cp_ev, H1, hw)))
            for fn in late[:3] if l == 0 else late[3:]:
                pool.do(fn, pe.now(), inc=False)
            mls = Part(mlstm(gr), CM)
            dense = Part(mx(chain(tokm(w_in, 3584, 2, 2, vc_ev, H1, YV, yt2),
                                  tokm(w_in, 3840, 2, 2, co_ev, H1, YV, yt2),
                                  feat(w_in, 2048, 4, N, to(12), H1),
                                  tokm(w_in, 2560, 2, 2, to_tok(lambda i: VB[:, :, 128 * i:128 * i + 128]), H1, YV,
                                       yt2),
                                  feat(w_in, 4096, 2, N, to_silu2(18), H1), flag(mgated), feat(w_in, 2816, 2, N, to_silu2(16), H1))),
                         CU)
            gat = Part(gates(gr), CG)
            weave(dense, gat, until=gat)
            weave(dense, mls, until=dense)
            ret = Part(retention(), CR)
            dense = Part(mx(chain(feat(w_in, 0, 4, N, to(0, 0.125), H1), feat(w_in, 512, 4, N, to(4), H1),
                                  tokm(w_in, 1024, 4, 2, to_tok(lambda i: VA[:, :, 128 * i:128 * i + 128]), H1, YV,
                                       yt2))), CU)
            weave(dense, mls, ret, until=dense)
            att = Part(attention(), CA)
            dense = Part(mx(chain(feat(w_in, 1536, 4, N, to_silu2(8), H1), flag(gated))), CU)
            weave(dense, mls, att, ret, until=dense)
            weave(mls, ret, att, until=mls)
            weave(ret, att, until=ret)
            ywt = [act.now(), dve.now()]
            dense = Part(mx(outp(1, ywt, None)), CU)
            weave(att, dense)
            ywt = [act.now(), dve.now()]
            nm = Norm(N, SS1, SQ1, DG1)
            run(mx(outp(0, ywt, nm.add)))
        for e in engines:
            e.do(None, (c2, 32), inc=False)
        nm1, nm = nm, Norm(512, SS, SQ, DG)
        norm_out(nm1, lambda k: vec("final_norm_w", k), lambda k: X[:, k, 0:256], nm.add)
        run(adas[0].gen)

        def ffn(nm, l, gu, dn, n, i0, nxt, fill):
            hw = norm_in(nm, lambda k, s: MOD[:, l, i0 + 1, k, s:s + 1], lambda k, s: MOD[:, l, i0, k, s:s + 1],
                         (HH, HL), NT, fill)
            ft = [None, None]
            ab = {}

            def ev(i, P, tok):
                x, m = divmod(i, 2)
                if x == 0:
                    T = FT[:, m, 0:n]
                    a = af(T, P[:, 0:n], ACT.Tanh, tok, ft[m], scale=0.5)
                    ab[m] = stt(T, T, 1.0, P[:, 0:n], ALU.add, ALU.mult, a)
                    return [ab[m]]
                T = FT[:, m, 0:n]
                g = stt(T, T, 0.5, P[:, 0:n], ALU.mult, ALU.mult, ab[m], tok)
                ft[m] = ysplit(GH[:, 2 * j + m, 0:n], GL[:, 2 * j + m, 0:n], T, g)
                return [g]
            for j in range(11):
                for x in range(2):
                    run(columns(gu, 2816 * x + 256 * j, 2, 8, n, (HH, HL), 0, ev, 2 * x, hw if j == 0 and x == 0 else None))
            gt = [act.now(), dve.now()]
            for j in range(4):
                bk = [bank(), bank()]
                for k0, kt in ((0, 8), (8, 8), (16, 6)):
                    chunk(kt, 256, [(0, 256, wsrc(dn, k0, kt, 256 * j, 256 * j + 256))], [(0, 128), (128, 256)])
                    for m in range(2):
                        (wh, wl, w_, u), = unit()
                        b, P, fr = bk[m]
                        for k in range(kt):
                            kk = k0 + k
                            tok = w3(P[:, 0:n], (wh[:, k, :], wl[:, k, :]), (GH[:, kk, 0:n], GL[:, kk, 0:n]),
                                     kk == 0, kk == 21, w_, fr, gt if kk >= 20 else None, inc=k == kt - 1)
                        ended[u] = tok
                        if k0 == 16:
                            i = 2 * j + m
                            for s in range(n // 256):
                                c = slice(256 * s, 256 * s + 256)
                                a = stt(X[:, i, c], P[:, c], MOD[:, l, i0 + 2, i, s:s + 1], X[:, i, c], ALU.mult,
                                        ALU.add, tok)
                            done(b, a)
                            nxt.add(i, a)

        def mixer(nm, l, last, nxt, fill, mixed):
            n = 512
            nq = 256 if last else 512
            nt = nq // 128
            w_in = t["w_in_2"][l]
            fw = [e.now() for e in engines]
            hw = norm_in(nm, lambda k, s: MOD[:, l, 4, k, s:s + 1], lambda k, s: MOD[:, l, 3, k, s:s + 1], (HH, HL), NT,
                         fill)
            nb = 0
            for r in range(4):
                for h in range(6):
                    src = bass.AP(tensor=scr.tensor, offset=(l * 64) * 2790 + 465 * h + (7 - r) * 31 + 15,
                                  ap=[[2789, 64], [31, 4], [1, 64]])
                    pp = 64 * (r % 2)
                    pool.do(lambda e, src=src, pp=pp, r=r, h=h: e.dma_start(
                        BM[pp:pp + 64, r // 2, h, :].rearrange("p (y x) -> p y x", x=64), src)
                        .then_inc(sems["bm1"], 16), fw, (sems["bm0"], 32), inc=False)
                    nb += 16
            bmt = (sems["bm1"], nb * (l + 1))
            z = dve.do(lambda e: e.memset(HP[:, :, :, :], 0.0), fw)
            hb = None

            def to(T, slot, w, scale=1.0):
                return lambda i, P, tok: [af(T[:, slot + i, 0:w], P[:, 0:w], ACT.Copy, tok, scale=scale)]

            def tov(c):
                return lambda i, P, tok: [cp(V2[:, :, c + 128 * i:c + 128 * i + 128],
                                             P[:, :].rearrange("p (q c) -> p q c", c=128), tok)]
            vt2 = [None, None]
            run(feat(w_in, 0, 3, nq, to(QA, 0, nq, 0.125), None, hw), feat(w_in, 384, 3, n, to(QA, 3, n)),
                tokm(w_in, 768, 3, 4, tov(0), None, TM2, vt2))
            bmr = None
            for q in range(2):
                v = BM[:, q, :, :].rearrange("p h (y x) -> p (h y) x", x=64)
                lim = bass.AP(tensor=WIN.tensor, offset=WIN.offset, ap=[list(WIN.ap[0]), [0, 24], [1, 64]])
                bmr = tt(v, v, lim, ALU.min, bmt)
            hb = ts(ST2[:, 216:240], vec("b_gate", 24 * l, 24), 0.5, None, ALU.mult, None)
            ns = ts(SM[:, 56:62], vec("sink", 6 * l, 6), -1.0, None, ALU.mult, None)
            ut = [None] * 2
            hp = [None, None]

            def uev(i, P, tok):
                if i < 2:
                    ut[i] = cp(TM2[:, i, 0:nq], P[:, 0:nq], tok, vt2[i])
                    return [ut[i]]
                T = TM2[:, 2, 0:nq]
                a = af(T, P[:, 0:nq], ACT.Tanh, tok, hp[0], scale=0.5)
                b_ = ts(T, T, 0.5, 0.5, ALU.mult, ALU.add, a)
                hp[i - 2] = tt(HP[:, i - 2, 0:nq // 256, 15:271], T.rearrange("p (s n) -> p s n", n=256),
                               TM2[:, i - 2, 0:nq].rearrange("p (s n) -> p s n", n=256), ALU.mult, b_, z, ut[i - 2])
                return [a]

            def projb():
                for j in range(3):
                    c_ = 1152 + 64 * j
                    chunk(8, 128, [(0, 64, wsrc(w_in, 0, 8, c_, c_ + 64)),
                                   (64, 128, wsrc(w_in, 0, 8, c_ + 192, c_ + 256))], [(0, 128)])
                    (wh, wl, w_, u), = unit()
                    b, P, fr = bank()
                    for k in range(8):
                        if k == 4:
                            yield
                        tok = w3(P[:, 0:nq], (wh[:, k, :], wl[:, k, :]), (HH[:, k, 0:nq], HL[:, k, 0:nq]),
                                 k == 0, k == 7, w_, fr, inc=k == 7)
                    ended[u] = tok
                    done(b, *to(QB, j, nq, 0.125)(0, P, tok))
                    yield
                yield from feat(w_in, 1536, 1, n, to(QB, 3, n))
                yield from tokm(w_in, 1664, 1, 4, tov(384), None, TM2, [hp[0], hp[1]])
                rt = None
                for i in range(4):
                    b, P, fr = bank()
                    tok = mm(P[:, 0:256], ROT, QB[:, i, 0:256], True, True, fr, act.now(), inc=True)
                    T = TM2[:, 0, 0:256]
                    a = tt(T, P[:, 0:256], CS2[:, 1, :], ALU.mult, tok, rt)
                    done(b, a)
                    c = tt(QB[:, i, 0:256], QB[:, i, 0:256], CS2[:, 0, :], ALU.mult, tok)
                    rt = tt(QB[:, i, 0:256], QB[:, i, 0:256], T, ALU.add, a, c)
                    yield
                rtt.append(rt)
            rtt = []
            ow = [None, None]
            cnt = [0]

            def ytile(o, yslot, q, ob):
                b, P, fr = bank()
                for i in range(3):
                    tok = tp(P[:, 128 * i:128 * i + 128], O2[:, ob, 128 * i:128 * i + 128], fr, o, inc=i == 2)
                yh = YH2[:, yslot:yslot + 3, 128 * q:128 * q + 128]
                yl = YL2[:, yslot:yslot + 3, 128 * q:128 * q + 128]
                Pv = P[:, 0:384].rearrange("p (i n) -> p i n", n=128)
                a = cp(yh, Pv, tok)
                c = tt(yl, Pv, yh.bitcast(f32), ALU.subtract, a)
                done(b, c)
                ow[ob] = tok

            def attn(br):
                jobs = []
                pend = []
                for q in range(nt):
                    ctx_q = q >= 2
                    k0, nk = (256, 256) if ctx_q else (0, 512)
                    for h in range(6):
                        if br == 0:
                            hs, Q_, K_ = h % 2, QA[:, h // 2, :], QA[:, 3 + h // 2, :]
                        else:
                            hs, Q_, K_ = h // 3, QB[:, h % 3, :], QB[:, 3, :]
                        r0 = slice(64 * hs, 64 * hs + 64)
                        vc = 64 * h if br == 0 else 384 + 64 * (h // 3)
                        ob = cnt[0] % 2
                        job = dict(q=Q_[r0, 128 * q:128 * q + 128], k=K_[r0, k0:k0 + nk], nk=nk,
                                   v=lambda x, vc=vc, k0=k0: V2[:, k0 // 128 + x, vc:vc + 64],
                                   o=O2[:, ob, 64 * h:64 * h + 64], w=rtt if br else None)
                        if not ctx_q:
                            if br == 0:
                                def bias(P, tok, tab=BM[:, q, h, :]):
                                    return tt(P[:, 0:256], P[:, 0:256], tab, ALU.add, tok, bmr)
                            else:
                                def bias(P, tok, c=slice(128, 256) if q == 0 else slice(0, 128), m=CAU if q == 0 else CAT):
                                    return tt(P[:, c], P[:, c], m, ALU.add, tok)
                            job["bias"] = bias
                        if br == 1:
                            job["sink"] = (vec("sink", 6 * l + h, 1), SM[:, 56 + h:57 + h])
                        if h == 0:
                            job["ow"] = lambda ob=ob: ow[ob]
                        if h == 5:
                            job["end"] = lambda o, q=q, ob=ob: pend.append((o, 3 * br, q, ob))
                        jobs.append(job)
                    cnt[0] += 1
                for _ in attend(jobs, P2, PT2, ST2, 1, 2):
                    yield
                    while pend:
                        ytile(*pend.pop(0))
                for p in pend:
                    ytile(*p)

            def conv():
                a = [None, None]
                for j in range(31):
                    for i in range(2):
                        A = CV[:, i, 0:nq].rearrange("p (s n) -> p s n", n=256)
                        x = HP[:, i, 0:nq // 256, j:j + 256]
                        wv = vec("dw_w", 62 * l + 2 * j + i)
                        if j == 0:
                            a[i] = ts(A, x, wv, vec("dw_b", 2 * l + i), ALU.mult, ALU.add, hp[i])
                        else:
                            a[i] = stt(A, x, wv, A, ALU.mult, ALU.add, a[i])
                        yield
                cvt.append(a)
            cvt = []

            def lnorm():
                w = yt = tt_ = None
                S6 = ST2[:, 240:246]
                tw = [None, None]
                for q in range(nt):
                    b, P, fr = bank()
                    for i in range(2):
                        tok = tp(P[:, 128 * i:128 * i + 128], CV[:, i, 128 * q:128 * q + 128], fr, cvt, inc=i == 1)
                    s = dve.do(lambda e, P=P: e.bn_stats(S6, P[:, 0:256]), tok)
                    s = dve.do(lambda e: e.bn_aggr(ST2[:, 246:248], S6), s)
                    v = ts(SM[:, 16:17], ST2[:, 247:248], 1e-6, None, ALU.add, None, s)
                    r = rpow(SM[:, 24:25], SM[:, 16:17], v)
                    yield
                    T = TM2[:, q % 2, 0:256]
                    y = ts(T, P[:, 0:256], ST2[:, 246:247], SM[:, 24:25], ALU.subtract, ALU.mult, r, s, tw[q % 2])
                    done(b, y)
                    b, P, fr = bank()
                    for i in range(2):
                        tok = tp(P[:, 128 * i:128 * i + 128], T[:, 128 * i:128 * i + 128], fr, y, inc=i == 1)
                    tw[q % 2] = tok
                    yield
                    for i in range(2):
                        U = TM2[:, 2, 128 * i:128 * i + 128]
                        V_ = TM2[:, 2, 256 + 128 * i:384 + 128 * i]
                        u = ts(U, P[:, 128 * i:128 * i + 128], vec("ln_g", 2 * l + i), vec("ln_b", 2 * l + i), ALU.mult,
                               ALU.add, tok, yt)
                        w = af(V_, U, ACT.Tanh, u, yt, scale=0.5)
                        w = stt(V_, V_, 1.0, U, ALU.add, ALU.mult, w)
                        yt2 = ysplit(YH2[:, 6 + i, 128 * q:128 * q + 128], YL2[:, 6 + i, 128 * q:128 * q + 128], V_, w, 0.5)
                    done(b, u)
                    yt = yt2
                    yield

            mw, bw = [None] * 2, [None] * 2
            accs = {}
            mtok = []

            def merge(br, wo, kb, kn):
                yt = [act.now(), dve.now()]
                for mp in range(4):
                    ga = [None, None]

                    def gev(m, P, tok):
                        i = 8 * br + 2 * mp + m
                        ga[m] = af(MT[:, m, 0:nq], P[:, 0:nq], ACT.Tanh, tok, hb, mw[m], scale=0.5,
                                   bias=ST2[:, 216 + i:217 + i])
                        return [ga[m]]
                    yield from columns(w_in, 2304 + 1024 * br + 256 * mp, 2, 8, nq, (HH, HL), 0, gev, 0, None)
                    chunk(kn, 256, [(0, 256, wsrc(t[wo][l], 0, kn, 256 * mp, 256 * mp + 256))], [(0, 256)])
                    (wh, wl, w_, u), = unit()
                    for m in range(2):
                        i = 2 * mp + m
                        b, P, fr = bank()
                        for k in range(kn):
                            tok = w3(P[:, 0:nq], (wh[:, k, 128 * m:128 * m + 128], wl[:, k, 128 * m:128 * m + 128]),
                                     (YH2[:, kb + k, 0:nq], YL2[:, kb + k, 0:nq]), k == 0, k == kn - 1, w_, fr, yt,
                                     inc=k == kn - 1)
                        A = ACC[:, i, 0:nq]
                        if br == 0:
                            accs[i] = mw[m] = stt(A, MT[:, m, 0:nq], 1.0, P[:, 0:nq], ALU.add, ALU.mult, tok, ga[m])
                        else:
                            B_ = MT[:, 2 + m, 0:nq]
                            mw[m] = stt(B_, MT[:, m, 0:nq], 1.0, P[:, 0:nq], ALU.add, ALU.mult, tok, ga[m], bw[m])
                            accs[i] = bw[m] = tt(A, A, B_, ALU.add, mw[m], accs[i], on=pool)
                            if br == 2:
                                mtok.append(ysplit(MH[:, i, 0:nq], ML[:, i, 0:nq], A, accs[i], 0.5))
                        done(b, mw[m])
                    ended[u] = tok
                    yield

            cvp = Part(conv(), KC)

            def pj2():
                yield from feat(w_in, 1792, 4, nq, uev)
                yield from projb()
            att = Part(mixed(attn(0), 1), 1.6 if last else 1.15)
            pj = Part(pj2(), KP)

            while hp[1] is None:
                att.step()
                pj.step()
            weave(att, pj, cvp, until=pj)
            weave(att, cvp, until=att)
            att = Part(mixed(attn(1), 2), 1.6 if last else 1.15)
            weave(att, Part(merge(0, "w_out_a_2", 0, 3), KM), cvp)
            weave(Part(lnorm(), 2.0 if last else 1.0), Part(merge(1, "w_out_b_2", 3, 3), KL))
            run(merge(2, "w_out_c_2", 6, 2))

            def xev(i, P, tok):
                for s in range(nq // 256):
                    c = slice(256 * s, 256 * s + 256)
                    a = stt(X[:, i, c], P[:, c], MOD[:, l, 5, i, s:s + 1], X[:, i, c], ALU.mult, ALU.add, tok)
                nxt.add(i, a)
                return [a]
            run(feat(t["w_out_2"][l], 0, 8, nq, xev, (MH, ML), mtok))

        for l in range(DEPTH):
            last = l == DEPTH - 1
            nxt_ada = None if last else adas[l + 1]
            fill = (lambda: None) if last else (lambda: nxt_ada.fill(4))
            mixed = (lambda g, every: g) if last else (lambda g, every: nxt_ada.mixed(g, every))
            nn = Norm(512, SS, SQ, DG)
            ffn(nm, l, t["w_ffn1_gu_2"][l], t["w_ffn1_down_2"][l], 512, 0, nn, fill)
            nq = 256 if last else 512
            n2 = Norm(nq, SS, SQ, DG)
            mixer(nn, l, last, n2, fill, mixed)
            nm = Norm(nq, SS, SQ, DG)
            ffn(n2, l, t["w_ffn2_gu_2"][l], t["w_ffn2_down_2"][l], nq, 6, nm, fill)
            if not last:
                run(nxt_ada.gen)
        def store(k, tok):
            if k % 2:
                dma(out.rearrange("(k p) n -> p k n", p=128)[:, k - 1:k + 1, :], OUT[:, k - 1:k + 1, :], sems["out"], tok)
        norm_out(nm, lambda k: vec("final_g", k), lambda k: OUT[:, k, :], store)
        sp.do(None, (sems["out"], 64), inc=False)
        return pe, act, dve, pool, sp, (chunks, units)

    plan = trace(None)[5]
    pe, act, dve, pool, sp, _ = trace(plan)
    with nc.Block() as block:
        @block.sync
        def _(e):
            sp.emit(e)

        @block.scalar
        def _(e):
            act.emit(e)

        @block.vector
        def _(e):
            dve.emit(e)

        @block.gpsimd
        def _(e):
            pool.emit(e)

        @block.tensor
        def _(e):
            pe.emit(e)


_WEIGHTS = ["w_in", "w_out", "w_ada_2", "w_ffn1_gu_2", "w_ffn1_down_2", "w_ffn2_gu_2", "w_ffn2_down_2", "w_in_2",
            "w_out_a_2", "w_out_b_2", "w_out_c_2", "w_out_2"]


def constants():
    import numpy as np
    f = np.float32
    i = np.arange(128)
    ident = np.eye(128, dtype=f)
    tri = (i[:, None] <= i[None, :]).astype(f)
    rot = np.zeros((128, 128), f)
    for h in (0, 64):
        for d in range(32):
            rot[h + 32 + d, h + d] = -1.0
            rot[h + d, h + 32 + d] = 1.0
    cau = np.where(i[None, :] <= i[:, None], 0.0, -1e30).astype(f)
    qc = i % 64
    w0 = np.clip(qc - 8, 0, 48)[:, None]
    x = np.arange(64)[None, :]
    inw = (x >= w0) & (x < w0 + 16)
    sel = np.zeros((128, 2), f)
    for g in range(4):
        sel[32 * g, 0] = sel[32 * g + 1, 1] = 1.0
    cst = np.concatenate([ident, tri, rot, cau, cau.T, np.where(inw, 3e38, -1e30).astype(f), sel], axis=1)
    q = (np.arange(2)[None, :, None] * 128 + i[:, None, None])
    k = np.arange(256)[None, None, :]
    alibi = np.where(k <= q, -(q - k).astype(f), f(-1e32)).astype(f)
    lg = np.log(f(1.0) - np.exp2(f(-5.0) - np.arange(4, dtype=f))).astype(f)
    dec = np.zeros((128, 4, 384), f)
    for h in range(4):
        d = (np.arange(256)[None, :] - i[:, None]).astype(f)
        full = np.where(d >= 0, np.exp((lg[h] * np.maximum(d, f(0.0))).astype(f)), f(0.0)).astype(f) * f(0.125)
        dec[:, h, 0:256] = full
        dec[:, h, 256:384] = full[:, 0:128]
    pos = np.arange(256, dtype=f)
    th = (f(1.0) / (f(10000.0) ** np.linspace(0.0, 1.0, 32, dtype=f))).astype(f)
    ang = (pos[:, None] * th[None, :]).astype(f).T
    cs1 = np.stack([np.tile(np.cos(ang), (4, 1)), np.tile(np.sin(ang), (4, 1))], axis=1).astype(f)
    inv = (f(10000.0) ** (-np.arange(16, dtype=f) / f(16))).astype(f)
    tk = np.arange(256)
    a2 = np.concatenate([(tk // 64).astype(f)[:, None] * inv, (tk % 64).astype(f)[:, None] * inv], axis=1).astype(f).T
    cs2 = np.stack([np.tile(np.cos(a2), (4, 1)), np.tile(np.sin(a2), (4, 1))], axis=1).astype(f)
    return {"cst": cst, "alibi": alibi, "decay": dec, "cs1": cs1, "cs2": cs2}


def kernel(**inputs):
    import numpy as _np
    import concourse.bacc as _bacc
    from concourse import mybir as _mybir
    from concourse.bass_utils import run_bass_kernel_spmd as _run

    nc = _bacc.Bacc("TRN2", target_bir_lowering=False, num_devices=1)
    a = {n: _np.asarray(v) for n, v in inputs.items()}

    def col(v):
        v = v.reshape(-1, v.shape[-1] // 128, 128)
        return v.transpose(2, 0, 1).reshape(128, -1)

    def row(v):
        return _np.broadcast_to(v.reshape(1, -1), (128, v.size))
    parts = [("norm_w", col(a["norm_w"])), ("conv_w", col(a["conv_w"].reshape(8, 512))), ("conv_b", col(a["conv_b"])),
             ("ret_norm_w", col(a["ret_norm_w"])), ("mlstm_norm_w", col(a["mlstm_norm_w"])),
             ("final_norm_w", col(a["final_norm_w"][None])), ("gate_bias", row(a["gate_bias"])),
             ("cc", col(_np.stack([a["c_2"][0], a["c_ctx_2"]])).reshape(128, 2, 8).transpose(0, 2, 1).reshape(128, 16)),
             ("b_ada", col(a["b_ada_2"])), ("norm_g", col(a["norm_g_2"].reshape(6, 1024))),
             ("b_gate", col(a["b_gate_2"])), ("sink", row(a["sw_sink_2"])),
             ("dw_w", col(a["conv_dw_w_2"].reshape(62, 256))), ("dw_b", col(a["conv_dw_b_2"])),
             ("ln_g", col(a["conv_ln_g_2"])), ("ln_b", col(a["conv_ln_b_2"])), ("final_g", col(a["final_g_2"][None]))]
    arrays = {"vec": _np.ascontiguousarray(_np.concatenate([p for _, p in parts], axis=1)),
              "xT": _np.ascontiguousarray(a["x"][0].T), "ctxT": _np.ascontiguousarray(a["ctx_2"][0].T),
              "rpb": _np.ascontiguousarray(a["na_rpb_2"].reshape(2, 2790))}
    for n in _WEIGHTS:
        arrays[n] = _np.ascontiguousarray(a[n])
    arrays.update(constants())
    t = {n: nc.dram_tensor(f"in_{n}", v.shape, _mybir.dt.from_np(v.dtype), kind="ExternalInput").ap()
         for n, v in arrays.items()}
    t["_vec"] = [(n, p.shape[1]) for n, p in parts]
    out = nc.dram_tensor("out_0_dram", (1024, 256), _mybir.dt.from_np(_np.dtype("float32")), kind="ExternalOutput").ap()
    program(nc, t, out)
    r = _run(nc, [{f"in_{n}": v for n, v in arrays.items()}], core_ids=[0])
    return _np.ascontiguousarray(r.results[0]["out_0_dram"].T)[None]
```
